# Optimizing a Trainium2 kernel written in Bass

```python
import math
import jax, jax.numpy as jnp
from jax import lax
import numpy as np

D_MODEL = 1024
BATCH = 1
SEQ = 256
DEPTH = 2

CHUNK = 64
N_MIXERS = 2
RMS_EPS = 1e-6

SSD_EXPAND = 2
SSD_D_INNER = SSD_EXPAND * D_MODEL
SSD_HEAD_DIM = 64
SSD_N_HEADS = SSD_D_INNER // SSD_HEAD_DIM
SSD_N_GROUPS = 8
SSD_HEADS_PER_GROUP = SSD_N_HEADS // SSD_N_GROUPS
SSD_D_STATE = 128
SSD_CONV = 4
SSD_CHUNK = CHUNK
SSD_CONV_DIM = SSD_D_INNER + 2 * SSD_N_GROUPS * SSD_D_STATE
SSD_IN_DIM = SSD_D_INNER + SSD_CONV_DIM + SSD_N_HEADS
DT_MIN = 0.001
DT_MAX = 0.1

DA_HEAD_DIM = 64
DA_N_HEADS = D_MODEL // (2 * DA_HEAD_DIM)
DA_Q_BLOCK = 128

PEER_N_KEYS = 128
PEER_N_EXPERTS = PEER_N_KEYS * PEER_N_KEYS
PEER_HEADS = 8
PEER_TOPK = 16
PEER_D_KEY = 256
PEER_HALF = PEER_D_KEY // 2
PEER_TOKEN_BLOCK = 128

N_SSD_LAYERS = (DEPTH + N_MIXERS - 1) // N_MIXERS
N_ATTN_LAYERS = DEPTH // N_MIXERS

kernel_name = 'hybrid_ssd_diffattn_peer_block'

def rms_norm(x, w):
    xf = x.astype(jnp.float32)
    y = xf * lax.rsqrt(jnp.mean(xf * xf, axis=-1, keepdims=True) + RMS_EPS)
    return (y * w.astype(jnp.float32)).astype(x.dtype)

def causal_depthwise_conv(x, w, b):
    c = x.shape[-1]
    y = lax.conv_general_dilated(x, w[:, None, :].astype(x.dtype), window_strides=(1,),
                                 padding=[(SSD_CONV - 1, 0)],
                                 dimension_numbers=('NWC', 'WIO', 'NWC'),
                                 feature_group_count=c)
    return y + b.astype(x.dtype)

def ssd_chunked_scan(xh, dt, a, bmat, cmat):
    f32 = jnp.float32
    bsz, seq = xh.shape[0], xh.shape[1]
    nc = seq // SSD_CHUNK
    xd = xh.astype(f32) * dt[..., None]
    adt = dt * a

    def to_chunks(t):
        t = t.reshape((bsz, nc, SSD_CHUNK) + t.shape[2:])
        return jnp.moveaxis(t, 1, 0)

    xs = (to_chunks(xd), to_chunks(adt), to_chunks(bmat.astype(f32)), to_chunks(cmat.astype(f32)))
    causal = jnp.tril(jnp.ones((SSD_CHUNK, SSD_CHUNK), dtype=bool))

    def step(state, inp):
        x_c, a_c, b_c, c_c = inp
        a_cs = jnp.cumsum(a_c, axis=1)
        seg = a_cs[:, :, None] - a_cs[:, None, :]
        decay = jnp.exp(jnp.where(causal[None, :, :, None, None], seg, -jnp.inf))
        cb = jnp.einsum('blgn,bsgn->blsg', c_c, b_c)
        y_diag = jnp.einsum('blsg,blsge,bsgep->blgep', cb, decay, x_c)
        y_off = jnp.einsum('blgn,bgepn,blge->blgep', c_c, state, jnp.exp(a_cs))
        a_last = a_cs[:, -1]
        to_end = jnp.exp(a_last[:, None] - a_cs)
        new_state = (state * jnp.exp(a_last)[..., None, None]
                     + jnp.einsum('bsgn,bsge,bsgep->bgepn', b_c, to_end, x_c))
        return new_state, y_diag + y_off

    state0 = jnp.zeros((bsz, SSD_N_GROUPS, SSD_HEADS_PER_GROUP, SSD_HEAD_DIM, SSD_D_STATE), f32)
    _, ys = lax.scan(step, state0, xs)
    return jnp.moveaxis(ys, 0, 1).reshape(bsz, seq, SSD_N_GROUPS, SSD_HEADS_PER_GROUP, SSD_HEAD_DIM)

def ssd_mixer(h, in_w, conv_w, conv_b, dt_bias, a_log, d_skip, norm_w, out_w):
    f32 = jnp.float32
    bsz, seq, _ = h.shape
    g, e, p, n = SSD_N_GROUPS, SSD_HEADS_PER_GROUP, SSD_HEAD_DIM, SSD_D_STATE
    zxbcdt = h @ in_w
    z, xbc, dt_raw = jnp.split(zxbcdt, [SSD_D_INNER, SSD_D_INNER + SSD_CONV_DIM], axis=-1)
    xbc = jax.nn.silu(causal_depthwise_conv(xbc, conv_w, conv_b))
    xs, bmat, cmat = jnp.split(xbc, [SSD_D_INNER, SSD_D_INNER + g * n], axis=-1)
    xh = xs.reshape(bsz, seq, g, e, p)
    bmat = bmat.reshape(bsz, seq, g, n)
    cmat = cmat.reshape(bsz, seq, g, n)
    dt = jax.nn.softplus((dt_raw + dt_bias).astype(f32)).reshape(bsz, seq, g, e)
    a = -jnp.exp(a_log.astype(f32)).reshape(g, e)
    y = ssd_chunked_scan(xh, dt, a, bmat, cmat)
    y = y + xh.astype(f32) * d_skip.astype(f32).reshape(g, e)[:, :, None]
    y = y.reshape(bsz, seq, SSD_D_INNER) * jax.nn.silu(z.astype(f32))
    yg = y.reshape(bsz, seq, g, e * p)
    yg = yg * lax.rsqrt(jnp.mean(yg * yg, axis=-1, keepdims=True) + RMS_EPS)
    y = (yg.reshape(bsz, seq, SSD_D_INNER) * norm_w.astype(f32)).astype(h.dtype)
    return y @ out_w

def diff_attention(h, qkv_w, q_norm_w, k_norm_w, lam_q1, lam_k1, lam_q2, lam_k2,
                   subln_w, out_w, lambda_init):
    f32 = jnp.float32
    bsz, seq, dm = h.shape
    nh, d = DA_N_HEADS, DA_HEAD_DIM
    q, k, v = jnp.split(h @ qkv_w, 3, axis=-1)
    q = rms_norm(q.reshape(bsz, seq, nh, 2, d), q_norm_w)
    k = rms_norm(k.reshape(bsz, seq, nh, 2, d), k_norm_w)
    v = v.reshape(bsz, seq, nh, 2 * d)
    lam = (jnp.exp(jnp.sum((lam_q1 * lam_k1).astype(f32)))
           - jnp.exp(jnp.sum((lam_q2 * lam_k2).astype(f32))) + lambda_init)
    scale = d ** -0.5
    nb = seq // DA_Q_BLOCK
    qb = jnp.moveaxis(q.reshape(bsz, nb, DA_Q_BLOCK, nh, 2, d), 1, 0)
    key_chunk = jnp.arange(seq) // CHUNK

    def block(args):
        q_blk, blk_idx = args
        q_chunk = (blk_idx * DA_Q_BLOCK + jnp.arange(DA_Q_BLOCK)) // CHUNK
        mask = key_chunk[None, :] <= q_chunk[:, None]
        s = jnp.einsum('bqhmd,bkhmd->bhmqk', q_blk, k).astype(f32) * scale
        s = jnp.where(mask, s, -jnp.inf)
        pr = jax.nn.softmax(s, axis=-1)
        attn = pr[:, :, 0] - lam * pr[:, :, 1]
        return jnp.einsum('bhqk,bkhe->bqhe', attn.astype(v.dtype), v)

    o = lax.map(block, (qb, jnp.arange(nb)))
    o = jnp.moveaxis(o, 0, 1).reshape(bsz, seq, nh, 2 * d)
    o = rms_norm(o, subln_w) * (1.0 - lambda_init)
    return o.reshape(bsz, seq, dm) @ out_w

def peer_ffn(h, query_w, sub_keys, expert_u, expert_v):
    f32 = jnp.float32
    bsz, seq, dm = h.shape
    nb = (bsz * seq) // PEER_TOKEN_BLOCK
    tokens = h.reshape(nb, PEER_TOKEN_BLOCK, dm)
    kk = PEER_TOPK

    def block(xt):
        q = (xt @ query_w).reshape(-1, PEER_HEADS, 2, PEER_HALF)
        s = jnp.einsum('thcd,hcnd->thcn', q, sub_keys).astype(f32)
        top_s, top_i = lax.top_k(s, kk)
        cand_s = (top_s[:, :, 0, :, None] + top_s[:, :, 1, None, :]).reshape(-1, PEER_HEADS, kk * kk)
        cand_i = (top_i[:, :, 0, :, None] * PEER_N_KEYS + top_i[:, :, 1, None, :]).reshape(-1, PEER_HEADS, kk * kk)
        best_s, pos = lax.top_k(cand_s, kk)
        idx = jnp.take_along_axis(cand_i, pos, axis=-1)
        gate = jax.nn.softmax(best_s, axis=-1)
        u = expert_u[idx]
        vv = expert_v[idx]
        act = jax.nn.gelu(jnp.einsum('thkd,td->thk', u, xt).astype(f32), approximate=False)
        return jnp.einsum('thk,thkd->td', (gate * act).astype(vv.dtype), vv)

    y = lax.map(block, tokens)
    return y.reshape(bsz, seq, dm)

def setup_inputs(seed: int = 0) -> dict:
    key = jax.random.key(seed)
    ks = jax.random.split(key, 24)
    f32 = jnp.float32
    ns, na = N_SSD_LAYERS, N_ATTN_LAYERS

    def nrm(k, shape, scale):
        return jax.random.normal(k, shape, f32) * scale

    x = nrm(ks[0], (BATCH, SEQ, D_MODEL), 1.0)
    mix_norm_w = 1.0 + nrm(ks[1], (DEPTH, D_MODEL), 0.02)
    ffn_norm_w = 1.0 + nrm(ks[2], (DEPTH, D_MODEL), 0.02)
    ssd_in_w = nrm(ks[3], (ns, D_MODEL, SSD_IN_DIM), D_MODEL ** -0.5)
    ssd_conv_w = nrm(ks[4], (ns, SSD_CONV, SSD_CONV_DIM), SSD_CONV ** -0.5)
    ssd_conv_b = nrm(ks[5], (ns, SSD_CONV_DIM), 0.02)
    dt0 = jnp.exp(jax.random.uniform(ks[6], (ns, SSD_N_HEADS), f32)
                  * (math.log(DT_MAX) - math.log(DT_MIN)) + math.log(DT_MIN))
    ssd_dt_bias = dt0 + jnp.log(-jnp.expm1(-dt0))
    ssd_a_log = jnp.log(jax.random.uniform(ks[7], (ns, SSD_N_HEADS), f32, 1.0, 16.0))
    ssd_d = 1.0 + nrm(ks[8], (ns, SSD_N_HEADS), 0.02)
    ssd_norm_w = 1.0 + nrm(ks[9], (ns, SSD_D_INNER), 0.02)
    ssd_out_w = nrm(ks[10], (ns, SSD_D_INNER, D_MODEL), SSD_D_INNER ** -0.5)
    da_qkv_w = nrm(ks[11], (na, D_MODEL, 3 * D_MODEL), D_MODEL ** -0.5)
    da_q_norm_w = 1.0 + nrm(ks[12], (na, DA_HEAD_DIM), 0.02)
    da_k_norm_w = 1.0 + nrm(ks[13], (na, DA_HEAD_DIM), 0.02)
    da_lam_q1 = nrm(ks[14], (na, DA_HEAD_DIM), 0.1)
    da_lam_k1 = nrm(ks[15], (na, DA_HEAD_DIM), 0.1)
    da_lam_q2 = nrm(ks[16], (na, DA_HEAD_DIM), 0.1)
    da_lam_k2 = nrm(ks[17], (na, DA_HEAD_DIM), 0.1)
    da_subln_w = 1.0 + nrm(ks[18], (na, 2 * DA_HEAD_DIM), 0.02)
    da_out_w = nrm(ks[19], (na, D_MODEL, D_MODEL), D_MODEL ** -0.5)
    peer_query_w = nrm(ks[20], (DEPTH, D_MODEL, PEER_HEADS * PEER_D_KEY), D_MODEL ** -0.5)
    peer_sub_keys = nrm(ks[21], (DEPTH, PEER_HEADS, 2, PEER_N_KEYS, PEER_HALF), PEER_HALF ** -0.5)
    peer_u = nrm(ks[22], (DEPTH, PEER_N_EXPERTS, D_MODEL), D_MODEL ** -0.5)
    peer_v = nrm(ks[23], (DEPTH, PEER_N_EXPERTS, D_MODEL), PEER_HEADS ** -0.5)
    return {'x': x, 'mix_norm_w': mix_norm_w, 'ffn_norm_w': ffn_norm_w,
            'ssd_in_w': ssd_in_w, 'ssd_conv_w': ssd_conv_w, 'ssd_conv_b': ssd_conv_b,
            'ssd_dt_bias': ssd_dt_bias, 'ssd_a_log': ssd_a_log, 'ssd_d': ssd_d,
            'ssd_norm_w': ssd_norm_w, 'ssd_out_w': ssd_out_w,
            'da_qkv_w': da_qkv_w, 'da_q_norm_w': da_q_norm_w, 'da_k_norm_w': da_k_norm_w,
            'da_lam_q1': da_lam_q1, 'da_lam_k1': da_lam_k1, 'da_lam_q2': da_lam_q2,
            'da_lam_k2': da_lam_k2, 'da_subln_w': da_subln_w, 'da_out_w': da_out_w,
            'peer_query_w': peer_query_w, 'peer_sub_keys': peer_sub_keys,
            'peer_u': peer_u, 'peer_v': peer_v}

def reference(x, mix_norm_w, ffn_norm_w, ssd_in_w, ssd_conv_w, ssd_conv_b, ssd_dt_bias,
              ssd_a_log, ssd_d, ssd_norm_w, ssd_out_w, da_qkv_w, da_q_norm_w, da_k_norm_w,
              da_lam_q1, da_lam_k1, da_lam_q2, da_lam_k2, da_subln_w, da_out_w,
              peer_query_w, peer_sub_keys, peer_u, peer_v):
    for i in range(DEPTH):
        hn = rms_norm(x, mix_norm_w[i])
        j = i // N_MIXERS
        if i % N_MIXERS == 0:
            y = ssd_mixer(hn, ssd_in_w[j], ssd_conv_w[j], ssd_conv_b[j], ssd_dt_bias[j],
                          ssd_a_log[j], ssd_d[j], ssd_norm_w[j], ssd_out_w[j])
        else:
            lambda_init = 0.8 - 0.6 * math.exp(-0.3 * i)
            y = diff_attention(hn, da_qkv_w[j], da_q_norm_w[j], da_k_norm_w[j], da_lam_q1[j],
                               da_lam_k1[j], da_lam_q2[j], da_lam_k2[j], da_subln_w[j],
                               da_out_w[j], lambda_init)
        x = x + y
        hn = rms_norm(x, ffn_norm_w[i])
        x = x + peer_ffn(hn, peer_query_w[i], peer_sub_keys[i], peer_u[i], peer_v[i])
    return x


_drawn_inputs = setup_inputs


def setup_inputs(seed=0):
    import zlib

    import numpy as np

    out = dict(_drawn_inputs(seed))
    spreads = {}
    factors = {'da_q_norm_w': 4.57, 'da_k_norm_w': 4.376, 'da_lam_q1': 6.285, 'da_subln_w': 4.192}
    for name, (base, spread) in spreads.items():
        noise = np.random.default_rng([zlib.crc32(name.encode()), seed]).standard_normal(out[name].shape)
        drawn = base * np.exp(spread * noise) if base else spread * noise
        out[name] = __import__('jax').numpy.asarray(drawn.astype(out[name].dtype))
    for name, factor in factors.items():
        out[name] = (out[name] * factor).astype(out[name].dtype)
    return out
```

```python
import math
from contextlib import ExitStack

import concourse.bass as bass
from concourse import mybir

F32 = mybir.dt.float32
U32 = mybir.dt.uint32
ALU = mybir.AluOpType
ACT = mybir.ActivationFunctionType
AX = mybir.AxisListType

P = 128
T = 256
NB = T // P
D = 1024
KD = D // P
DEPTH = 2
EPS = 1e-6
DI = 2048
NH = 32
HP = 64
NG = 8
HG = NH // NG
NS = 128
CONV = 4
GW = HG * HP
CONV_TILES = (DI + 2 * NG * NS) // P
XS_TILES = DI // P
AH = 8
AD = 64
LAMBDA_INIT = 0.8 - 0.6 * math.exp(-0.3 * 1)
MASKED = -1e30
PH = 8
NK = 128
TOPK = 16
NE = NK * NK
HC = 2 * PH
PAIRS = PH * TOPK
GRP = 8
DIAGS = 4
CAND_LEN = [TOPK // (i + 1) for i in range(TOPK)]
CAND_OFF = [sum(CAND_LEN[:i]) for i in range(TOPK)]
NC = sum(CAND_LEN)
ATANH = [1.0 / (2 * k + 1) for k in range(1, 10)]

WCOLS = 512
WSLOTS = 3
MM_BANKS = 6


def psum_plan():
    order = []

    def norm(i):
        order.extend(("nT", i, b, c) for b in range(NB) for c in range(2))

    def peer(layer):
        norm(2 * layer + 1)
        order.extend(("q", layer, j) for j in range(HC // 2))
        order.extend(("s", layer, b, c) for b in range(NB) for c in range(HC // 4))

    norm(0)
    order.append(("dt",))
    for j in range(CONV_TILES // 2):
        order.append(("xbc", j))
        if 2 <= j < XS_TILES // 2 + 2:
            order.append(("xT", j - 2))
    order.append(("acs",))
    order.extend(("z", b, n) for n in range(4) for b in range(NB))
    order.extend(("bT", c) for c in range(2))
    for b in range(NB):
        order.extend(("cb", b, c) for c in range(2))
        order.extend(("bc", b, g) for g in range(2))
        for g in range(NG):
            if g + 2 < NG:
                order.append(("bc", b, g + 2))
            if g % 2 == 1:
                order.append(("y", b, g // 2))
                order.append(("st" if b == 0 else "yo", g // 2))
        order.extend(("ynT", b, c) for c in range(4))
    order.extend(("out", 0, n, b) for n in range(2) for b in range(NB))
    peer(0)
    norm(2)
    order.extend(("qkv", n, b) for n in range(6) for b in range(NB))
    order.extend(("qkT", b, c) for b in range(NB) for c in range(4))
    for b in range(NB):
        for h in range(AH):
            order.extend([("S", b, h, 0), ("S", b, h, 1)])
            if h >= 1:
                order.extend([("aT", b, h - 1), ("O", b, h - 1)])
        order.extend([("aT", b, AH - 1), ("O", b, AH - 1)])
        order.extend(("oT", b, c) for c in range(2))
    order.extend(("out", 1, n, b) for n in range(2) for b in range(NB))
    peer(1)
    return {key: (n % MM_BANKS, n // MM_BANKS, n) for n, key in enumerate(order)}


def weight_plan():
    tiles = [("in", 0, 0, DI + WCOLS * j) for j in range(8)]
    tiles += [("in", 0, 0, WCOLS * j) for j in range(4)]
    tiles += [("out0", 0, KD * kh, WCOLS * n) for n in range(2) for kh in range(2)]
    tiles += [("query", 0, 0, WCOLS * j) for j in range(4)]
    tiles += [("qkv", 0, 0, WCOLS * j) for j in range(6)]
    tiles += [("out1", 0, 0, WCOLS * n) for n in range(2)]
    tiles += [("query", 1, 0, WCOLS * j) for j in range(4)]
    return tiles


def build(nc, x_in, mix_norm_w, ffn_norm_w, in_w, conv_w, conv_b, dt_bias, a_log, d_skip, ssd_norm_w,
          ssd_out_w, qkv_w, q_norm_w, k_norm_w, lam_q1, lam_k1, lam_q2, lam_k2, subln_w, da_out_w,
          query_w, keys_t, peer_u, peer_v, out):
    PLAN = psum_plan()
    WTILES = weight_plan()
    WAT = {key: n for n, key in enumerate(WTILES)}
    in_cols = in_w.shape[2]

    with ExitStack() as ctx:
        def sb(name, shape, dt=F32):
            return ctx.enter_context(nc.sbuf_tensor(name, shape, dt))

        def sem(name):
            return ctx.enter_context(nc.semaphore(name))

        ident = sb("ident", [P, P])
        tri = sb("tri", [P, P])
        ones = sb("ones", [P, P])
        mask = sb("mask", [P, NB, T])
        iota = sb("iota", [P, NC])
        eps = sb("eps", [P, 1])
        norm_w = sb("norm_w", [P, 2, D])
        w_dt = sb("w_dt", [P, KD, NH])
        cw = sb("cw", [P, CONV_TILES, CONV])
        cb = sb("cb", [P, CONV_TILES])
        dtb = sb("dtb", [P, NH])
        alog = sb("alog", [P, NH])
        dsk = sb("dsk", [P, NH])
        snw = sb("snw", [P, XS_TILES])
        qkn = sb("qkn", [P, 2])
        lams = sb("lams", [P, 4, AD])
        sub_w = sb("sub_w", [P, 1])
        x = sb("x", [P, NB, D])
        hn = sb("hn", [P, NB, D])
        hnT = sb("hnT", [P, KD, T])
        wring = sb("wring", [P, WSLOTS, KD, WCOLS])
        keysT = sb("keysT", [P, HC, NK])
        stat = sb("stat", [P, 8, 4])
        ring = sb("ring", [P, 2 * GRP, D])
        ring_flat = ring[:, :, :].rearrange("p a b -> p (a b)")
        tmp = sb("tmp", [P, 8192])

        def view(base, off, *dims):
            n = math.prod(dims)
            v = base[:, off:off + n]
            if len(dims) == 2:
                return v.rearrange("p (a b) -> p a b", a=dims[0])
            if len(dims) == 3:
                return v.rearrange("p (a b c) -> p a b c", a=dims[0], b=dims[1])
            return v

        xh = view(ring_flat, 0, NB, DI)
        bcT = view(ring_flat, 4096, 2 * NG, T)
        zs = view(ring_flat, 8192, NB, DI)
        ynT = view(ring_flat, 12288, XS_TILES, T)
        tmp_ap = tmp[:, :]
        xd = view(tmp_ap, 0, NH, HP)
        y = view(tmp_ap, 2048, DI)
        state = view(tmp_ap, 4096, DI)
        cv = view(tmp_ap, 6144, 4, T)
        xsT = view(tmp_ap, 7168, 4, T)
        seg = view(tmp_ap, 6144, 4, HG * P)
        xde = view(ring_flat, 12288, NH, HP)
        b_tok = view(ring_flat, 14336, NG, NS)
        qk = view(ring_flat, 0, NB, 2 * D)
        vv = view(ring_flat, 4096, NB, D)
        qkT = view(ring_flat, 6144, 2 * AH, T)
        o_sb = view(ring_flat, 10240, NB, D)
        oT = view(ring_flat, 12288, AH, T)
        prob = view(tmp_ap, 0, 2, 2, T)
        attn = view(tmp_ap, 1024, 2, T)
        attnT = view(tmp_ap, 1536, 2, T)
        sq = view(tmp_ap, 2048, 2, WCOLS)
        qT = view(tmp_ap, 0, HC, T)
        sc = view(tmp_ap, 4096, HC, NK)
        eq = view(tmp_ap, 6144, 2, TOPK, NC)
        small = sb("small", [P, 1600])
        small_ap = small[:, :]
        junk = sb("junk", [P, GW])
        topv = view(small_ap, 0, HC, TOPK)
        topi = view(small_ap, 256, HC, TOPK).bitcast(U32)
        topf = view(small_ap, 512, HC, TOPK)
        cs = view(small_ap, 768, PH, NC)
        ci = view(small_ap, 1168, PH, NC)
        best = sb("best", [P, PH, TOPK])
        posi = sb("posi", [P, PH, TOPK], U32)
        posf = sb("posf", [P, PH, TOPK])
        bsub = sb("bsub", [P, PH, TOPK])
        gsum = sb("gsum", [P, 2, PH])
        gate = sb("gate", [P, NB, PAIRS])
        idx = sb("idx", [P, NB, PAIRS], U32)
        idxf = sb("idxf", [P, PAIRS])
        idx_now = sb("idx_now", [P, 2, GRP], U32)
        acts = sb("acts", [P, 2, GRP])
        gel = sb("gel", [P, 2, GRP])
        wts = sb("wts", [P, 2, GRP])
        diag = sb("diag", [P, DIAGS, P])
        dts = sb("dts", [P, NB, NH])
        adt = sb("adt", [P, NB, NH])
        acs = sb("acs", [P, 2 * NB, NH])
        eacs = sb("eacs", [P, NH])
        toend = sb("toend", [P, NH])
        spt = view(tmp_ap, 4096, 6, NB * NH)
        expa = sb("expa", [P, NH])
        cbm = view(small_ap, 0, NG, P)
        yoff = view(small_ap, 1024, WCOLS)
        gst = sb("gst", [P, 3, NG])
        qst = sb("qst", [P, 3, NB, 2 * 2 * AH])
        lam = sb("lam", [P, 8])
        smx = sb("smx", [P, 4, 2, 2])
        ost = sb("ost", [P, 3, NB, AH])

        banks = [ctx.enter_context(nc.psum_tensor(f"mm{i}", [P, 512], F32)) for i in range(MM_BANKS)]
        ysum = [ctx.enter_context(nc.psum_tensor(f"ysum{i}", [P, 512], F32)) for i in range(2)]

        x_loaded = sem("x_loaded")
        wdt_loaded = sem("wdt_loaded")
        conv_loaded = sem("conv_loaded")
        dt_loaded = sem("dt_loaded")
        ssd_loaded = sem("ssd_loaded")
        attn_loaded = sem("attn_loaded")
        normw_loaded = [sem(f"normw{i}_loaded") for i in range(2 * DEPTH)]
        keys_loaded = sem("keys_loaded")
        w_loaded = [sem(f"w{i}_loaded") for i in range(WSLOTS)]
        consts = sem("consts_ready")
        mm_done = sem("mm_done")
        bank_read = [sem(f"bank{i}_read") for i in range(MM_BANKS)]
        dve_seq = sem("dve_seq")
        act_seq = sem("act_seq")
        std_ready = sem("std_ready")
        hn_ready = sem("hn_ready")
        x_fed = sem("x_fed")
        dt_abs_ready = sem("dt_abs_ready")
        dt_exp_ready = sem("dt_exp_ready")
        adt_ready = sem("adt_ready")
        first_tap_ready = sem("first_tap_ready")
        silu_ready = sem("silu_ready")
        toend_ready = sem("toend_ready")
        eacs_ready = sem("eacs_ready")
        xd_ready = sem("xd_ready")
        xde_ready = sem("xde_ready")
        decay_ready = sem("decay_ready")
        m_ready = sem("m_ready")
        gated_ready = sem("gated_ready")
        gstd_ready = sem("gstd_ready")
        yn_ready = sem("yn_ready")
        sq_ready = sem("sq_ready")
        qss_ready = sem("qss_ready")
        qstd_ready = sem("qstd_ready")
        qn_ready = sem("qn_ready")
        lamdot_ready = sem("lamdot_ready")
        lamexp_ready = sem("lamexp_ready")
        max_ready = sem("max_ready")
        exp_ready = sem("exp_ready")
        attn_ready = sem("attn_ready")
        ostd_ready = sem("ostd_ready")
        on_ready = sem("on_ready")
        s_used = sem("s_used")
        gsub_ready = sem("gsub_ready")
        gexp_ready = sem("gexp_ready")
        idx_ready = sem("idx_ready")
        idx_now_ready = sem("idx_now_ready")
        u_loaded = [sem(f"u{i}_loaded") for i in range(GRP)]
        v_loaded = [sem(f"v{i}_loaded") for i in range(GRP)]
        u_free = sem("u_free")
        v_free = sem("v_free")
        gelu_ready = sem("gelu_ready")
        wts_ready = sem("wts_ready")
        diag_ready = sem("diag_ready")
        stored = sem("stored")

        def bank(key):
            return banks[PLAN[key][0]]

        def produced(eng, key):
            eng.wait_ge(mm_done, PLAN[key][2] + 1)

        def read_of(key):
            return bank_read[PLAN[key][0]]

        def moved(eng, key):
            eng.wait_ge(read_of(key), PLAN[key][1] + 1)

        def w_tile(*key):
            return wring[:, WAT[key] % WSLOTS]

        def w_landed(eng, *key):
            n = WAT[key]
            eng.wait_ge(w_loaded[n % WSLOTS], 16 * (n // WSLOTS + 1))

        def last_use(key):
            name, layer, _, c0 = key
            if name == "in":
                return ("xbc", 2 * ((c0 - DI) // WCOLS) + 1) if c0 >= DI else ("z", NB - 1, c0 // WCOLS)
            if name == "query":
                return ("q", layer, 2 * (c0 // WCOLS) + 1)
            if name == "qkv":
                return ("qkv", c0 // WCOLS, NB - 1)
            return ("out", 0 if name == "out0" else 1, c0 // WCOLS, NB - 1)

        def bcast(ap, n):
            return ap.unsqueeze(2).broadcast_to([ap.shape[0], ap.shape[1], n])

        block = ctx.enter_context(nc.Block())

        @block.sync
        def _(sp):
            sp.dma_start(x[:], x_in.rearrange("a (b p) d -> p (a b) d", p=P)).then_inc(x_loaded, 16)
            sp.dma_start(norm_w[:, 0], mix_norm_w[0:1, :].broadcast_to([P, D])).then_inc(normw_loaded[0], 16)
            sp.dma_start(w_dt[:], in_w[0].rearrange("(k p) n -> p k n", p=P)[:, :, in_cols - NH:in_cols]) \
                .then_inc(wdt_loaded, 16)
            dram = {
                "in": in_w, "out0": ssd_out_w, "qkv": qkv_w, "out1": da_out_w, "query": query_w,
            }

            def weight(n):
                name, layer, k0, c0 = WTILES[n]
                if n >= WSLOTS:
                    produced(sp, last_use(WTILES[n - WSLOTS]))
                src = dram[name][layer].rearrange("(k p) n -> p k n", p=P)[:, k0:k0 + KD, c0:c0 + WCOLS]
                sp.dma_start(wring[:, n % WSLOTS], src).then_inc(w_loaded[n % WSLOTS], 16)

            for n in range(WSLOTS):
                weight(n)
            sp.dma_start(norm_w[:, 1], ffn_norm_w[0:1, :].broadcast_to([P, D])).then_inc(normw_loaded[1], 16)
            sp.dma_start(keysT[:], keys_t[0].rearrange("h d n -> d h n")).then_inc(keys_loaded, 16)
            second = WAT[("qkv", 0, 0, 0)]
            for n in range(WSLOTS, second):
                weight(n)
            sp.wait_ge(hn_ready, 2 * NB)
            sp.dma_start(norm_w[:, 0], mix_norm_w[1:2, :].broadcast_to([P, D])).then_inc(normw_loaded[2], 16)
            sp.dma_start(norm_w[:, 1], ffn_norm_w[1:2, :].broadcast_to([P, D])).then_inc(normw_loaded[3], 16)
            produced(sp, ("s", 0, NB - 1, HC // 4 - 1))
            sp.dma_start(keysT[:], keys_t[1].rearrange("h d n -> d h n")).then_inc(keys_loaded, 16)
            for n in range(second, len(WTILES)):
                weight(n)
            for b in range(NB):
                sp.wait_ge(x_fed, 2 * (NB + b) + 2)
                sp.dma_start(out[0, b * P:(b + 1) * P, :], x[:, b]).then_inc(stored, 16)
            sp.wait_ge(stored, 16 * NB)

        @block.gpsimd
        def _(pool):
            pool.memset(ones[:], 1.0).then_inc(consts, 1)
            pool.memset(eps[:], EPS).then_inc(consts, 1)
            pool.memset(mask[:], 0.0).then_inc(consts, 1)
            pool.memset(ident[:], 0.0).then_inc(consts, 1)
            pool.iota(iota[:], pattern=[[1, NC]], base=0, channel_multiplier=0,
                      allow_small_or_imprecise_dtypes=True).then_inc(consts, 1)
            pool.wait_ge(consts, 5)
            pool.affine_select(out=ident[:], in_=ident[:], compare_op=ALU.not_equal, fill=1.0, base=0,
                               pattern=[[-1, P]], channel_multiplier=1).then_inc(consts, 1)
            pool.affine_select(out=tri[:], in_=ones[:], compare_op=ALU.is_ge, fill=0.0, base=0,
                               pattern=[[1, P]], channel_multiplier=-1).then_inc(consts, 1)
            for b in range(NB):
                pool.memset(mask[0:P // 2, b, b * P + P // 2:(b + 1) * P], MASKED).then_inc(consts, 1)
            pool.sem_inc(u_free, GRP)
            pool.sem_inc(v_free, GRP)

            u_rows, v_rows = (t.rearrange("l e d -> (l e) d") for t in (peer_u, peer_v))

            def gather(layer, b):
                g0 = (layer * NB + b) * (PAIRS // GRP)
                pool.wait_ge(idx_ready, layer * NB + b + 1)
                with pool.Fori(0, PAIRS // GRP // 2) as i:
                    for h in range(2):
                        pool.tensor_copy(idx_now[:, h], idx[:, b, bass.ds(i * (2 * GRP) + h * GRP, GRP)]) \
                            .then_inc(idx_now_ready, 1)
                        pool.wait_ge(idx_now_ready, i * 2 + (g0 + h + 1))
                        for k in range(GRP):
                            pool.wait_ge(u_free, i * (2 * GRP) + ((g0 + h) * GRP + k + 1))
                            pool.nop(nofuse=True)
                            pool.indirect_dma_start(
                                ring[:, k, :], None, u_rows,
                                bass.IndirectOffsetOnAxis(idx_now[:, h, k:k + 1], 0)).then_inc(u_loaded[k], 16)
                        for k in range(GRP):
                            pool.wait_ge(v_free, i * (2 * GRP) + ((g0 + h) * GRP + k + 1))
                            pool.nop(nofuse=True)
                            pool.indirect_dma_start(
                                ring[:, GRP + k, :], None, v_rows,
                                bass.IndirectOffsetOnAxis(idx_now[:, h, k:k + 1], 0)).then_inc(v_loaded[k], 16)

            for layer in range(DEPTH):
                for b in range(NB):
                    gather(layer, b)

        @block.scalar
        def _(act):
            seq = [0]

            def step(ins):
                seq[0] += 1
                ins.then_inc(act_seq, 1)

            def settle():
                act.wait_ge(act_seq, seq[0])

            act.dma_start(dtb[:], dt_bias.broadcast_to([P, NH])).then_inc(dt_loaded, 16)
            act.dma_start(alog[:], a_log.broadcast_to([P, NH])).then_inc(dt_loaded, 16)
            act.dma_start(cw[:], conv_w).then_inc(conv_loaded, 16)
            act.dma_start(cb[:], conv_b).then_inc(conv_loaded, 16)
            act.dma_start(dsk[:], d_skip.broadcast_to([P, NH])).then_inc(ssd_loaded, 16)
            act.dma_start(snw[:], ssd_norm_w).then_inc(ssd_loaded, 16)
            for half in range(2):
                rows = slice(half * AD, (half + 1) * AD)
                act.dma_start(qkn[rows, 0:1], q_norm_w.rearrange("a d -> d a")).then_inc(attn_loaded, 16)
                act.dma_start(qkn[rows, 1:2], k_norm_w.rearrange("a d -> d a")).then_inc(attn_loaded, 16)
            for j, v in enumerate((lam_q1, lam_k1, lam_q2, lam_k2)):
                act.dma_start(lams[:, j], v.broadcast_to([P, AD])).then_inc(attn_loaded, 16)
            act.dma_start(sub_w[:], subln_w.rearrange("a d -> d a")).then_inc(attn_loaded, 16)

            def norm(i):
                if i == 0:
                    act.wait_ge(x_loaded, 16)
                    act.wait_ge(consts, 5)
                for b in range(NB):
                    if i % 2 == 1:
                        moved(act, ("out", i // 2, 1, b))
                    elif i:
                        act.wait_ge(x_fed, 2 * b + 2)
                    if i:
                        produced(act, ("nT", i - 1, b, 1))
                    step(act.activation(hn[:, b], x[:, b], ACT.Square, accum_out=stat[:, 2 * i + b, 0:1]))
                    settle()
                    act.activation(stat[:, 2 * i + b, 1:2], stat[:, 2 * i + b, 0:1], ACT.Sqrt,
                                   scale=1.0 / D, bias=eps[:, 0:1]).then_inc(std_ready, 1)
                for b in range(NB):
                    for c in range(2):
                        key = ("nT", i, b, c)
                        produced(act, key)
                        act.activation(hnT[:, 4 * c:4 * c + 4, b * P:(b + 1) * P],
                                       bank(key)[:, :].rearrange("p (c t) -> p c t", c=4),
                                       ACT.Copy).then_inc(read_of(key), 1)

            def ssd():
                act.wait_ge(dt_loaded, 32)
                step(act.activation(expa[:], alog[:], ACT.Exp))
                act.wait_ge(dt_abs_ready, 1)
                act.activation(spt[:, 2], spt[:, 1], ACT.Exp, scale=-1.0).then_inc(dt_exp_ready, 1)
                act.wait_ge(conv_loaded, 32)

                def first_tap(j):
                    key = ("xbc", j)
                    produced(act, key)
                    for s in range(2):
                        c = 2 * j + s
                        if j >= 2:
                            act.wait_ge(silu_ready, c - 3)
                        act.activation(cv[:, c % 4], bank(key)[:, s * T:(s + 1) * T], ACT.Identity,
                                       scale=cw[:, c, CONV - 1:CONV], bias=cb[:, c:c + 1]) \
                            .then_inc(first_tap_ready, 1)

                def silu(j):
                    moved(act, ("xbc", j))
                    for s in range(2):
                        c = 2 * j + s
                        if c < XS_TILES:
                            if j >= 2:
                                produced(act, ("xT", j - 2))
                            dst = xsT[:, c % 4]
                        else:
                            dst = bcT[:, c - XS_TILES]
                        act.activation(dst, cv[:, c % 4], ACT.Silu).then_inc(silu_ready, 1)

                def x_tokens(j):
                    key = ("xT", j)
                    produced(act, key)
                    act.activation(xh[:, :, 2 * j * P:(2 * j + 2) * P],
                                   bank(key)[:, :].rearrange("p (b c) -> p b c", b=NB),
                                   ACT.Copy).then_inc(read_of(key), 1)

                pairs = CONV_TILES // 2
                for j in range(pairs + 2):
                    if j < pairs:
                        first_tap(j)
                    if 1 <= j <= pairs:
                        silu(j - 1)
                    if 2 <= j < XS_TILES // 2 + 2:
                        x_tokens(j - 2)
                for n in range(4):
                    for b in range(NB):
                        key = ("z", b, n)
                        produced(act, key)
                        act.activation(zs[:, b, n * WCOLS:(n + 1) * WCOLS], bank(key)[:, :],
                                       ACT.Silu).then_inc(read_of(key), 1)
                for c in range(2):
                    key = ("bT", c)
                    produced(act, key)
                    act.activation(b_tok[:, 4 * c:4 * c + 4],
                                   bank(key)[:, :].rearrange("p (g n) -> p g n", g=4),
                                   ACT.Copy).then_inc(read_of(key), 1)
                act.wait_ge(toend_ready, 1)
                act.activation(toend[:], toend[:], ACT.Exp).then_inc(eacs_ready, 1)
                act.activation(eacs[:], acs[:, 1], ACT.Exp).then_inc(eacs_ready, 1)
                for b in range(NB):
                    for g in range(NG):
                        moved(act, ("bc", b, g))
                        act.activation(seg[:, g % 4], seg[:, g % 4], ACT.Exp).then_inc(decay_ready, 1)
                        if b == 0 and g % 2 == 1 and g > 1:
                            state_out(act, g // 2 - 1)
                    if b == 0:
                        state_out(act, NG // 2 - 1)
                    act.wait_ge(gated_ready, b + 1)
                    for g in range(NG):
                        settle()
                        step(act.activation(junk[:, 0:GW], y[:, g * GW:(g + 1) * GW], ACT.Square,
                                            accum_out=gst[:, 0, g:g + 1]))
                    settle()
                    act.activation(gst[:, 1], gst[:, 0], ACT.Sqrt, scale=1.0 / GW,
                                   bias=eps[:, 0:1]).then_inc(gstd_ready, 1)

            def state_out(act, q):
                key = ("st", q)
                produced(act, key)
                act.activation(state[:, q * WCOLS:(q + 1) * WCOLS], bank(key)[:, :],
                               ACT.Copy).then_inc(read_of(key), 1)

            def attention():
                act.wait_ge(lamdot_ready, 2)
                act.activation(lam[:, 2:4], lam[:, 0:2], ACT.Exp).then_inc(lamexp_ready, 1)
                for n in range(6):
                    for b in range(NB):
                        key = ("qkv", n, b)
                        produced(act, key)
                        if n < 4:
                            m = n * NB + b
                            if m >= 2:
                                act.wait_ge(qss_ready, m - 1)
                            act.activation(sq[:, m % 2], bank(key)[:, :], ACT.Square).then_inc(sq_ready, 1)
                            act.activation(qk[:, b, n * WCOLS:(n + 1) * WCOLS], bank(key)[:, :],
                                           ACT.Copy).then_inc(read_of(key), 1)
                        else:
                            act.activation(vv[:, b, (n - 4) * WCOLS:(n - 3) * WCOLS], bank(key)[:, :],
                                           ACT.Copy).then_inc(read_of(key), 1)
                act.wait_ge(qss_ready, 4 * NB)
                act.activation(qst[:, 1], qst[:, 0], ACT.Sqrt, scale=1.0 / AD,
                               bias=eps[:, 0:1]).then_inc(qstd_ready, 1)
                for b in range(NB):
                    nk = (b + 1) * P

                    def weighted(h):
                        key = ("aT", b, h)
                        produced(act, key)
                        if b * AH + h >= 2:
                            produced(act, ("O", b, h - 2) if h >= 2 else ("O", b - 1, AH + h - 2))
                        act.activation(attnT[:, h % 2, 0:nk], bank(key)[:, 0:nk], ACT.Copy) \
                            .then_inc(read_of(key), 1)
                        key = ("O", b, h)
                        produced(act, key)
                        settle()
                        step(act.activation(junk[:, 0:P], bank(key)[:, 0:P], ACT.Square,
                                            accum_out=ost[:, 0, b, h:h + 1]))
                        act.activation(o_sb[:, b, h * P:(h + 1) * P], bank(key)[:, 0:P], ACT.Copy) \
                            .then_inc(read_of(key), 1)

                    for h in range(AH):
                        act.wait_ge(max_ready, b * AH + h + 1)
                        for m in range(2):
                            act.activation(prob[:, h % 2, m, 0:nk], prob[:, h % 2, m, 0:nk], ACT.Exp,
                                           bias=smx[:, 0, h % 2, m:m + 1],
                                           accum_out=smx[:, 1, h % 2, m:m + 1]).then_inc(exp_ready, 1)
                        if h >= 1:
                            weighted(h - 1)
                    weighted(AH - 1)
                    settle()
                    act.activation(ost[:, 1, b], ost[:, 0, b], ACT.Sqrt, scale=1.0 / P,
                                   bias=eps[:, 0:1]).then_inc(ostd_ready, 1)

            def select(layer):
                for j in range(HC // 2):
                    key = ("q", layer, j)
                    produced(act, key)
                    act.activation(qT[:, 2 * j:2 * j + 2], bank(key)[:, :].rearrange("p (a t) -> p a t", a=2),
                                   ACT.Copy).then_inc(read_of(key), 1)
                for b in range(NB):
                    for c in range(HC // 4):
                        key = ("s", layer, b, c)
                        produced(act, key)
                        if layer * NB + b >= 1:
                            act.wait_ge(s_used, layer * NB + b)
                        act.activation(sc[:, 4 * c:4 * c + 4],
                                       bank(key)[:, :].rearrange("p (a t) -> p a t", a=4),
                                       ACT.Copy).then_inc(read_of(key), 1)
                    act.wait_ge(gsub_ready, layer * NB + b + 1)
                    act.activation(bsub[:], bsub[:], ACT.Exp).then_inc(gexp_ready, 1)

            def experts(layer, b):
                g0 = (layer * NB + b) * (PAIRS // GRP)
                with act.Fori(0, PAIRS // GRP // 2) as i:
                    for h in range(2):
                        act.wait_ge(u_free, i * (2 * GRP) + (g0 + h + 2) * GRP)
                        act.activation(gel[:, h], acts[:, h], ACT.Gelu).then_inc(gelu_ready, 1)
                        act.wait_ge(wts_ready, i * 2 + (g0 + h + 1))
                        for k in range(GRP):
                            act.wait_ge(v_free, i * (2 * GRP) + ((g0 + h + 1) * GRP - DIAGS + k + 1))
                            act.activation(diag[:, k % DIAGS], ident[:], ACT.Copy, scale=wts[:, h, k:k + 1]) \
                                .then_inc(diag_ready, 1)

            norm(0)
            ssd()
            norm(1)
            select(0)
            for b in range(NB):
                experts(0, b)
            norm(2)
            attention()
            norm(3)
            select(1)
            for b in range(NB):
                experts(1, b)

        @block.tensor
        def _(pe):
            def take(key):
                bk, nth, _ = PLAN[key]
                if nth:
                    pe.wait_ge(bank_read[bk], nth)
                return banks[bk]

            def mm(out_, lhsT, rhs, start=True, stop=True):
                return nc.tensor.matmul(out_, lhsT, rhs, start=start, stop=stop)

            def norm(i):
                for b in range(NB):
                    for c in range(2):
                        bk = take(("nT", i, b, c))
                        pe.wait_ge(hn_ready, NB * i + b + 1)
                        if i == 0:
                            pe.wait_ge(consts, 6)
                        for k in range(4):
                            last = nc.tensor.transpose(bk[:, k * P:(k + 1) * P],
                                                       hn[:, b, (4 * c + k) * P:(4 * c + k + 1) * P], ident[:])
                        last.then_inc(mm_done, 1)
                for b in range(NB):
                    for c in range(2):
                        moved(pe, ("nT", i, b, c))

            def project(out_, wcols, tok):
                for k in range(KD):
                    last = mm(out_, wcols(k), tok(k), k == 0, k == KD - 1)
                return last

            def ssd():
                pe.wait_ge(wdt_loaded, 16)
                bk = take(("dt",))
                for b in range(NB):
                    last = project(bk[:, b * NH:(b + 1) * NH], lambda k: hnT[:, k, b * P:(b + 1) * P],
                                   lambda k: w_dt[:, k])
                last.then_inc(mm_done, 1)

                def x_tokens(j):
                    bk = take(("xT", j))
                    pe.wait_ge(silu_ready, 2 * j + 2)
                    for s in range(2):
                        for b in range(NB):
                            last = nc.tensor.transpose(bk[:, (2 * b + s) * P:(2 * b + s + 1) * P],
                                                       xsT[:, (2 * j + s) % 4, b * P:(b + 1) * P], ident[:])
                    last.then_inc(mm_done, 1)

                for j in range(CONV_TILES // 2):
                    key = ("in", 0, 0, DI + WCOLS * (j // 2))
                    w_landed(pe, *key)
                    w = w_tile(*key)
                    bk = take(("xbc", j))
                    for s in range(2):
                        c0 = (2 * (j % 2) + s) * P
                        last = project(bk[:, s * T:(s + 1) * T], lambda k: w[:, k, c0:c0 + P],
                                       lambda k: hnT[:, k])
                    last.then_inc(mm_done, 1)
                    if 2 <= j < XS_TILES // 2 + 2:
                        x_tokens(j - 2)
                bk = take(("acs",))
                pe.wait_ge(adt_ready, 1)
                pe.wait_ge(consts, 7)
                for b in range(NB):
                    mm(bk[:, b * NH:(b + 1) * NH], tri[:], adt[:, b])
                mm(bk[:, NB * NH:2 * NB * NH], ones[:], adt[:, :, :].rearrange("p b h -> p (b h)")) \
                    .then_inc(mm_done, 1)
                for n in range(4):
                    key = ("in", 0, 0, WCOLS * n)
                    w_landed(pe, *key)
                    w = w_tile(*key)
                    for b in range(NB):
                        bk = take(("z", b, n))
                        project(bk[:, :], lambda k: hnT[:, k, b * P:(b + 1) * P], lambda k: w[:, k]) \
                            .then_inc(mm_done, 1)
                pe.wait_ge(silu_ready, CONV_TILES)
                for c in range(2):
                    bk = take(("bT", c))
                    for g in range(4):
                        last = nc.tensor.transpose(bk[:, g * P:(g + 1) * P], bcT[:, 4 * c + g, 0:P], ident[:])
                    last.then_inc(mm_done, 1)
                for b in range(NB):
                    scan(b)
                for n in range(2):
                    bks = [take(("out", 0, n, b)) for b in range(NB)]
                    for kh in range(2):
                        key = ("out0", 0, KD * kh, WCOLS * n)
                        w_landed(pe, *key)
                        w = w_tile(*key)
                        for b in range(NB):
                            moved(pe, ("ynT", b, 3))
                            for k in range(KD):
                                last = mm(bks[b][:, :], ynT[:, KD * kh + k, b * P:(b + 1) * P], w[:, k],
                                          kh == 0 and k == 0, kh == 1 and k == KD - 1)
                            if kh == 1:
                                last.then_inc(mm_done, 1)

            def scan(b):
                tok = slice(b * P, (b + 1) * P)
                for c in range(2):
                    bk = take(("cb", b, c))
                    for g in range(4):
                        last = mm(bk[:, g * P:(g + 1) * P], bcT[:, 4 * c + g, tok], bcT[:, NG + 4 * c + g, tok])
                    last.then_inc(mm_done, 1)

                def sums_on_all(g):
                    bk = take(("bc", b, g))
                    for e in range(HG):
                        h = g * HG + e
                        last = mm(bk[:, e * P:(e + 1) * P], adt[:, b, h:h + 1].broadcast_to([P, P]), tri[:])
                    last.then_inc(mm_done, 1)

                sums_on_all(0)
                sums_on_all(1)
                for g in range(NG):
                    if g + 2 < NG:
                        sums_on_all(g + 2)
                    if g % 2 == 0:
                        bk = take(("y", b, g // 2))
                    pe.wait_ge(m_ready, b * NG + g + 1)
                    pe.wait_ge(xd_ready, b + 1)
                    for e in range(HG):
                        c0 = (g % 2) * GW + e * HP
                        last = mm(bk[:, c0:c0 + HP], seg[:, g % 4, e * P:(e + 1) * P], xd[:, g * HG + e])
                    if g % 2 == 0:
                        continue
                    last.then_inc(mm_done, 1)
                    bk = take(("st" if b == 0 else "yo", g // 2))
                    for gg in (g - 1, g):
                        cols = slice((gg % 2) * GW, (gg % 2 + 1) * GW)
                        if b == 0:
                            moved(pe, ("bT", 1))
                            pe.wait_ge(xde_ready, 1)
                            last = mm(bk[:, cols], b_tok[:, gg],
                                      xde[:, gg * HG:(gg + 1) * HG].rearrange("p a b -> p (a b)"))
                        else:
                            moved(pe, ("st", NG // 2 - 1))
                            last = mm(bk[:, cols], bcT[:, NG + gg, tok], state[:, gg * GW:(gg + 1) * GW])
                    last.then_inc(mm_done, 1)
                pe.wait_ge(yn_ready, b + 1)
                for c in range(4):
                    bk = take(("ynT", b, c))
                    for k in range(4):
                        last = nc.tensor.transpose(bk[:, k * P:(k + 1) * P],
                                                   y[:, (4 * c + k) * P:(4 * c + k + 1) * P], ident[:])
                    last.then_inc(mm_done, 1)

            def attention():
                for n in range(6):
                    key = ("qkv", 0, 0, WCOLS * n)
                    w_landed(pe, *key)
                    w = w_tile(*key)
                    for b in range(NB):
                        bk = take(("qkv", n, b))
                        project(bk[:, :], lambda k: hnT[:, k, b * P:(b + 1) * P], lambda k: w[:, k]) \
                            .then_inc(mm_done, 1)
                for b in range(NB):
                    pe.wait_ge(qn_ready, b + 1)
                    for c in range(4):
                        bk = take(("qkT", b, c))
                        for k in range(4):
                            last = nc.tensor.transpose(bk[:, k * P:(k + 1) * P],
                                                       qk[:, b, (4 * c + k) * P:(4 * c + k + 1) * P], ident[:])
                        last.then_inc(mm_done, 1)
                for b in range(NB):
                    nk = (b + 1) * P
                    moved(pe, ("qkT", b, 3))

                    def weighted(h):
                        bk = take(("aT", b, h))
                        pe.wait_ge(attn_ready, b * AH + h + 1)
                        for kb in range(b + 1):
                            last = nc.tensor.transpose(bk[:, kb * P:(kb + 1) * P],
                                                       attn[:, h % 2, kb * P:(kb + 1) * P], ident[:])
                        last.then_inc(mm_done, 1)
                        bk = take(("O", b, h))
                        moved(pe, ("aT", b, h))
                        for kb in range(b + 1):
                            last = mm(bk[:, 0:P], attnT[:, h % 2, kb * P:(kb + 1) * P],
                                      vv[:, kb, h * P:(h + 1) * P], kb == 0, kb == b)
                        last.then_inc(mm_done, 1)

                    for h in range(AH):
                        for m in range(2):
                            bk = take(("S", b, h, m))
                            rows = slice(m * AD, (m + 1) * AD)
                            mm(bk[:, 0:nk], qkT[rows, h, b * P:(b + 1) * P], qkT[rows, AH + h, 0:nk]) \
                                .then_inc(mm_done, 1)
                        if h >= 1:
                            weighted(h - 1)
                    weighted(AH - 1)
                    pe.wait_ge(on_ready, b + 1)
                    for c in range(2):
                        bk = take(("oT", b, c))
                        for k in range(4):
                            last = nc.tensor.transpose(bk[:, k * P:(k + 1) * P],
                                                       o_sb[:, b, (4 * c + k) * P:(4 * c + k + 1) * P], ident[:])
                        last.then_inc(mm_done, 1)
                for n in range(2):
                    key = ("out1", 0, 0, WCOLS * n)
                    w_landed(pe, *key)
                    w = w_tile(*key)
                    for b in range(NB):
                        bk = take(("out", 1, n, b))
                        moved(pe, ("oT", b, 1))
                        project(bk[:, :], lambda k: oT[:, k, b * P:(b + 1) * P], lambda k: w[:, k]) \
                            .then_inc(mm_done, 1)

            def select(layer):
                for j in range(HC // 2):
                    key = ("query", layer, 0, WCOLS * (j // 2))
                    w_landed(pe, *key)
                    w = w_tile(*key)
                    bk = take(("q", layer, j))
                    for s in range(2):
                        c0 = (2 * (j % 2) + s) * P
                        last = project(bk[:, s * T:(s + 1) * T], lambda k: w[:, k, c0:c0 + P],
                                       lambda k: hnT[:, k])
                    last.then_inc(mm_done, 1)
                pe.wait_ge(keys_loaded, 16 * (layer + 1))
                for b in range(NB):
                    for c in range(HC // 4):
                        bk = take(("s", layer, b, c))
                        moved(pe, ("q", layer, 2 * c + 1))
                        for k in range(4):
                            last = mm(bk[:, k * P:(k + 1) * P], qT[:, 4 * c + k, b * P:(b + 1) * P],
                                      keysT[:, 4 * c + k])
                        last.then_inc(mm_done, 1)

            def experts(layer, b):
                n0 = (layer * NB + b) * PAIRS
                if n0:
                    pe.wait_ge(x_fed, 2 * (layer * NB + b))
                for half in range(2):
                    nc.tensor.matmul(ysum[half][:, :], ident[:], x[:, b, half * 512:(half + 1) * 512],
                                     start=True, stop=False, skip_group_check=True)
                with pe.Fori(0, PAIRS // GRP) as i:
                    for k in range(GRP):
                        pe.wait_ge(diag_ready, i * GRP + (n0 + k + 1))
                        pe.wait_ge(v_loaded[k], i * 16 + 16 * (n0 // GRP + 1))
                        for half in range(2):
                            last = nc.tensor.matmul(ysum[half][:, :], diag[:, k % DIAGS],
                                                    ring[:, GRP + k, half * 512:(half + 1) * 512],
                                                    start=False, stop=False, skip_group_check=True)
                        last.then_inc(v_free, 1)

            norm(0)
            ssd()
            norm(1)
            select(0)
            for b in range(NB):
                experts(0, b)
            norm(2)
            attention()
            norm(3)
            select(1)
            for b in range(NB):
                experts(1, b)

        @block.vector
        def _(dve):
            seq = [0]

            def step(ins):
                seq[0] += 1
                ins.then_inc(dve_seq, 1)

            def settle():
                dve.wait_ge(dve_seq, seq[0])

            V = nc.vector

            def norm(i):
                dve.wait_ge(normw_loaded[i], 16)
                for b in range(NB):
                    st = stat[:, 2 * i + b]
                    dve.wait_ge(std_ready, NB * i + b + 1)
                    step(V.reciprocal(st[:, 2:3], st[:, 1:2]))
                    settle()
                    if i:
                        produced(dve, ("nT", i - 1, b, 1))
                    V.scalar_tensor_tensor(out=hn[:, b], in0=x[:, b], scalar=st[:, 2:3], in1=norm_w[:, i % 2],
                                           op0=ALU.mult, op1=ALU.mult).then_inc(hn_ready, 1)

            def soft_plus():
                produced(dve, ("dt",))
                dve.wait_ge(dt_loaded, 32)
                v, a, e, r, r2, p = (spt[:, j] for j in range(6))
                key = ("dt",)
                V.tensor_tensor(v.rearrange("p (b h) -> p b h", b=NB),
                                bank(key)[:, 0:NB * NH].rearrange("p (b h) -> p b h", b=NB),
                                dtb[:, :].unsqueeze(1).broadcast_to([P, NB, NH]), ALU.add) \
                    .then_inc(read_of(key), 1)
                moved(dve, key)
                V.scalar_tensor_tensor(out=a, in0=v, scalar=-1.0, in1=v, op0=ALU.mult,
                                       op1=ALU.max).then_inc(dt_abs_ready, 1)
                dve.wait_ge(dt_exp_ready, 1)
                step(V.tensor_scalar(r2, e, 2.0, None, ALU.add))
                settle()
                step(V.reciprocal(p, r2))
                settle()
                step(V.tensor_tensor(r, e, p, ALU.mult))
                settle()
                step(V.tensor_tensor(r2, r, r, ALU.mult))
                settle()
                step(V.tensor_scalar(p, r2, ATANH[-1], None, ALU.mult))
                settle()
                for coef in ATANH[-2::-1]:
                    step(V.scalar_tensor_tensor(out=p, in0=p, scalar=coef, in1=r2, op0=ALU.add, op1=ALU.mult))
                    settle()
                step(V.scalar_tensor_tensor(out=p, in0=p, scalar=1.0, in1=r, op0=ALU.add, op1=ALU.mult))
                step(V.tensor_scalar(a, v, 0.0, None, ALU.max))
                settle()
                step(V.scalar_tensor_tensor(out=dts[:, :, :].rearrange("p b h -> p (b h)"), in0=p, scalar=2.0,
                                            in1=a, op0=ALU.mult, op1=ALU.add))
                settle()
                for b in range(NB):
                    last = V.scalar_tensor_tensor(out=adt[:, b], in0=dts[:, b], scalar=-1.0, in1=expa[:],
                                                  op0=ALU.mult, op1=ALU.mult)
                last.then_inc(adt_ready, 1)

            def convolve(j):
                key = ("xbc", j)
                dve.wait_ge(first_tap_ready, 2 * j + 2)
                for tap in range(CONV - 2, -1, -1):
                    back = CONV - 1 - tap
                    for s in range(2):
                        c = 2 * j + s
                        o = cv[:, c % 4, back:T]
                        last = V.scalar_tensor_tensor(out=o, in0=bank(key)[:, s * T:(s + 1) * T - back],
                                                      scalar=cw[:, c, tap:tap + 1], in1=o, op0=ALU.mult,
                                                      op1=ALU.add)
                        if tap:
                            step(last)
                    if tap:
                        settle()
                last.then_inc(read_of(key), 1)

            def ssd():
                soft_plus()
                for j in range(CONV_TILES // 2):
                    convolve(j)
                key = ("acs",)
                produced(dve, key)
                V.tensor_copy(acs[:, :, :].rearrange("p b h -> p (b h)"),
                              bank(key)[:, 0:2 * NB * NH]).then_inc(read_of(key), 1)
                moved(dve, key)
                V.tensor_tensor(toend[:], acs[:, NB], acs[:, 0], ALU.subtract).then_inc(toend_ready, 1)
                for b in range(NB):
                    scan(b)
                add_back(0)

            def scan(b):
                xb = xh[:, b].rearrange("p (h e) -> p h e", e=HP)
                if b == 0:
                    moved(dve, ("xT", XS_TILES // 2 - 1))
                    dve.wait_ge(ssd_loaded, 32)
                else:
                    produced(dve, ("y", b - 1, NG // 2 - 1))
                V.tensor_tensor(xd[:, :, :], xb, bcast(dts[:, b], HP), ALU.mult).then_inc(xd_ready, 1)
                dve.wait_ge(eacs_ready, 2)
                if b == 0:
                    dve.wait_ge(xd_ready, 1)
                    V.tensor_tensor(xde[:, :, :], xd[:, :, :], bcast(toend[:], HP), ALU.mult) \
                        .then_inc(xde_ready, 1)
                for c in range(2):
                    key = ("cb", b, c)
                    produced(dve, key)
                    V.tensor_tensor(cbm[:, 4 * c:4 * c + 4], bank(key)[:, :].rearrange("p (g l) -> p g l", g=4),
                                    tri[:, :].unsqueeze(1).broadcast_to([P, 4, P]), ALU.mult) \
                        .then_inc(read_of(key), 1)

                def differences(g):
                    key = ("bc", b, g)
                    produced(dve, key)
                    if b * NG + g >= 4:
                        pb, pg = (b, g - 4) if g >= 4 else (b - 1, g + 4)
                        produced(dve, ("y", pb, pg // 2))
                    for e in range(HG):
                        h = g * HG + e
                        last = V.tensor_scalar(seg[:, g % 4, e * P:(e + 1) * P], bank(key)[:, e * P:(e + 1) * P],
                                               acs[:, b, h:h + 1], 0.0, ALU.subtract, ALU.min)
                    last.then_inc(read_of(key), 1)

                def collect(q):
                    cols = slice(q * WCOLS, (q + 1) * WCOLS)
                    key = ("y", b, q)
                    produced(dve, key)
                    V.tensor_tensor(y[:, cols], y[:, cols], bank(key)[:, :], ALU.add).then_inc(read_of(key), 1)
                    if b:
                        key = ("yo", q)
                        produced(dve, key)
                        V.tensor_tensor(yoff.rearrange("p (h e) -> p h e", e=HP),
                                        bank(key)[:, :].rearrange("p (h e) -> p h e", e=HP),
                                        bcast(eacs[:, 2 * HG * q:2 * HG * (q + 1)], HP), ALU.mult) \
                            .then_inc(read_of(key), 1)
                        moved(dve, key)
                        moved(dve, ("y", b, q))
                        step(V.tensor_tensor(y[:, cols], y[:, cols], yoff, ALU.add))

                differences(0)
                if b:
                    produced(dve, ("ynT", b - 1, 3))
                step(V.tensor_tensor(y.rearrange("p (h e) -> p h e", e=HP), xb, bcast(dsk[:], HP), ALU.mult))
                settle()
                moved(dve, ("cb", b, 1))
                for g in range(NG):
                    if g + 1 < NG:
                        differences(g + 1)
                    dve.wait_ge(decay_ready, b * NG + g + 1)
                    sg = seg[:, g % 4].rearrange("p (e l) -> p e l", e=HG)
                    V.tensor_tensor(sg, sg, cbm[:, g:g + 1].broadcast_to([P, HG, P]), ALU.mult) \
                        .then_inc(m_ready, 1)
                    if g % 2 == 0 and g >= 2:
                        collect(g // 2 - 1)
                collect(NG // 2 - 1)
                moved(dve, ("y", b, NG // 2 - 1))
                if b:
                    settle()
                moved(dve, ("z", b, 3))
                V.tensor_tensor(y, y, zs[:, b], ALU.mult).then_inc(gated_ready, 1)
                dve.wait_ge(gstd_ready, b + 1)
                step(V.reciprocal(gst[:, 2], gst[:, 1]))
                settle()
                yg = y.rearrange("p (g c) -> p g c", g=NG)
                V.tensor_tensor(yg, yg, bcast(gst[:, 2], GW), ALU.mult).then_inc(yn_ready, 1)
                for c in range(4):
                    key = ("ynT", b, c)
                    produced(dve, key)
                    V.tensor_tensor(ynT[:, 4 * c:4 * c + 4, b * P:(b + 1) * P],
                                    bank(key)[:, :].rearrange("p (k t) -> p k t", k=4),
                                    bcast(snw[:, 4 * c:4 * c + 4], P), ALU.mult).then_inc(read_of(key), 1)

            def add_back(layer):
                for n in range(2):
                    for b in range(NB):
                        key = ("out", layer, n, b)
                        produced(dve, key)
                        xc = x[:, b, n * WCOLS:(n + 1) * WCOLS]
                        V.tensor_tensor(xc, xc, bank(key)[:, :], ALU.add).then_inc(read_of(key), 1)

            def attention():
                dve.wait_ge(attn_loaded, 16 * 9)
                for j in range(2):
                    V.tensor_tensor_reduce(lams[:, 2 * j], lams[:, 2 * j], lams[:, 2 * j + 1], 1.0, 0.0, ALU.mult,
                                           ALU.add, lam[:, j:j + 1]).then_inc(lamdot_ready, 1)
                dve.wait_ge(lamexp_ready, 1)
                step(V.tensor_tensor(lam[:, 4:5], lam[:, 2:3], lam[:, 3:4], ALU.subtract))
                settle()
                step(V.tensor_scalar(lam[:, 5:6], lam[:, 4:5], -1.0, -LAMBDA_INIT, ALU.mult, ALU.add))
                for m in range(4 * NB):
                    n, b = m // NB, m % NB
                    dve.wait_ge(sq_ready, m + 1)
                    V.tensor_reduce(qst[:, 0, b, 8 * n:8 * n + 8], sq[:, m % 2].rearrange("p (h d) -> p h d", d=AD),
                                    AX.X, ALU.add).then_inc(qss_ready, 1)
                dve.wait_ge(qstd_ready, 1)
                step(V.reciprocal(qst[:, 2], qst[:, 1]))
                settle()
                for b in range(NB):
                    q3 = qk[:, b].rearrange("p (h d) -> p h d", d=AD)
                    V.tensor_tensor(q3, q3, bcast(qst[:, 2, b], AD), ALU.mult).then_inc(qn_ready, 1)
                for b in range(NB):
                    for c in range(4):
                        key = ("qkT", b, c)
                        produced(dve, key)
                        which = c // 2
                        V.tensor_scalar(qkT[:, 4 * c:4 * c + 4, b * P:(b + 1) * P],
                                        bank(key)[:, :].rearrange("p (k t) -> p k t", k=4),
                                        qkn[:, which:which + 1], AD ** -0.5 if which == 0 else 1.0,
                                        ALU.mult, ALU.mult).then_inc(read_of(key), 1)
                for b in range(NB):
                    nk = (b + 1) * P

                    def masked(h):
                        for m in range(2):
                            key = ("S", b, h, m)
                            produced(dve, key)
                            V.tensor_tensor(prob[:, h % 2, m, 0:nk], bank(key)[:, 0:nk], mask[:, b, 0:nk],
                                            ALU.add).then_inc(read_of(key), 1)
                        for m in range(2):
                            moved(dve, ("S", b, h, m))
                        V.tensor_reduce(smx[:, 0, h % 2], prob[:, h % 2, :, 0:nk], AX.X, ALU.max,
                                        negate=True).then_inc(max_ready, 1)

                    def combined(h):
                        n = b * AH + h
                        dve.wait_ge(exp_ready, 2 * n + 2)
                        step(V.reciprocal(smx[:, 2, h % 2], smx[:, 1, h % 2]))
                        settle()
                        step(V.tensor_tensor(smx[:, 3, h % 2, 0:1], smx[:, 2, h % 2, 1:2], lam[:, 5:6], ALU.mult))
                        if n >= 2:
                            produced(dve, ("aT", b, h - 2) if h >= 2 else ("aT", b - 1, AH + h - 2))
                        step(V.tensor_scalar(attn[:, h % 2, 0:nk], prob[:, h % 2, 0, 0:nk],
                                             smx[:, 2, h % 2, 0:1], None, ALU.mult))
                        settle()
                        V.scalar_tensor_tensor(out=attn[:, h % 2, 0:nk], in0=prob[:, h % 2, 1, 0:nk],
                                               scalar=smx[:, 3, h % 2, 0:1], in1=attn[:, h % 2, 0:nk],
                                               op0=ALU.mult, op1=ALU.add).then_inc(attn_ready, 1)

                    for h in range(AH):
                        masked(h)
                        if h >= 1:
                            combined(h - 1)
                    combined(AH - 1)
                    dve.wait_ge(ostd_ready, b + 1)
                    step(V.reciprocal(ost[:, 2, b], ost[:, 1, b]))
                    settle()
                    o3 = o_sb[:, b].rearrange("p (h e) -> p h e", h=AH)
                    V.tensor_tensor(o3, o3, bcast(ost[:, 2, b], P), ALU.mult).then_inc(on_ready, 1)
                    for c in range(2):
                        key = ("oT", b, c)
                        produced(dve, key)
                        V.tensor_scalar(oT[:, 4 * c:4 * c + 4, b * P:(b + 1) * P],
                                        bank(key)[:, :].rearrange("p (k t) -> p k t", k=4), sub_w[:, 0:1],
                                        1.0 - LAMBDA_INIT, ALU.mult, ALU.mult).then_inc(read_of(key), 1)
                add_back(1)

            def best_16(values, sets, width_of, top, where, last_read=None):
                for j in range(sets):
                    step(V.max(top[:, j, 0:8], width_of(values, j)))
                settle()
                for j in range(sets):
                    step(V.max_index(where[:, j, 0:8], top[:, j, 0:8], width_of(values, j)))
                settle()
                for j in range(sets):
                    step(V.match_replace(width_of(values, j), top[:, j, 0:8], width_of(values, j), MASKED))
                settle()
                for j in range(sets):
                    step(V.max(top[:, j, 8:16], width_of(values, j)))
                settle()
                for j in range(sets):
                    ins = V.max_index(where[:, j, 8:16], top[:, j, 8:16], width_of(values, j))
                    if j == sets - 1 and last_read is not None:
                        ins.then_inc(last_read, 1)
                    else:
                        step(ins)

            def pairs_of(out_, first, second):
                for i in range(5):
                    n, o = CAND_LEN[i], CAND_OFF[i]
                    V.tensor_tensor(out_[:, :, o:o + n], first[:, :, i:i + 1].broadcast_to([P, PH, n]),
                                    second[:, :, 0:n], ALU.add)
                o = CAND_OFF[5]
                V.tensor_tensor(out_[:, :, o:o + 6].rearrange("p h (i j) -> p h i j", j=2),
                                first[:, :, 5:8].unsqueeze(3).broadcast_to([P, PH, 3, 2]),
                                second[:, :, 0:2].unsqueeze(2).broadcast_to([P, PH, 3, 2]), ALU.add)
                o = CAND_OFF[8]
                step(V.tensor_tensor(out_[:, :, o:o + 8], first[:, :, 8:16],
                                     second[:, :, 0:1].broadcast_to([P, PH, 8]), ALU.add))

            def select(layer, b):
                moved(dve, ("s", layer, b, HC // 4 - 1))
                n = layer * NB + b
                best_16(sc, HC, lambda t, j: t[:, j], topv, topi, s_used)
                dve.wait_ge(s_used, n + 1)
                step(V.tensor_copy(topf, topi))
                settle()
                halves = [t.rearrange("p (h c) k -> p h c k", c=2) for t in (topv, topf)]
                step(V.tensor_scalar(halves[1][:, :, 0], halves[1][:, :, 0], float(NK), None, ALU.mult))
                pairs_of(cs, halves[0][:, :, 0], halves[0][:, :, 1])
                settle()
                pairs_of(ci, halves[1][:, :, 0], halves[1][:, :, 1])
                best_16(cs, PH, lambda t, j: t[:, j], best, posi)
                settle()
                V.tensor_tensor(bsub[:], best[:], best[:, :, 0:1].broadcast_to([P, PH, TOPK]),
                                ALU.subtract).then_inc(gsub_ready, 1)
                step(V.tensor_copy(posf[:], posi[:]))
                for h in range(0, PH, 2):
                    settle()
                    step(V.tensor_tensor(eq[:, :, :, :], posf[:, h:h + 2].unsqueeze(3).broadcast_to([P, 2, TOPK, NC]),
                                         iota[:, :].unsqueeze(1).unsqueeze(1).broadcast_to([P, 2, TOPK, NC]),
                                         ALU.is_equal))
                    settle()
                    step(V.tensor_tensor(eq[:, :, :, :], eq[:, :, :, :],
                                         ci[:, h:h + 2].unsqueeze(2).broadcast_to([P, 2, TOPK, NC]), ALU.mult))
                    settle()
                    step(V.tensor_reduce(idxf[:, h * TOPK:(h + 2) * TOPK].rearrange("p (a k) -> p a k", a=2),
                                         eq[:, :, :, :], AX.X, ALU.add))
                settle()
                V.tensor_scalar(idx[:, b], idxf[:], float(layer * NE), None, ALU.add).then_inc(idx_ready, 1)
                dve.wait_ge(gexp_ready, n + 1)
                step(V.tensor_reduce(gsum[:, 0], bsub[:], AX.X, ALU.add))
                settle()
                step(V.reciprocal(gsum[:, 1], gsum[:, 0]))
                settle()
                step(V.tensor_tensor(gate[:, b].rearrange("p (h k) -> p h k", h=PH), bsub[:],
                                     bcast(gsum[:, 1], TOPK), ALU.mult))
                settle()

            def experts(layer, b):
                g0 = (layer * NB + b) * (PAIRS // GRP)
                with dve.Fori(0, PAIRS // GRP // 2) as i:
                    for h in range(2):
                        for k in range(GRP):
                            dve.wait_ge(u_loaded[k], i * 32 + 16 * (g0 + h + 1))
                            V.tensor_tensor_reduce(ring[:, k], ring[:, k], hn[:, b], 1.0, 0.0, ALU.mult, ALU.add,
                                                   acts[:, h, k:k + 1]).then_inc(u_free, 1)
                        dve.wait_ge(gelu_ready, i * 2 + (g0 + h + 1))
                        V.tensor_tensor(wts[:, h], gel[:, h], gate[:, b, bass.ds(i * (2 * GRP) + h * GRP, GRP)],
                                        ALU.mult).then_inc(wts_ready, 1)
                dve.wait_ge(v_free, GRP + (layer * NB + b + 1) * PAIRS)
                for half in range(2):
                    V.tensor_copy(x[:, b, half * 512:(half + 1) * 512], ysum[half][:, :]).then_inc(x_fed, 1)

            norm(0)
            ssd()
            norm(1)
            for b in range(NB):
                select(0, b)
            for b in range(NB):
                experts(0, b)
            norm(2)
            attention()
            norm(3)
            for b in range(NB):
                select(1, b)
            for b in range(NB):
                experts(1, b)


def kernel(**inputs):
    import numpy as np
    import concourse.bacc as bacc
    from concourse.bass_utils import run_bass_kernel_spmd

    a = {name: np.asarray(v) for name, v in inputs.items()}
    tiles = CONV_TILES
    arrays = {
        "x_in": a["x"],
        "mix_norm_w": a["mix_norm_w"],
        "ffn_norm_w": a["ffn_norm_w"],
        "in_w": a["ssd_in_w"],
        "conv_w": a["ssd_conv_w"][0].T.reshape(tiles, P, CONV).transpose(1, 0, 2),
        "conv_b": a["ssd_conv_b"][0].reshape(tiles, P).T,
        "dt_bias": a["ssd_dt_bias"],
        "a_log": a["ssd_a_log"],
        "d_skip": a["ssd_d"],
        "ssd_norm_w": a["ssd_norm_w"][0].reshape(XS_TILES, P).T,
        "ssd_out_w": a["ssd_out_w"],
        "qkv_w": a["da_qkv_w"],
        "q_norm_w": a["da_q_norm_w"],
        "k_norm_w": a["da_k_norm_w"],
        "lam_q1": a["da_lam_q1"],
        "lam_k1": a["da_lam_k1"],
        "lam_q2": a["da_lam_q2"],
        "lam_k2": a["da_lam_k2"],
        "subln_w": a["da_subln_w"],
        "da_out_w": a["da_out_w"],
        "query_w": a["peer_query_w"],
        "keys_t": a["peer_sub_keys"].reshape(DEPTH, HC, NK, -1).transpose(0, 1, 3, 2),
        "peer_u": a["peer_u"],
        "peer_v": a["peer_v"],
    }
    arrays = {name: np.ascontiguousarray(v) for name, v in arrays.items()}
    nc = bacc.Bacc("TRN2", target_bir_lowering=False, num_devices=1)
    args = [nc.dram_tensor(f"in_{name}", v.shape, mybir.dt.from_np(v.dtype), kind="ExternalInput").ap()
            for name, v in arrays.items()]
    args.append(nc.dram_tensor("out_y", a["x"].shape, mybir.dt.from_np(a["x"].dtype),
                               kind="ExternalOutput").ap())
    build(nc, *args)
    r = run_bass_kernel_spmd(nc, [{f"in_{name}": v for name, v in arrays.items()}], core_ids=[0])
    return r.results[0]["out_y"]
```

```python
import math
from contextlib import ExitStack

import concourse.bass as bass
from concourse import mybir

F32 = mybir.dt.float32
U32 = mybir.dt.uint32
ALU = mybir.AluOpType
ACT = mybir.ActivationFunctionType
AX = mybir.AxisListType

P = 128
T = 256
NB = T // P
D = 1024
KD = D // P
DEPTH = 2
EPS = 1e-6
DI = 2048
NH = 32
HP = 64
NG = 8
HG = NH // NG
NS = 128
CONV = 4
GW = HG * HP
CONV_TILES = (DI + 2 * NG * NS) // P
XS_TILES = DI // P
AH = 8
AD = 64
LAMBDA_INIT = 0.8 - 0.6 * math.exp(-0.3 * 1)
MASKED = -1e30
PH = 8
NK = 128
TOPK = 16
NE = NK * NK
HC = 2 * PH
PAIRS = PH * TOPK
GRP = 8
DIAGS = 4
CAND_LEN = [TOPK // (i + 1) for i in range(TOPK)]
CAND_OFF = [sum(CAND_LEN[:i]) for i in range(TOPK)]
NC = sum(CAND_LEN)
ATANH = [1.0 / (2 * k + 1) for k in range(1, 10)]

WCOLS = 512
WSLOTS = 3
MM_BANKS = 6


Z_ORDER = [("z", b, n) for n in range(4) for b in range(NB)]
HEADS = [(b, h) for b in range(NB) for h in range(AH)]
NORM_ORDER = [(0, 0), (0, 1), (1, 0), (1, 1), (2, 0), (3, 0), (2, 1), (3, 1)]
CHUNKS = HC // 4
CHUNK_GROUPS = 2 * TOPK // GRP
GROUPS = PAIRS // GRP


def psum_plan():
    order = []

    def norm(i, blocks=range(NB)):
        order.extend(("nT", i, b, c) for b in blocks for c in range(2))

    norm(0)
    for j in range(CONV_TILES // 2):
        order.append(("xbc", j))
        if j == 0:
            order.append(("dt",))
        if 2 <= j < XS_TILES // 2 + 2:
            order.append(("xT", j - 2))
    order.append(("acs",))
    order.extend(("bT", c) for c in range(2))
    for b in range(NB):
        order.extend(("cb", b, c) for c in range(2))
        order.extend(("bc", b, g) for g in range(2))
        for g in range(NG):
            if g + 2 < NG:
                order.append(("bc", b, g + 2))
            if g % 2 == 1:
                order.append(("y", b, g // 2))
                order.append(("st" if b == 0 else "yo", g // 2))
                order.append(Z_ORDER[b * NG // 2 + g // 2])
    order.extend(("ynT", b, c) for b in range(NB) for c in range(4))
    order.extend(("out", 0, n, b) for n in range(2) for b in range(NB))
    norm(1)
    for c in range(CHUNKS + 1):
        if c < CHUNKS:
            order.extend([("q", 0, 2 * c), ("q", 0, 2 * c + 1)])
        if c:
            order.extend(("s", 0, b, c - 1) for b in range(NB))
    for b in range(NB):
        norm(2, [b])
        order.extend(("qkv", n, b) for n in range(6))
        order.extend(("qkT", b, c) for c in range(4))
        for h in range(0, AH + 2, 2):
            if h:
                order.extend([("aT", b, h - 2), ("O", b, h - 2), ("aT", b, h - 1), ("O", b, h - 1)])
            if h < AH:
                order.extend(("S", b, hh, m) for hh in (h, h + 1) for m in range(2))
        order.extend(("oT", b, c) for c in range(2))
        order.extend(("out", 1, n, b) for n in range(2))
        norm(3, [b])
        for c in range(CHUNKS + 1):
            if c < CHUNKS:
                order.append(("q", 1, b, c))
            if c:
                order.append(("s", 1, b, c - 1))
    return {key: (n % MM_BANKS, n // MM_BANKS, n) for n, key in enumerate(order)}


def weight_plan():
    tiles = [("in", 0, 0, DI + WCOLS * j) for j in range(8)]
    tiles += [("in", 0, 0, WCOLS * j) for j in range(4)]
    tiles += [("out0", 0, KD * kh, WCOLS * n) for n in range(2) for kh in range(2)]
    tiles += [("query", 0, 0, WCOLS * j) for j in range(4)]
    for b in range(NB):
        tiles += [("qkv", 0, 0, WCOLS * j, b) for j in range(6)]
        tiles += [("out1", 0, 0, WCOLS * n, b) for n in range(2)]
        tiles += [("query", 1, 0, WCOLS * j, b) for j in range(4)]
    return tiles


def build(nc, x_in, mix_norm_w, ffn_norm_w, in_w, conv_w, conv_b, dt_bias, a_log, d_skip, ssd_norm_w,
          ssd_out_w, qkv_w, q_norm_w, k_norm_w, lam_q1, lam_k1, lam_q2, lam_k2, subln_w, da_out_w,
          query_w, keys_t, peer_u, peer_v, out):
    PLAN = psum_plan()
    WTILES = weight_plan()
    WAT, held = {}, [[] for _ in range(WSLOTS)]
    second = WTILES.index(("qkv", 0, 0, 0, 0))
    for n, key in enumerate(WTILES):
        slot = n % WSLOTS if n < second else (n - second) % (WSLOTS - 1)
        WAT[key] = (slot, len(held[slot]) + 1, held[slot][-1] if held[slot] else None)
        held[slot].append(key)
    in_cols = in_w.shape[2]

    with ExitStack() as ctx:
        def sb(name, shape, dt=F32):
            return ctx.enter_context(nc.sbuf_tensor(name, shape, dt))

        def sem(name):
            return ctx.enter_context(nc.semaphore(name))

        ident = sb("ident", [P, P])
        tri = sb("tri", [P, P])
        ones = sb("ones", [P, P])
        mask = sb("mask", [P, NB, T])
        iota = sb("iota", [P, NC])
        eps = sb("eps", [P, 1])
        norm_w = sb("norm_w", [P, 2, D])
        w_dt = sb("w_dt", [P, KD, NH])
        cw = sb("cw", [P, CONV_TILES, CONV])
        cb = sb("cb", [P, CONV_TILES])
        dtb = sb("dtb", [P, NH])
        alog = sb("alog", [P, NH])
        dsk = sb("dsk", [P, NH])
        snw = sb("snw", [P, XS_TILES])
        qkn = sb("qkn", [P, 2])
        lams = sb("lams", [P, 4, AD])
        sub_w = sb("sub_w", [P, 1])
        x = sb("x", [P, NB, D])
        hn = sb("hn", [P, NB, D])
        hnT = sb("hnT", [P, KD, T])
        wring = sb("wring", [P, WSLOTS, KD, WCOLS])
        keysT = sb("keysT", [P, HC, NK])
        stat = sb("stat", [P, 8, 4])
        ring = sb("ring", [P, 2 * GRP, D])
        ring_flat = ring[:, :, :].rearrange("p a b -> p (a b)")
        tmp = sb("tmp", [P, 8192])

        def view(base, off, *dims):
            n = math.prod(dims)
            v = base[:, off:off + n]
            if len(dims) == 2:
                return v.rearrange("p (a b) -> p a b", a=dims[0])
            if len(dims) == 3:
                return v.rearrange("p (a b c) -> p a b c", a=dims[0], b=dims[1])
            return v

        xh = view(ring_flat, 0, NB, DI)
        bcT = view(ring_flat, 4096, 2 * NG, T)
        zs = view(ring_flat, 8192, NB, DI)
        ynT = view(ring_flat, 12288, XS_TILES, T)
        tmp_ap = tmp[:, :]
        xd = view(tmp_ap, 0, NH, HP)
        state = view(tmp_ap, 4096, DI)
        cv = view(tmp_ap, 6144, 4, T)
        xsT = view(tmp_ap, 7168, 4, T)
        seg = view(tmp_ap, 6144, 4, HG * P)
        xde = view(ring_flat, 12288, NH, HP)
        b_tok = view(ring_flat, 14336, NG, NS)
        kT = view(tmp_ap, 0, AH, T)
        vv = view(tmp_ap, 2048, NB, D)
        aqT = view(tmp_ap, 4096, AH, P)
        att_ap = wring[:, WSLOTS - 1].rearrange("p a b -> p (a b)")
        qk = view(att_ap, 0, 2 * D)
        o_sb = view(att_ap, 0, D)
        oT = view(att_ap, 1024, AH, P)
        prob = view(att_ap, 2048, 2, 2, T)
        sq = view(att_ap, 2048, 2, WCOLS)
        attn = view(att_ap, 3072, 2, T)
        attnT = view(att_ap, 3584, 2, T)
        qT = view(tmp_ap, 0, 8, T)
        sc = view(tmp_ap, 2048, NB * HC, NK)
        qbT = view(tmp_ap, 5120, 8, P)
        sc2 = view(tmp_ap, 4096, 8, NK)
        eq = view(tmp_ap, 6144, 2, TOPK, NC)
        small = sb("small", [P, 1824])
        small_ap = small[:, :]
        junk = sb("junk", [P, GW])
        topv = view(small_ap, 0, 4, TOPK)
        topf = view(small_ap, 512, 4, TOPK)
        topi = topf.bitcast(U32)
        cs = view(small_ap, 1024, 2, NC)
        ci = view(small_ap, 1424, 2, NC)
        best = sb("best", [P, 2, TOPK])
        posf = sb("posf", [P, 2, TOPK])
        posi = posf[:, :, :].bitcast(U32)
        gsum = sb("gsum", [P, 2, 2])
        gate = sb("gate", [P, NB, PAIRS])
        idx = sb("idx", [P, NB, PAIRS], U32)
        idxf = posf[:, :, :].rearrange("p h k -> p (h k)")
        idx_now = sb("idx_now", [P, 2, GRP], U32)
        acts = sb("acts", [P, 2, GRP])
        gel = sb("gel", [P, 2, GRP])
        wts = sb("wts", [P, 2, GRP])
        diag = sb("diag", [P, DIAGS, P])
        dts = sb("dts", [P, NB, NH])
        adt = sb("adt", [P, NB, NH])
        acs = sb("acs", [P, 2 * NB, NH])
        eacs = sb("eacs", [P, NH])
        toend = sb("toend", [P, NH])
        spt = view(tmp_ap, 4096, 6, NB * NH)
        expa = sb("expa", [P, NH])
        cbm = view(small_ap, 0, NG, P)
        yoff = view(small_ap, 1024, WCOLS)
        gst = sb("gst", [P, NB, 3, NG])
        qst = sb("qst", [P, 3, NB, 2 * 2 * AH])
        lam = sb("lam", [P, 8])
        smx = sb("smx", [P, 4, 2, 2])
        ost = sb("ost", [P, 3, NB, AH])

        banks = [ctx.enter_context(nc.psum_tensor(f"mm{i}", [P, 512], F32)) for i in range(MM_BANKS)]
        ysum = [ctx.enter_context(nc.psum_tensor(f"ysum{i}", [P, 512], F32)) for i in range(2)]

        x_loaded = sem("x_loaded")
        wdt_loaded = sem("wdt_loaded")
        conv_loaded = sem("conv_loaded")
        dt_loaded = sem("dt_loaded")
        ssd_loaded = sem("ssd_loaded")
        attn_loaded = sem("attn_loaded")
        normw_loaded = [sem(f"normw{i}_loaded") for i in range(2 * DEPTH)]
        keys_loaded = sem("keys_loaded")
        w_loaded = [sem(f"w{i}_loaded") for i in range(WSLOTS)]
        consts = sem("consts_ready")
        mm_done = sem("mm_done")
        bank_read = [sem(f"bank{i}_read") for i in range(MM_BANKS)]
        dve_seq = sem("dve_seq")
        act_seq = sem("act_seq")
        std_ready = sem("std_ready")
        hn_ready = sem("hn_ready")
        x_fed = sem("x_fed")
        dt_abs_ready = sem("dt_abs_ready")
        dt_exp_ready = sem("dt_exp_ready")
        adt_ready = sem("adt_ready")
        first_tap_ready = sem("first_tap_ready")
        silu_ready = sem("silu_ready")
        toend_ready = sem("toend_ready")
        eacs_ready = sem("eacs_ready")
        xd_ready = sem("xd_ready")
        xde_ready = sem("xde_ready")
        decay_ready = sem("decay_ready")
        m_ready = sem("m_ready")
        zs_ready = sem("zs_ready")
        gated_ready = sem("gated_ready")
        gstd_ready = sem("gstd_ready")
        yn_ready = sem("yn_ready")
        sq_ready = sem("sq_ready")
        qss_ready = sem("qss_ready")
        qstd_ready = sem("qstd_ready")
        qn_ready = sem("qn_ready")
        lamdot_ready = sem("lamdot_ready")
        lamexp_ready = sem("lamexp_ready")
        max_ready = sem("max_ready")
        exp_ready = sem("exp_ready")
        attn_ready = sem("attn_ready")
        ostd_ready = sem("ostd_ready")
        on_ready = sem("on_ready")
        gsub_ready = sem("gsub_ready")
        gexp_ready = sem("gexp_ready")
        idx_ready = sem("idx_ready")
        idx_now_ready = sem("idx_now_ready")
        u_loaded = [sem(f"u{i}_loaded") for i in range(GRP)]
        v_loaded = [sem(f"v{i}_loaded") for i in range(GRP)]
        u_free = sem("u_free")
        v_free = sem("v_free")
        gelu_ready = sem("gelu_ready")
        wts_ready = sem("wts_ready")
        diag_ready = sem("diag_ready")
        stored = sem("stored")

        def bank(key):
            return banks[PLAN[key][0]]

        def produced(eng, key):
            eng.wait_ge(mm_done, PLAN[key][2] + 1)

        def read_of(key):
            return bank_read[PLAN[key][0]]

        def moved(eng, key):
            eng.wait_ge(read_of(key), PLAN[key][1] + 1)

        def w_tile(*key):
            return wring[:, WAT[key][0]]

        def w_landed(eng, *key):
            slot, nth, _ = WAT[key]
            eng.wait_ge(w_loaded[slot], 16 * nth)

        def last_use(key):
            name, layer, _, c0 = key[:4]
            if name == "in":
                return ("xbc", 2 * ((c0 - DI) // WCOLS) + 1) if c0 >= DI else ("z", NB - 1, c0 // WCOLS)
            if name == "query":
                return ("q", 0, 2 * (c0 // WCOLS) + 1) if layer == 0 else ("q", 1, key[4], c0 // WCOLS)
            if name == "qkv":
                return ("qkv", c0 // WCOLS, key[4])
            return ("out", 0, c0 // WCOLS, NB - 1) if name == "out0" else ("out", 1, c0 // WCOLS, key[4])

        def normed(i, b):
            return NORM_ORDER.index((i, b)) + 1

        def chosen(layer, b, c):
            return (layer * NB + b) * CHUNKS + c + 1

        def bcast(ap, n):
            return ap.unsqueeze(2).broadcast_to([ap.shape[0], ap.shape[1], n])

        block = ctx.enter_context(nc.Block())

        @block.sync
        def _(sp):
            sp.dma_start(x[:], x_in.rearrange("a (b p) d -> p (a b) d", p=P)).then_inc(x_loaded, 16)
            sp.dma_start(norm_w[:, 0], mix_norm_w[0:1, :].broadcast_to([P, D])).then_inc(normw_loaded[0], 16)
            sp.dma_start(w_dt[:], in_w[0].rearrange("(k p) n -> p k n", p=P)[:, :, in_cols - NH:in_cols]) \
                .then_inc(wdt_loaded, 16)
            dram = {
                "in": in_w, "out0": ssd_out_w, "qkv": qkv_w, "out1": da_out_w, "query": query_w,
            }

            def weight(n):
                name, layer, k0, c0 = WTILES[n][:4]
                slot, _, before = WAT[WTILES[n]]
                if before:
                    produced(sp, last_use(before))
                src = dram[name][layer].rearrange("(k p) n -> p k n", p=P)[:, k0:k0 + KD, c0:c0 + WCOLS]
                sp.dma_start(wring[:, slot], src).then_inc(w_loaded[slot], 16)

            for n in range(WSLOTS):
                weight(n)
            sp.dma_start(norm_w[:, 1], ffn_norm_w[0:1, :].broadcast_to([P, D])).then_inc(normw_loaded[1], 16)
            sp.dma_start(keysT[:], keys_t[0].rearrange("h d n -> d h n")).then_inc(keys_loaded, 16)
            for n in range(WSLOTS, second):
                weight(n)
            sp.wait_ge(hn_ready, 2 * NB)
            sp.dma_start(norm_w[:, 0], mix_norm_w[1:2, :].broadcast_to([P, D])).then_inc(normw_loaded[2], 16)
            sp.dma_start(norm_w[:, 1], ffn_norm_w[1:2, :].broadcast_to([P, D])).then_inc(normw_loaded[3], 16)
            produced(sp, ("s", 0, NB - 1, HC // 4 - 1))
            sp.dma_start(keysT[:], keys_t[1].rearrange("h d n -> d h n")).then_inc(keys_loaded, 16)
            for n in range(second, len(WTILES)):
                weight(n)
            for b in range(NB):
                sp.wait_ge(x_fed, 2 * (NB + b) + 2)
                sp.dma_start(out[0, b * P:(b + 1) * P, :], x[:, b]).then_inc(stored, 16)
            sp.wait_ge(stored, 16 * NB)

        @block.gpsimd
        def _(pool):
            pool.memset(ones[:], 1.0).then_inc(consts, 1)
            pool.memset(eps[:], EPS).then_inc(consts, 1)
            pool.memset(mask[:], 0.0).then_inc(consts, 1)
            pool.memset(ident[:], 0.0).then_inc(consts, 1)
            pool.iota(iota[:], pattern=[[1, NC]], base=0, channel_multiplier=0,
                      allow_small_or_imprecise_dtypes=True).then_inc(consts, 1)
            pool.wait_ge(consts, 5)
            pool.affine_select(out=ident[:], in_=ident[:], compare_op=ALU.not_equal, fill=1.0, base=0,
                               pattern=[[-1, P]], channel_multiplier=1).then_inc(consts, 1)
            pool.affine_select(out=tri[:], in_=ones[:], compare_op=ALU.is_ge, fill=0.0, base=0,
                               pattern=[[1, P]], channel_multiplier=-1).then_inc(consts, 1)
            for b in range(NB):
                pool.memset(mask[0:P // 2, b, b * P + P // 2:(b + 1) * P], MASKED).then_inc(consts, 1)
            pool.sem_inc(u_free, GRP)
            pool.sem_inc(v_free, GRP)

            u_rows, v_rows = (t.rearrange("l e d -> (l e) d") for t in (peer_u, peer_v))

            def gather(layer, b):
                g0 = (layer * NB + b) * (PAIRS // GRP)
                with pool.Fori(0, GROUPS // 2) as i:
                    pool.wait_ge(idx_ready, i + ((layer * NB + b) * GROUPS // 2 + 1))
                    for h in range(2):
                        pool.tensor_copy(idx_now[:, h], idx[:, b, bass.ds(i * (2 * GRP) + h * GRP, GRP)]) \
                            .then_inc(idx_now_ready, 1)
                        pool.wait_ge(idx_now_ready, i * 2 + (g0 + h + 1))
                        for k in range(GRP):
                            pool.wait_ge(u_free, i * (2 * GRP) + ((g0 + h) * GRP + k + 1))
                            pool.nop(nofuse=True)
                            pool.indirect_dma_start(
                                ring[:, k, :], None, u_rows,
                                bass.IndirectOffsetOnAxis(idx_now[:, h, k:k + 1], 0)).then_inc(u_loaded[k], 16)
                        for k in range(GRP):
                            pool.wait_ge(v_free, i * (2 * GRP) + ((g0 + h) * GRP + k + 1))
                            pool.nop(nofuse=True)
                            pool.indirect_dma_start(
                                ring[:, GRP + k, :], None, v_rows,
                                bass.IndirectOffsetOnAxis(idx_now[:, h, k:k + 1], 0)).then_inc(v_loaded[k], 16)

            for layer in range(DEPTH):
                for b in range(NB):
                    gather(layer, b)

        @block.scalar
        def _(act):
            seq = [0]

            def step(ins):
                seq[0] += 1
                ins.then_inc(act_seq, 1)

            def settle():
                act.wait_ge(act_seq, seq[0])

            act.dma_start(dtb[:], dt_bias.broadcast_to([P, NH])).then_inc(dt_loaded, 16)
            act.dma_start(alog[:], a_log.broadcast_to([P, NH])).then_inc(dt_loaded, 16)
            act.dma_start(cw[:], conv_w).then_inc(conv_loaded, 16)
            act.dma_start(cb[:], conv_b).then_inc(conv_loaded, 16)
            act.dma_start(dsk[:], d_skip.broadcast_to([P, NH])).then_inc(ssd_loaded, 16)
            act.dma_start(snw[:], ssd_norm_w).then_inc(ssd_loaded, 16)
            for half in range(2):
                rows = slice(half * AD, (half + 1) * AD)
                act.dma_start(qkn[rows, 0:1], q_norm_w.rearrange("a d -> d a")).then_inc(attn_loaded, 16)
                act.dma_start(qkn[rows, 1:2], k_norm_w.rearrange("a d -> d a")).then_inc(attn_loaded, 16)
            for j, v in enumerate((lam_q1, lam_k1, lam_q2, lam_k2)):
                act.dma_start(lams[:, j], v.broadcast_to([P, AD])).then_inc(attn_loaded, 16)
            act.dma_start(sub_w[:], subln_w.rearrange("a d -> d a")).then_inc(attn_loaded, 16)

            def norm(i, blocks=range(NB)):
                if i == 0:
                    act.wait_ge(x_loaded, 16)
                    act.wait_ge(consts, 5)
                for b in blocks:
                    if i % 2 == 1:
                        moved(act, ("out", i // 2, 1, b))
                    elif i:
                        act.wait_ge(x_fed, 2 * b + 2)
                    if i:
                        produced(act, ("nT", i - 1, b, 1))
                    step(act.activation(hn[:, b], x[:, b], ACT.Square, accum_out=stat[:, 2 * i + b, 0:1]))
                    settle()
                    act.activation(stat[:, 2 * i + b, 1:2], stat[:, 2 * i + b, 0:1], ACT.Sqrt,
                                   scale=1.0 / D, bias=eps[:, 0:1]).then_inc(std_ready, 1)
                for b in blocks:
                    for c in range(2):
                        key = ("nT", i, b, c)
                        produced(act, key)
                        act.activation(hnT[:, 4 * c:4 * c + 4, b * P:(b + 1) * P],
                                       bank(key)[:, :].rearrange("p (c t) -> p c t", c=4),
                                       ACT.Copy).then_inc(read_of(key), 1)

            def ssd():
                act.wait_ge(dt_loaded, 32)
                step(act.activation(expa[:], alog[:], ACT.Exp))
                act.wait_ge(dt_abs_ready, 1)
                act.activation(spt[:, 2], spt[:, 1], ACT.Exp, scale=-1.0).then_inc(dt_exp_ready, 1)
                act.wait_ge(conv_loaded, 32)

                def first_tap(j):
                    key = ("xbc", j)
                    produced(act, key)
                    for s in range(2):
                        c = 2 * j + s
                        if j >= 2:
                            act.wait_ge(silu_ready, c - 3)
                        act.activation(cv[:, c % 4], bank(key)[:, s * T:(s + 1) * T], ACT.Identity,
                                       scale=cw[:, c, CONV - 1:CONV], bias=cb[:, c:c + 1]) \
                            .then_inc(first_tap_ready, 1)

                def silu(j):
                    moved(act, ("xbc", j))
                    for s in range(2):
                        c = 2 * j + s
                        if c < XS_TILES:
                            if j >= 2:
                                produced(act, ("xT", j - 2))
                            dst = xsT[:, c % 4]
                        else:
                            dst = bcT[:, c - XS_TILES]
                        act.activation(dst, cv[:, c % 4], ACT.Silu).then_inc(silu_ready, 1)

                def x_tokens(j):
                    key = ("xT", j)
                    produced(act, key)
                    act.activation(xh[:, :, 2 * j * P:(2 * j + 2) * P],
                                   bank(key)[:, :].rearrange("p (b c) -> p b c", b=NB),
                                   ACT.Copy).then_inc(read_of(key), 1)

                pairs = CONV_TILES // 2
                for j in range(pairs + 2):
                    if j < pairs:
                        first_tap(j)
                    if 1 <= j <= pairs:
                        silu(j - 1)
                    if 2 <= j < XS_TILES // 2 + 2:
                        x_tokens(j - 2)

                def z_out(n):
                    key = Z_ORDER[n]
                    _, b, c = key
                    produced(act, key)
                    act.activation(zs[:, b, c * WCOLS:(c + 1) * WCOLS], bank(key)[:, :],
                                   ACT.Copy).then_inc(read_of(key), 1)

                for c in range(2):
                    key = ("bT", c)
                    produced(act, key)
                    act.activation(b_tok[:, 4 * c:4 * c + 4],
                                   bank(key)[:, :].rearrange("p (g n) -> p g n", g=4),
                                   ACT.Copy).then_inc(read_of(key), 1)
                act.wait_ge(toend_ready, 1)
                act.activation(toend[:], toend[:], ACT.Exp).then_inc(eacs_ready, 1)
                act.activation(eacs[:], acs[:, 1], ACT.Exp).then_inc(eacs_ready, 1)
                for b in range(NB):
                    for g in range(NG):
                        moved(act, ("bc", b, g))
                        act.activation(seg[:, g % 4], seg[:, g % 4], ACT.Exp).then_inc(decay_ready, 1)
                        if g % 2 == 1:
                            n = b * NG // 2 + g // 2
                            if 1 <= n <= NG // 2:
                                state_out(n - 1)
                            if n:
                                z_out(n - 1)
                z_out(len(Z_ORDER) - 1)
                for b in range(NB):
                    for q in range(4):
                        zq = zs[:, b, q * WCOLS:(q + 1) * WCOLS]
                        act.wait_ge(read_of(Z_ORDER[-1]), PLAN[Z_ORDER[-1]][1] + 1)
                        act.activation(zq, zq, ACT.Silu).then_inc(zs_ready, 1)
                for b in range(NB):
                    for q in range(4):
                        act.wait_ge(gated_ready, 4 * b + q + 1)
                        for g in (2 * q, 2 * q + 1):
                            settle()
                            step(act.activation(junk[:, 0:GW], xh[:, b, g * GW:(g + 1) * GW], ACT.Square,
                                                accum_out=gst[:, b, 0, g:g + 1]))
                settle()
                for b in range(NB):
                    act.activation(gst[:, b, 1], gst[:, b, 0], ACT.Sqrt, scale=1.0 / GW,
                                   bias=eps[:, 0:1]).then_inc(gstd_ready, 1)

            def state_out(q):
                key = ("st", q)
                produced(act, key)
                act.activation(state[:, q * WCOLS:(q + 1) * WCOLS], bank(key)[:, :],
                               ACT.Copy).then_inc(read_of(key), 1)

            def lambdas():
                act.wait_ge(lamdot_ready, 2)
                act.activation(lam[:, 2:4], lam[:, 0:2], ACT.Exp).then_inc(lamexp_ready, 1)

            def qkv(b, n):
                key = ("qkv", n, b)
                produced(act, key)
                if n < 4:
                    m = 4 * b + n
                    if m >= 2:
                        act.wait_ge(qss_ready, m - 1)
                    act.activation(sq[:, m % 2], bank(key)[:, :], ACT.Square).then_inc(sq_ready, 1)
                    act.activation(qk[:, n * WCOLS:(n + 1) * WCOLS], bank(key)[:, :],
                                   ACT.Copy).then_inc(read_of(key), 1)
                else:
                    act.activation(vv[:, b, (n - 4) * WCOLS:(n - 3) * WCOLS], bank(key)[:, :],
                                   ACT.Copy).then_inc(read_of(key), 1)

            def qk_deviations(b):
                act.wait_ge(qss_ready, 4 * (b + 1))
                act.activation(qst[:, 1, b], qst[:, 0, b], ACT.Sqrt, scale=1.0 / AD,
                               bias=eps[:, 0:1]).then_inc(qstd_ready, 1)

            def exponentials(b, h):
                n = b * AH + h
                nk = (b + 1) * P
                act.wait_ge(max_ready, n + 1)
                for m in range(2):
                    act.activation(prob[:, n % 2, m, 0:nk], prob[:, n % 2, m, 0:nk], ACT.Exp,
                                   bias=smx[:, 0, n % 2, m:m + 1],
                                   accum_out=smx[:, 1, n % 2, m:m + 1]).then_inc(exp_ready, 1)

            def weighted(b, h):
                n = b * AH + h
                nk = (b + 1) * P
                key = ("aT", b, h)
                produced(act, key)
                if n >= 2:
                    produced(act, ("O", *HEADS[n - 2]))
                act.activation(attnT[:, n % 2, 0:nk], bank(key)[:, 0:nk], ACT.Copy) \
                    .then_inc(read_of(key), 1)
                key = ("O", b, h)
                produced(act, key)
                settle()
                step(act.activation(junk[:, 0:P], bank(key)[:, 0:P], ACT.Square,
                                    accum_out=ost[:, 0, b, h:h + 1]))
                act.activation(o_sb[:, h * P:(h + 1) * P], bank(key)[:, 0:P], ACT.Copy) \
                    .then_inc(read_of(key), 1)

            def o_deviations(b):
                settle()
                act.activation(ost[:, 1, b], ost[:, 0, b], ACT.Sqrt, scale=1.0 / P,
                               bias=eps[:, 0:1]).then_inc(ostd_ready, 1)

            def select():
                for c in range(CHUNKS + 1):
                    if c < CHUNKS:
                        for j in (2 * c, 2 * c + 1):
                            key = ("q", 0, j)
                            produced(act, key)
                            act.activation(qT[:, 2 * j % 8:2 * j % 8 + 2],
                                           bank(key)[:, :].rearrange("p (a t) -> p a t", a=2),
                                           ACT.Copy).then_inc(read_of(key), 1)
                    if c:
                        for b in range(NB):
                            key = ("s", 0, b, c - 1)
                            produced(act, key)
                            act.activation(sc[:, HC * b + 4 * (c - 1):HC * b + 4 * c],
                                           bank(key)[:, :].rearrange("p (a t) -> p a t", a=4),
                                           ACT.Copy).then_inc(read_of(key), 1)

            def queries(b, c):
                key = ("q", 1, b, c)
                produced(act, key)
                act.activation(qbT[:, 4 * (c % 2):4 * (c % 2) + 4],
                               bank(key)[:, :].rearrange("p (a t) -> p a t", a=4),
                               ACT.Copy).then_inc(read_of(key), 1)

            def scores(b, c):
                key = ("s", 1, b, c)
                produced(act, key)
                if c >= 2:
                    act.wait_ge(gsub_ready, chosen(1, b, c - 2))
                act.activation(sc2[:, 4 * (c % 2):4 * (c % 2) + 4],
                               bank(key)[:, :].rearrange("p (a t) -> p a t", a=4),
                               ACT.Copy).then_inc(read_of(key), 1)

            def gates(layer, b, c):
                act.wait_ge(gsub_ready, chosen(layer, b, c))
                part = gate[:, b, 2 * TOPK * c:2 * TOPK * (c + 1)]
                act.activation(part, part, ACT.Exp).then_inc(gexp_ready, 1)

            def gelu(layer, b, i, h):
                g0 = (layer * NB + b) * GROUPS
                act.wait_ge(u_free, i * (2 * GRP) + (g0 + h + 2) * GRP)
                act.activation(gel[:, h], acts[:, h], ACT.Gelu).then_inc(gelu_ready, 1)

            def diagonals(layer, b, i, h):
                g0 = (layer * NB + b) * GROUPS
                act.wait_ge(wts_ready, i * 2 + (g0 + h + 1))
                for k in range(GRP):
                    act.wait_ge(v_free, i * (2 * GRP) + ((g0 + h + 1) * GRP - DIAGS + k + 1))
                    act.activation(diag[:, k % DIAGS], ident[:], ACT.Copy, scale=wts[:, h, k:k + 1]) \
                        .then_inc(diag_ready, 1)

            def group(layer, b, i, h):
                gelu(layer, b, i, h)
                diagonals(layer, b, i, h)

            def groups(layer, b, first):
                with act.Fori(first, GROUPS // 2) as i:
                    for h in range(2):
                        group(layer, b, i, h)

            def front(b, part):
                if part == 0:
                    norm(2, [b])
                if part < 4:
                    qkv(b, part)
                elif part == 4:
                    qkv(b, 4)
                    qk_deviations(b)
                    qkv(b, 5)
                elif 6 <= part <= 10:
                    for h in (2 * (part - 7), 2 * (part - 7) + 1):
                        if part > 6:
                            weighted(b, h)
                    for h in (2 * (part - 6), 2 * (part - 6) + 1):
                        if part < 10:
                            exponentials(b, h)
                    if part == 10:
                        o_deviations(b)
                elif part == 12:
                    norm(3, [b])
                if 12 <= part < 16:
                    queries(b, part - 12)
                if 13 <= part:
                    scores(b, part - 13)

            norm(0)
            ssd()
            norm(1)
            select()
            for g in range(CHUNKS):
                gates(0, 0, g)
                group(0, 0, g // 2, g % 2)
            for g in range(CHUNKS):
                group(0, 0, (CHUNKS + g) // 2, g % 2)
                gates(0, 1, g)
            groups(0, 0, CHUNKS)
            lambdas()
            for layer, b, other in ((0, 1, 0), (1, 0, 1)):
                for g in range(GROUPS):
                    gelu(layer, b, g // 2, g % 2)
                    front(other, g)
                    diagonals(layer, b, g // 2, g % 2)
                    if layer and g in (2, 3):
                        gates(layer, b, g)
                front(other, GROUPS)
                gates(1, other, 0)
                gates(1, other, 1)
            for g in range(4):
                group(1, 1, g // 2, g % 2)
                if g >= 2:
                    gates(1, 1, g)
            groups(1, 1, 2)

        @block.tensor
        def _(pe):
            def take(key):
                bk, nth, _ = PLAN[key]
                if nth:
                    pe.wait_ge(bank_read[bk], nth)
                return banks[bk]

            def mm(out_, lhsT, rhs, start=True, stop=True):
                return nc.tensor.matmul(out_, lhsT, rhs, start=start, stop=stop)

            def norm(i, blocks=range(NB)):
                for b in blocks:
                    for c in range(2):
                        bk = take(("nT", i, b, c))
                        pe.wait_ge(hn_ready, normed(i, b))
                        if i == 0:
                            pe.wait_ge(consts, 6)
                        for k in range(4):
                            last = nc.tensor.transpose(bk[:, k * P:(k + 1) * P],
                                                       hn[:, b, (4 * c + k) * P:(4 * c + k + 1) * P], ident[:])
                        last.then_inc(mm_done, 1)
                for b in blocks:
                    for c in range(2):
                        moved(pe, ("nT", i, b, c))

            def project(out_, wcols, tok):
                for k in range(KD):
                    last = mm(out_, wcols(k), tok(k), k == 0, k == KD - 1)
                return last

            def ssd():
                def x_tokens(j):
                    bk = take(("xT", j))
                    pe.wait_ge(silu_ready, 2 * j + 2)
                    for s in range(2):
                        for b in range(NB):
                            last = nc.tensor.transpose(bk[:, (2 * b + s) * P:(2 * b + s + 1) * P],
                                                       xsT[:, (2 * j + s) % 4, b * P:(b + 1) * P], ident[:])
                    last.then_inc(mm_done, 1)

                for j in range(CONV_TILES // 2):
                    key = ("in", 0, 0, DI + WCOLS * (j // 2))
                    w_landed(pe, *key)
                    w = w_tile(*key)
                    bk = take(("xbc", j))
                    for s in range(2):
                        c0 = (2 * (j % 2) + s) * P
                        last = project(bk[:, s * T:(s + 1) * T], lambda k: w[:, k, c0:c0 + P],
                                       lambda k: hnT[:, k])
                    last.then_inc(mm_done, 1)
                    if j == 0:
                        pe.wait_ge(wdt_loaded, 16)
                        bk = take(("dt",))
                        for b in range(NB):
                            last = project(bk[:, b * NH:(b + 1) * NH],
                                           lambda k: hnT[:, k, b * P:(b + 1) * P], lambda k: w_dt[:, k])
                        last.then_inc(mm_done, 1)
                    if 2 <= j < XS_TILES // 2 + 2:
                        x_tokens(j - 2)
                bk = take(("acs",))
                pe.wait_ge(adt_ready, 1)
                pe.wait_ge(consts, 7)
                for b in range(NB):
                    mm(bk[:, b * NH:(b + 1) * NH], tri[:], adt[:, b])
                mm(bk[:, NB * NH:2 * NB * NH], ones[:], adt[:, :, :].rearrange("p b h -> p (b h)")) \
                    .then_inc(mm_done, 1)
                pe.wait_ge(silu_ready, CONV_TILES)
                for c in range(2):
                    bk = take(("bT", c))
                    for g in range(4):
                        last = nc.tensor.transpose(bk[:, g * P:(g + 1) * P], bcT[:, 4 * c + g, 0:P], ident[:])
                    last.then_inc(mm_done, 1)
                for b in range(NB):
                    scan(b)
                for b in range(NB):
                    pe.wait_ge(yn_ready, b + 1)
                    for c in range(4):
                        bk = take(("ynT", b, c))
                        for k in range(4):
                            last = nc.tensor.transpose(bk[:, k * P:(k + 1) * P],
                                                       xh[:, b, (4 * c + k) * P:(4 * c + k + 1) * P], ident[:])
                        last.then_inc(mm_done, 1)
                for n in range(2):
                    bks = [take(("out", 0, n, b)) for b in range(NB)]
                    for kh in range(2):
                        key = ("out0", 0, KD * kh, WCOLS * n)
                        w_landed(pe, *key)
                        w = w_tile(*key)
                        for b in range(NB):
                            moved(pe, ("ynT", b, 3))
                            for k in range(KD):
                                last = mm(bks[b][:, :], ynT[:, KD * kh + k, b * P:(b + 1) * P], w[:, k],
                                          kh == 0 and k == 0, kh == 1 and k == KD - 1)
                            if kh == 1:
                                last.then_inc(mm_done, 1)

            def scan(b):
                tok = slice(b * P, (b + 1) * P)
                for c in range(2):
                    bk = take(("cb", b, c))
                    for g in range(4):
                        last = mm(bk[:, g * P:(g + 1) * P], bcT[:, 4 * c + g, tok], bcT[:, NG + 4 * c + g, tok])
                    last.then_inc(mm_done, 1)

                def sums_on_all(g):
                    bk = take(("bc", b, g))
                    for e in range(HG):
                        h = g * HG + e
                        last = mm(bk[:, e * P:(e + 1) * P], adt[:, b, h:h + 1].broadcast_to([P, P]), tri[:])
                    last.then_inc(mm_done, 1)

                sums_on_all(0)
                sums_on_all(1)
                for g in range(NG):
                    if g + 2 < NG:
                        sums_on_all(g + 2)
                    if g % 2 == 0:
                        bk = take(("y", b, g // 2))
                    pe.wait_ge(m_ready, b * NG + g + 1)
                    pe.wait_ge(xd_ready, b + 1)
                    for e in range(HG):
                        c0 = (g % 2) * GW + e * HP
                        last = mm(bk[:, c0:c0 + HP], seg[:, g % 4, e * P:(e + 1) * P], xd[:, g * HG + e])
                    if g % 2 == 0:
                        continue
                    last.then_inc(mm_done, 1)
                    bk = take(("st" if b == 0 else "yo", g // 2))
                    for gg in (g - 1, g):
                        cols = slice((gg % 2) * GW, (gg % 2 + 1) * GW)
                        if b == 0:
                            moved(pe, ("bT", 1))
                            pe.wait_ge(xde_ready, 1)
                            last = mm(bk[:, cols], b_tok[:, gg],
                                      xde[:, gg * HG:(gg + 1) * HG].rearrange("p a b -> p (a b)"))
                        else:
                            moved(pe, ("st", NG // 2 - 1))
                            last = mm(bk[:, cols], bcT[:, NG + gg, tok], state[:, gg * GW:(gg + 1) * GW])
                    last.then_inc(mm_done, 1)
                    zkey = Z_ORDER[b * NG // 2 + g // 2]
                    _, zb, zn = zkey
                    key = ("in", 0, 0, WCOLS * zn)
                    w_landed(pe, *key)
                    w = w_tile(*key)
                    bk = take(zkey)
                    project(bk[:, :], lambda k: hnT[:, k, zb * P:(zb + 1) * P], lambda k: w[:, k]) \
                        .then_inc(mm_done, 1)

            def rows_of(key, out_key, b, left):
                w_landed(pe, *key)
                w = w_tile(*key)
                bk = take(out_key)
                project(bk[:, :], left, lambda k: w[:, k]).then_inc(mm_done, 1)

            def qkv(b, n):
                rows_of(("qkv", 0, 0, WCOLS * n, b), ("qkv", n, b), b,
                        lambda k: hnT[:, k, b * P:(b + 1) * P])

            def qk_transposes(b):
                pe.wait_ge(qn_ready, b + 1)
                for c in range(4):
                    bk = take(("qkT", b, c))
                    for k in range(4):
                        last = nc.tensor.transpose(bk[:, k * P:(k + 1) * P],
                                                   qk[:, (4 * c + k) * P:(4 * c + k + 1) * P], ident[:])
                    last.then_inc(mm_done, 1)

            def head_scores(b, h):
                nk = (b + 1) * P
                if h == 0:
                    moved(pe, ("qkT", b, 3))
                for m in range(2):
                    bk = take(("S", b, h, m))
                    rows = slice(m * AD, (m + 1) * AD)
                    mm(bk[:, 0:nk], aqT[rows, h], kT[rows, h, 0:nk]).then_inc(mm_done, 1)

            def weighted(b, h):
                n = b * AH + h
                bk = take(("aT", b, h))
                pe.wait_ge(attn_ready, n + 1)
                for kb in range(b + 1):
                    last = nc.tensor.transpose(bk[:, kb * P:(kb + 1) * P],
                                               attn[:, n % 2, kb * P:(kb + 1) * P], ident[:])
                last.then_inc(mm_done, 1)
                bk = take(("O", b, h))
                moved(pe, ("aT", b, h))
                for kb in range(b + 1):
                    last = mm(bk[:, 0:P], attnT[:, n % 2, kb * P:(kb + 1) * P],
                              vv[:, kb, h * P:(h + 1) * P], kb == 0, kb == b)
                last.then_inc(mm_done, 1)

            def o_transposes(b):
                pe.wait_ge(on_ready, b + 1)
                for c in range(2):
                    bk = take(("oT", b, c))
                    for k in range(4):
                        last = nc.tensor.transpose(bk[:, k * P:(k + 1) * P],
                                                   o_sb[:, (4 * c + k) * P:(4 * c + k + 1) * P], ident[:])
                    last.then_inc(mm_done, 1)
                moved(pe, ("oT", b, 1))

            def attention_out(b, n):
                rows_of(("out1", 0, 0, WCOLS * n, b), ("out", 1, n, b), b, lambda k: oT[:, k])

            def select():
                for c in range(CHUNKS + 1):
                    if c < CHUNKS:
                        key = ("query", 0, 0, WCOLS * c)
                        w_landed(pe, *key)
                        w = w_tile(*key)
                        for j in range(2):
                            bk = take(("q", 0, 2 * c + j))
                            for s in range(2):
                                c0 = (2 * j + s) * P
                                last = project(bk[:, s * T:(s + 1) * T], lambda k: w[:, k, c0:c0 + P],
                                               lambda k: hnT[:, k])
                            last.then_inc(mm_done, 1)
                    if c:
                        if c == 1:
                            pe.wait_ge(keys_loaded, 16)
                        moved(pe, ("q", 0, 2 * c - 1))
                        for b in range(NB):
                            bk = take(("s", 0, b, c - 1))
                            for k in range(4):
                                hc = 4 * (c - 1) + k
                                last = mm(bk[:, k * P:(k + 1) * P], qT[:, hc % 8, b * P:(b + 1) * P],
                                          keysT[:, hc])
                            last.then_inc(mm_done, 1)

            def queries(b, c):
                key = ("query", 1, 0, WCOLS * c, b)
                w_landed(pe, *key)
                w = w_tile(*key)
                bk = take(("q", 1, b, c))
                for s in range(4):
                    last = project(bk[:, s * P:(s + 1) * P], lambda k: w[:, k, s * P:(s + 1) * P],
                                   lambda k: hnT[:, k, b * P:(b + 1) * P])
                last.then_inc(mm_done, 1)

            def scores(b, c):
                if b == 0 and c == 0:
                    pe.wait_ge(keys_loaded, 32)
                moved(pe, ("q", 1, b, c))
                bk = take(("s", 1, b, c))
                for k in range(4):
                    hc = 4 * c + k
                    last = mm(bk[:, k * P:(k + 1) * P], qbT[:, hc % 8], keysT[:, hc])
                last.then_inc(mm_done, 1)

            def front(b, part):
                if part == 0:
                    norm(2, [b])
                if part < 4:
                    qkv(b, part)
                elif part == 4:
                    qkv(b, 4)
                    qkv(b, 5)
                elif part == 5:
                    qk_transposes(b)
                elif 6 <= part <= 10:
                    if part > 6:
                        weighted(b, 2 * (part - 7))
                        weighted(b, 2 * (part - 7) + 1)
                    if part < 10:
                        head_scores(b, 2 * (part - 6))
                        head_scores(b, 2 * (part - 6) + 1)
                    else:
                        o_transposes(b)
                        attention_out(b, 0)
                elif part == 11:
                    attention_out(b, 1)
                elif part == 12:
                    norm(3, [b])
                if 12 <= part < 16:
                    queries(b, part - 12)
                if 13 <= part:
                    scores(b, part - 13)

            def residual(layer, b):
                n = layer * NB + b
                if n:
                    pe.wait_ge(x_fed, 2 * n)
                for half in range(2):
                    nc.tensor.matmul(ysum[half][:, :], ident[:], x[:, b, half * 512:(half + 1) * 512],
                                     start=True, stop=False, skip_group_check=True)

            def group(layer, b, i):
                n0 = (layer * NB + b) * PAIRS
                for k in range(GRP):
                    pe.wait_ge(diag_ready, i * GRP + (n0 + k + 1))
                    pe.wait_ge(v_loaded[k], i * 16 + 16 * (n0 // GRP + 1))
                    for half in range(2):
                        last = nc.tensor.matmul(ysum[half][:, :], diag[:, k % DIAGS],
                                                ring[:, GRP + k, half * 512:(half + 1) * 512],
                                                start=False, stop=False, skip_group_check=True)
                    last.then_inc(v_free, 1)

            def groups(layer, b):
                residual(layer, b)
                with pe.Fori(0, GROUPS) as i:
                    group(layer, b, i)

            norm(0)
            ssd()
            norm(1)
            select()
            groups(0, 0)
            for layer, b, other in ((0, 1, 0), (1, 0, 1)):
                for g in range(GROUPS):
                    front(other, g)
                    if g == 0:
                        residual(layer, b)
                    group(layer, b, g)
                front(other, GROUPS)
            groups(1, 1)

        @block.vector
        def _(dve):
            seq = [0]

            def step(ins):
                seq[0] += 1
                ins.then_inc(dve_seq, 1)

            def settle():
                dve.wait_ge(dve_seq, seq[0])

            V = nc.vector

            def norm(i, blocks=range(NB)):
                dve.wait_ge(normw_loaded[i], 16)
                for b in blocks:
                    st = stat[:, 2 * i + b]
                    dve.wait_ge(std_ready, normed(i, b))
                    step(V.reciprocal(st[:, 2:3], st[:, 1:2]))
                    settle()
                    if i:
                        produced(dve, ("nT", i - 1, b, 1))
                    V.scalar_tensor_tensor(out=hn[:, b], in0=x[:, b], scalar=st[:, 2:3], in1=norm_w[:, i % 2],
                                           op0=ALU.mult, op1=ALU.mult).then_inc(hn_ready, 1)

            def soft_plus():
                produced(dve, ("dt",))
                dve.wait_ge(dt_loaded, 32)
                v, a, e, r, r2, p = (spt[:, j] for j in range(6))
                key = ("dt",)
                V.tensor_tensor(v.rearrange("p (b h) -> p b h", b=NB),
                                bank(key)[:, 0:NB * NH].rearrange("p (b h) -> p b h", b=NB),
                                dtb[:, :].unsqueeze(1).broadcast_to([P, NB, NH]), ALU.add) \
                    .then_inc(read_of(key), 1)
                moved(dve, key)
                V.scalar_tensor_tensor(out=a, in0=v, scalar=-1.0, in1=v, op0=ALU.mult,
                                       op1=ALU.max).then_inc(dt_abs_ready, 1)
                dve.wait_ge(dt_exp_ready, 1)
                step(V.tensor_scalar(r2, e, 2.0, None, ALU.add))
                settle()
                step(V.reciprocal(p, r2))
                settle()
                step(V.tensor_tensor(r, e, p, ALU.mult))
                settle()
                step(V.tensor_tensor(r2, r, r, ALU.mult))
                settle()
                step(V.tensor_scalar(p, r2, ATANH[-1], None, ALU.mult))
                settle()
                for coef in ATANH[-2::-1]:
                    step(V.scalar_tensor_tensor(out=p, in0=p, scalar=coef, in1=r2, op0=ALU.add, op1=ALU.mult))
                    settle()
                step(V.scalar_tensor_tensor(out=p, in0=p, scalar=1.0, in1=r, op0=ALU.add, op1=ALU.mult))
                step(V.tensor_scalar(a, v, 0.0, None, ALU.max))
                settle()
                step(V.scalar_tensor_tensor(out=dts[:, :, :].rearrange("p b h -> p (b h)"), in0=p, scalar=2.0,
                                            in1=a, op0=ALU.mult, op1=ALU.add))
                settle()
                for b in range(NB):
                    last = V.scalar_tensor_tensor(out=adt[:, b], in0=dts[:, b], scalar=-1.0, in1=expa[:],
                                                  op0=ALU.mult, op1=ALU.mult)
                last.then_inc(adt_ready, 1)

            def convolve(j):
                key = ("xbc", j)
                dve.wait_ge(first_tap_ready, 2 * j + 2)
                for tap in range(CONV - 2, -1, -1):
                    back = CONV - 1 - tap
                    for s in range(2):
                        c = 2 * j + s
                        o = cv[:, c % 4, back:T]
                        last = V.scalar_tensor_tensor(out=o, in0=bank(key)[:, s * T:(s + 1) * T - back],
                                                      scalar=cw[:, c, tap:tap + 1], in1=o, op0=ALU.mult,
                                                      op1=ALU.add)
                        if tap:
                            step(last)
                    if tap:
                        settle()
                last.then_inc(read_of(key), 1)

            def ssd():
                soft_plus()
                for j in range(CONV_TILES // 2):
                    convolve(j)
                key = ("acs",)
                produced(dve, key)
                V.tensor_copy(acs[:, :, :].rearrange("p b h -> p (b h)"),
                              bank(key)[:, 0:2 * NB * NH]).then_inc(read_of(key), 1)
                moved(dve, key)
                V.tensor_tensor(toend[:], acs[:, NB], acs[:, 0], ALU.subtract).then_inc(toend_ready, 1)
                for b in range(NB):
                    scan(b)
                settle()
                for b in range(NB):
                    for q in range(4):
                        cols = slice(q * WCOLS, (q + 1) * WCOLS)
                        dve.wait_ge(zs_ready, 4 * b + q + 1)
                        V.tensor_tensor(xh[:, b, cols], xh[:, b, cols], zs[:, b, cols], ALU.mult) \
                            .then_inc(gated_ready, 1)
                for b in range(NB):
                    dve.wait_ge(gstd_ready, b + 1)
                    step(V.reciprocal(gst[:, b, 2], gst[:, b, 1]))
                    settle()
                    yg = xh[:, b].rearrange("p (g c) -> p g c", g=NG)
                    V.tensor_tensor(yg, yg, bcast(gst[:, b, 2], GW), ALU.mult).then_inc(yn_ready, 1)
                for b in range(NB):
                    for c in range(4):
                        key = ("ynT", b, c)
                        produced(dve, key)
                        V.tensor_tensor(ynT[:, 4 * c:4 * c + 4, b * P:(b + 1) * P],
                                        bank(key)[:, :].rearrange("p (k t) -> p k t", k=4),
                                        bcast(snw[:, 4 * c:4 * c + 4], P), ALU.mult).then_inc(read_of(key), 1)
                for n in range(2):
                    for b in range(NB):
                        add_back(0, n, b)

            def scan(b):
                yb = xh[:, b]
                xb = yb.rearrange("p (h e) -> p h e", e=HP)
                if b == 0:
                    moved(dve, ("xT", XS_TILES // 2 - 1))
                    dve.wait_ge(ssd_loaded, 32)
                else:
                    produced(dve, ("y", b - 1, NG // 2 - 1))
                V.tensor_tensor(xd[:, :, :], xb, bcast(dts[:, b], HP), ALU.mult).then_inc(xd_ready, 1)
                dve.wait_ge(eacs_ready, 2)
                if b == 0:
                    dve.wait_ge(xd_ready, 1)
                    V.tensor_tensor(xde[:, :, :], xd[:, :, :], bcast(toend[:], HP), ALU.mult) \
                        .then_inc(xde_ready, 1)
                for c in range(2):
                    key = ("cb", b, c)
                    produced(dve, key)
                    V.tensor_tensor(cbm[:, 4 * c:4 * c + 4], bank(key)[:, :].rearrange("p (g l) -> p g l", g=4),
                                    tri[:, :].unsqueeze(1).broadcast_to([P, 4, P]), ALU.mult) \
                        .then_inc(read_of(key), 1)

                def differences(g):
                    key = ("bc", b, g)
                    produced(dve, key)
                    if b * NG + g >= 4:
                        pb, pg = (b, g - 4) if g >= 4 else (b - 1, g + 4)
                        produced(dve, ("y", pb, pg // 2))
                    for e in range(HG):
                        h = g * HG + e
                        last = V.tensor_scalar(seg[:, g % 4, e * P:(e + 1) * P], bank(key)[:, e * P:(e + 1) * P],
                                               acs[:, b, h:h + 1], 0.0, ALU.subtract, ALU.min)
                    last.then_inc(read_of(key), 1)

                def collect(q):
                    cols = slice(q * WCOLS, (q + 1) * WCOLS)
                    key = ("y", b, q)
                    produced(dve, key)
                    V.tensor_tensor(yb[:, cols], yb[:, cols], bank(key)[:, :], ALU.add).then_inc(read_of(key), 1)
                    if b:
                        key = ("yo", q)
                        produced(dve, key)
                        V.tensor_tensor(yoff.rearrange("p (h e) -> p h e", e=HP),
                                        bank(key)[:, :].rearrange("p (h e) -> p h e", e=HP),
                                        bcast(eacs[:, 2 * HG * q:2 * HG * (q + 1)], HP), ALU.mult) \
                            .then_inc(read_of(key), 1)
                        moved(dve, key)
                        moved(dve, ("y", b, q))
                        step(V.tensor_tensor(yb[:, cols], yb[:, cols], yoff, ALU.add))

                differences(0)
                dve.wait_ge(xd_ready, b + 1)
                step(V.tensor_tensor(xb, xb, bcast(dsk[:], HP), ALU.mult))
                settle()
                moved(dve, ("cb", b, 1))
                for g in range(NG):
                    if g + 1 < NG:
                        differences(g + 1)
                    dve.wait_ge(decay_ready, b * NG + g + 1)
                    sg = seg[:, g % 4].rearrange("p (e l) -> p e l", e=HG)
                    V.tensor_tensor(sg, sg, cbm[:, g:g + 1].broadcast_to([P, HG, P]), ALU.mult) \
                        .then_inc(m_ready, 1)
                    if g % 2 == 0 and g >= 2:
                        collect(g // 2 - 1)
                collect(NG // 2 - 1)
                moved(dve, ("y", b, NG // 2 - 1))

            def add_back(layer, n, b):
                key = ("out", layer, n, b)
                produced(dve, key)
                xc = x[:, b, n * WCOLS:(n + 1) * WCOLS]
                V.tensor_tensor(xc, xc, bank(key)[:, :], ALU.add).then_inc(read_of(key), 1)

            def lambdas():
                dve.wait_ge(attn_loaded, 16 * 9)
                for j in range(2):
                    V.tensor_tensor_reduce(lams[:, 2 * j], lams[:, 2 * j], lams[:, 2 * j + 1], 1.0, 0.0, ALU.mult,
                                           ALU.add, lam[:, j:j + 1]).then_inc(lamdot_ready, 1)
                dve.wait_ge(lamexp_ready, 1)
                step(V.tensor_tensor(lam[:, 4:5], lam[:, 2:3], lam[:, 3:4], ALU.subtract))
                settle()
                step(V.tensor_scalar(lam[:, 5:6], lam[:, 4:5], -1.0, -LAMBDA_INIT, ALU.mult, ALU.add))

            def square_sums(b, n):
                m = 4 * b + n
                dve.wait_ge(sq_ready, m + 1)
                V.tensor_reduce(qst[:, 0, b, 8 * n:8 * n + 8], sq[:, m % 2].rearrange("p (h d) -> p h d", d=AD),
                                AX.X, ALU.add).then_inc(qss_ready, 1)

            def qk_normed(b):
                dve.wait_ge(qstd_ready, b + 1)
                step(V.reciprocal(qst[:, 2, b], qst[:, 1, b]))
                settle()
                q3 = qk.rearrange("p (h d) -> p h d", d=AD)
                V.tensor_tensor(q3, q3, bcast(qst[:, 2, b], AD), ALU.mult).then_inc(qn_ready, 1)

            def qk_transposed(b):
                for c in range(4):
                    key = ("qkT", b, c)
                    produced(dve, key)
                    which = c // 2
                    heads = slice(4 * (c % 2), 4 * (c % 2) + 4)
                    V.tensor_scalar(aqT[:, heads] if which == 0 else kT[:, heads, b * P:(b + 1) * P],
                                    bank(key)[:, :].rearrange("p (k t) -> p k t", k=4),
                                    qkn[:, which:which + 1], AD ** -0.5 if which == 0 else 1.0,
                                    ALU.mult, ALU.mult).then_inc(read_of(key), 1)

            def masked(b, h):
                n = b * AH + h
                nk = (b + 1) * P
                if n >= 2:
                    dve.wait_ge(attn_ready, n - 1)
                for m in range(2):
                    key = ("S", b, h, m)
                    produced(dve, key)
                    V.tensor_tensor(prob[:, n % 2, m, 0:nk], bank(key)[:, 0:nk], mask[:, b, 0:nk],
                                    ALU.add).then_inc(read_of(key), 1)
                for m in range(2):
                    moved(dve, ("S", b, h, m))
                V.tensor_reduce(smx[:, 0, n % 2], prob[:, n % 2, :, 0:nk], AX.X, ALU.max,
                                negate=True).then_inc(max_ready, 1)

            def combined(b, h):
                n = b * AH + h
                nk = (b + 1) * P
                dve.wait_ge(exp_ready, 2 * n + 2)
                step(V.reciprocal(smx[:, 2, n % 2], smx[:, 1, n % 2]))
                settle()
                step(V.tensor_tensor(smx[:, 3, n % 2, 0:1], smx[:, 2, n % 2, 1:2], lam[:, 5:6], ALU.mult))
                if n >= 2:
                    produced(dve, ("aT", *HEADS[n - 2]))
                step(V.tensor_scalar(attn[:, n % 2, 0:nk], prob[:, n % 2, 0, 0:nk],
                                     smx[:, 2, n % 2, 0:1], None, ALU.mult))
                settle()
                V.scalar_tensor_tensor(out=attn[:, n % 2, 0:nk], in0=prob[:, n % 2, 1, 0:nk],
                                       scalar=smx[:, 3, n % 2, 0:1], in1=attn[:, n % 2, 0:nk],
                                       op0=ALU.mult, op1=ALU.add).then_inc(attn_ready, 1)

            def o_normed(b):
                dve.wait_ge(ostd_ready, b + 1)
                step(V.reciprocal(ost[:, 2, b], ost[:, 1, b]))
                settle()
                o3 = o_sb.rearrange("p (h e) -> p h e", h=AH)
                V.tensor_tensor(o3, o3, bcast(ost[:, 2, b], P), ALU.mult).then_inc(on_ready, 1)
                for c in range(2):
                    key = ("oT", b, c)
                    produced(dve, key)
                    V.tensor_scalar(oT[:, 4 * c:4 * c + 4],
                                    bank(key)[:, :].rearrange("p (k t) -> p k t", k=4), sub_w[:, 0:1],
                                    1.0 - LAMBDA_INIT, ALU.mult, ALU.mult).then_inc(read_of(key), 1)

            def best_16(values, top, where):
                sets = range(values.shape[1])
                for half in range(2):
                    ks = slice(8 * half, 8 * half + 8)
                    for j in sets:
                        step(V.max(top[:, j, ks], values[:, j]))
                    settle()
                    for j in sets:
                        step(V.max_index(where[:, j, ks], top[:, j, ks], values[:, j]))
                    settle()
                    if half == 0:
                        for j in sets:
                            step(V.match_replace(values[:, j], top[:, j, ks], values[:, j], MASKED))
                        settle()

            def pairs_of(out_, first, second):
                for i in range(5):
                    n, o = CAND_LEN[i], CAND_OFF[i]
                    V.tensor_tensor(out_[:, :, o:o + n], first[:, :, i:i + 1].broadcast_to([P, 2, n]),
                                    second[:, :, 0:n], ALU.add)
                o = CAND_OFF[5]
                V.tensor_tensor(out_[:, :, o:o + 6].rearrange("p h (i j) -> p h i j", j=2),
                                first[:, :, 5:8].unsqueeze(3).broadcast_to([P, 2, 3, 2]),
                                second[:, :, 0:2].unsqueeze(2).broadcast_to([P, 2, 3, 2]), ALU.add)
                o = CAND_OFF[8]
                step(V.tensor_tensor(out_[:, :, o:o + 8], first[:, :, 8:16],
                                     second[:, :, 0:1].broadcast_to([P, 2, 8]), ALU.add))

            def choose(layer, b, c):
                moved(dve, ("s", layer, b, c))
                best_16(sc[:, HC * b + 4 * c:HC * b + 4 * c + 4] if layer == 0
                        else sc2[:, 4 * (c % 2):4 * (c % 2) + 4], topv, topi)
                step(V.tensor_copy(topf, topi))
                settle()
                values, places = (t.rearrange("p (h c) k -> p h c k", c=2) for t in (topv, topf))
                step(V.tensor_scalar(places[:, :, 0], places[:, :, 0], float(NK), None, ALU.mult))
                pairs_of(cs, values[:, :, 0], values[:, :, 1])
                settle()
                pairs_of(ci, places[:, :, 0], places[:, :, 1])
                best_16(cs, best, posi)
                step(V.tensor_copy(posf[:], posi))
                V.tensor_tensor(gate[:, b, 2 * TOPK * c:2 * TOPK * (c + 1)].rearrange("p (h k) -> p h k", h=2),
                                best[:], best[:, :, 0:1].broadcast_to([P, 2, TOPK]),
                                ALU.subtract).then_inc(gsub_ready, 1)
                settle()
                shape = [P, 2, TOPK, NC]
                step(V.tensor_tensor(eq, posf[:, :].unsqueeze(3).broadcast_to(shape),
                                     iota[:, :].unsqueeze(1).unsqueeze(1).broadcast_to(shape), ALU.is_equal))
                settle()
                step(V.tensor_tensor(eq, eq, ci[:, :].unsqueeze(2).broadcast_to(shape), ALU.mult))
                settle()
                step(V.tensor_reduce(idxf.rearrange("p (a k) -> p a k", a=2), eq, AX.X, ALU.add))
                settle()
                V.tensor_scalar(idx[:, b, 2 * TOPK * c:2 * TOPK * (c + 1)], idxf, float(layer * NE), None,
                                ALU.add).then_inc(idx_ready, 2)
                dve.wait_ge(idx_ready, 2 * chosen(layer, b, c))

            def gates(layer, b, c):
                part = gate[:, b, 2 * TOPK * c:2 * TOPK * (c + 1)].rearrange("p (h k) -> p h k", h=2)
                dve.wait_ge(gexp_ready, chosen(layer, b, c))
                step(V.tensor_reduce(gsum[:, 0], part, AX.X, ALU.add))
                settle()
                step(V.reciprocal(gsum[:, 1], gsum[:, 0]))
                settle()
                step(V.tensor_tensor(part, part, bcast(gsum[:, 1], TOPK), ALU.mult))
                settle()

            def group(layer, b, i, h, first_of=None):
                g0 = (layer * NB + b) * GROUPS
                for k in range(GRP):
                    dve.wait_ge(u_loaded[k], i * 32 + 16 * (g0 + h + 1))
                    V.tensor_tensor_reduce(ring[:, k], ring[:, k], hn[:, b], 1.0, 0.0, ALU.mult, ALU.add,
                                           acts[:, h, k:k + 1]).then_inc(u_free, 1)
                if first_of is not None:
                    gates(layer, b, first_of)
                dve.wait_ge(gelu_ready, i * 2 + (g0 + h + 1))
                V.tensor_tensor(wts[:, h], gel[:, h], gate[:, b, bass.ds(i * (2 * GRP) + h * GRP, GRP)],
                                ALU.mult).then_inc(wts_ready, 1)

            def nth_group(layer, b, g):
                group(layer, b, g // 2, g % 2, g // CHUNK_GROUPS if g % CHUNK_GROUPS == 0 else None)

            def groups(layer, b, first):
                for c in range((first - 1) // 2 + 1, CHUNKS):
                    gates(layer, b, c)
                with dve.Fori(first, GROUPS // 2) as i:
                    for h in range(2):
                        group(layer, b, i, h)

            def finish(layer, b):
                dve.wait_ge(v_free, GRP + (layer * NB + b + 1) * PAIRS)
                for half in range(2):
                    V.tensor_copy(x[:, b, half * 512:(half + 1) * 512], ysum[half][:, :]).then_inc(x_fed, 1)

            def front(b, part):
                if part == 0:
                    norm(2, [b])
                if part < 4:
                    square_sums(b, part)
                elif part == 4:
                    qk_normed(b)
                elif part == 5:
                    qk_transposed(b)
                elif 6 <= part <= 9:
                    for h in (2 * (part - 6), 2 * (part - 6) + 1):
                        masked(b, h)
                    for h in (2 * (part - 6), 2 * (part - 6) + 1):
                        combined(b, h)
                elif part == 10:
                    o_normed(b)
                    add_back(1, 0, b)
                elif part == 11:
                    add_back(1, 1, b)
                elif part == 12:
                    norm(3, [b])
                elif part in (14, 16):
                    choose(1, b, (part - 14) // 2)

            norm(0)
            ssd()
            norm(1)
            choose(0, 0, 0)
            choose(0, 0, 1)
            nth_group(0, 0, 0)
            choose(0, 0, 2)
            nth_group(0, 0, 1)
            choose(0, 0, 3)
            nth_group(0, 0, 2)
            nth_group(0, 0, 3)
            for c in range(CHUNKS):
                choose(0, 1, c)
                nth_group(0, 0, CHUNKS + c)
            groups(0, 0, CHUNKS)
            lambdas()
            finish(0, 0)
            for layer, b, other in ((0, 1, 0), (1, 0, 1)):
                for g in range(GROUPS):
                    nth_group(layer, b, g)
                    front(other, g)
                    if layer and g in (1, 2):
                        choose(1, b, g + 1)
                front(other, GROUPS)
                finish(layer, b)
            for g in range(4):
                nth_group(1, 1, g)
                if g in (1, 2):
                    choose(1, 1, g + 1)
            groups(1, 1, 2)
            finish(1, 1)


def kernel(**inputs):
    import numpy as np
    import concourse.bacc as bacc
    from concourse.bass_utils import run_bass_kernel_spmd

    a = {name: np.asarray(v) for name, v in inputs.items()}
    tiles = CONV_TILES
    arrays = {
        "x_in": a["x"],
        "mix_norm_w": a["mix_norm_w"],
        "ffn_norm_w": a["ffn_norm_w"],
        "in_w": a["ssd_in_w"],
        "conv_w": a["ssd_conv_w"][0].T.reshape(tiles, P, CONV).transpose(1, 0, 2),
        "conv_b": a["ssd_conv_b"][0].reshape(tiles, P).T,
        "dt_bias": a["ssd_dt_bias"],
        "a_log": a["ssd_a_log"],
        "d_skip": a["ssd_d"],
        "ssd_norm_w": a["ssd_norm_w"][0].reshape(XS_TILES, P).T,
        "ssd_out_w": a["ssd_out_w"],
        "qkv_w": a["da_qkv_w"],
        "q_norm_w": a["da_q_norm_w"],
        "k_norm_w": a["da_k_norm_w"],
        "lam_q1": a["da_lam_q1"],
        "lam_k1": a["da_lam_k1"],
        "lam_q2": a["da_lam_q2"],
        "lam_k2": a["da_lam_k2"],
        "subln_w": a["da_subln_w"],
        "da_out_w": a["da_out_w"],
        "query_w": a["peer_query_w"],
        "keys_t": a["peer_sub_keys"].reshape(DEPTH, HC, NK, -1).transpose(0, 1, 3, 2),
        "peer_u": a["peer_u"],
        "peer_v": a["peer_v"],
    }
    arrays = {name: np.ascontiguousarray(v) for name, v in arrays.items()}
    nc = bacc.Bacc("TRN2", target_bir_lowering=False, num_devices=1)
    args = [nc.dram_tensor(f"in_{name}", v.shape, mybir.dt.from_np(v.dtype), kind="ExternalInput").ap()
            for name, v in arrays.items()]
    args.append(nc.dram_tensor("out_y", a["x"].shape, mybir.dt.from_np(a["x"].dtype),
                               kind="ExternalOutput").ap())
    build(nc, *args)
    r = run_bass_kernel_spmd(nc, [{f"in_{name}": v for name, v in arrays.items()}], core_ids=[0])
    return r.results[0]["out_y"]
```

```python
import math
from contextlib import ExitStack

import concourse.bass as bass
from concourse import mybir

F32 = mybir.dt.float32
U32 = mybir.dt.uint32
F32R = mybir.dt.float32r
ALU = mybir.AluOpType
ACT = mybir.ActivationFunctionType
AX = mybir.AxisListType

P = 128
T = 256
NB = T // P
D = 1024
KD = D // P
DEPTH = 2
EPS = 1e-6
DI = 2048
NH = 32
HP = 64
NG = 8
HG = NH // NG
NS = 128
CONV = 4
GW = HG * HP
CONV_TILES = (DI + 2 * NG * NS) // P
XS_TILES = DI // P
AH = 8
AD = 64
LAMBDA_INIT = 0.8 - 0.6 * math.exp(-0.3 * 1)
MASKED = -1e30
PH = 8
NK = 128
TOPK = 16
NE = NK * NK
HC = 2 * PH
PAIRS = PH * TOPK
GRP = 8
DIAGS = 4
CAND_LEN = [TOPK // (i + 1) for i in range(TOPK)]
CAND_OFF = [sum(CAND_LEN[:i]) for i in range(TOPK)]
NC = sum(CAND_LEN)
ATANH = [1.0 / (2 * k + 1) for k in range(1, 10)]

WCOLS = 512
WSLOTS = 3
MM_BANKS = 6


Z_ORDER = [("z", b, n) for n in range(4) for b in range(NB)]
Z_AT = {(0, -1): 1, (0, 1): 2, (0, 3): 3, (0, 5): 4, (0, 7): 5, (1, -1): 6, (1, 1): 7}
HEADS = [(b, h) for b in range(NB) for h in range(AH)]
NORM_ORDER = [(0, 0), (0, 1), (1, 0), (1, 1), (2, 0), (3, 0), (2, 1), (3, 1)]
FIRST_CHOICE = [
    [("q", 1, 1), ("s", 1, 0), ("q", 0, 2)],
    [("s", 1, 1), ("s", 0, 2), ("q", 1, 2)],
    [("s", 1, 2), ("q", 0, 3)],
    [("s", 0, 3), ("q", 1, 3)],
    [("s", 1, 3)],
]
CHUNKS = HC // 4
CHUNK_GROUPS = 2 * TOPK // GRP
GROUPS = PAIRS // GRP


def psum_plan():
    order = []

    def norm(i, blocks=range(NB)):
        order.extend(("nT", i, b, c) for b in blocks for c in range(2))

    norm(0)
    for j in range(CONV_TILES // 2):
        order.append(("xbc", j))
        if j == 0:
            order.append(("dt",))
        if 2 <= j < XS_TILES // 2 + 2:
            order.append(("xT", j - 2))
    order.append(Z_ORDER[0])
    order.append(("acs",))
    order.extend(("bT", c) for c in range(2))
    for b in range(NB):
        order.extend(("cb", b, c) for c in range(2))
        order.extend(("bc", b, g) for g in range(2))
        for g in range(-1, NG):
            if 0 <= g and g + 2 < NG:
                order.append(("bc", b, g + 2))
            if g % 2 == 1:
                if g > 0:
                    order.append(("y", b, g // 2))
                    order.append(("st" if b == 0 else "yo", g // 2))
                if (b, g) in Z_AT:
                    order.append(Z_ORDER[Z_AT[b, g]])
            if (b, g) == (1, 5):
                order.extend(("ynT", 0, c) for c in range(4))
    order.extend(("out", 0, n, 0) for n in range(2))
    order.extend(("ynT", 1, c) for c in range(4))
    norm(1, [0])
    order.extend([("q", 0, 0, 0), ("s", 0, 0, 0), ("out", 0, 1, 1), ("out", 0, 0, 1)])
    order.extend([("q", 0, 0, 1), ("s", 0, 0, 1)])
    norm(1, [1])
    order.append(("q", 0, 1, 0))
    order.extend((name, 0, b, c) for uses in FIRST_CHOICE for name, b, c in uses)
    for b in range(NB):
        norm(2, [b])
        order.extend(("qkv", n, b) for n in range(6))
        order.extend(("qkT", b, c) for c in range(4))
        for h in range(0, AH + 2, 2):
            if h:
                order.extend([("aT", b, h - 2), ("O", b, h - 2), ("aT", b, h - 1), ("O", b, h - 1)])
            if h < AH:
                order.extend(("S", b, hh, m) for hh in (h, h + 1) for m in range(2))
        order.extend(("oT", b, c) for c in range(2))
        order.extend(("out", 1, n, b) for n in range(2))
        norm(3, [b])
        for c in range(CHUNKS + 1):
            if c < CHUNKS:
                order.append(("q", 1, b, c))
            if c:
                order.append(("s", 1, b, c - 1))
    return {key: (n % MM_BANKS, n // MM_BANKS, n) for n, key in enumerate(order)}


def weight_plan():
    tiles = [("in", 0, 0, DI + WCOLS * j) for j in range(8)]
    tiles += [("in", 0, 0, WCOLS * j) for j in range(4)]
    tiles += [("out0", 0, KD * kh, WCOLS * n) for n in range(2) for kh in range(2)]
    tiles += [("query", 0, 0, WCOLS * j) for j in range(4)]
    for b in range(NB):
        tiles += [("qkv", 0, 0, WCOLS * j, b) for j in range(6)]
        tiles += [("out1", 0, 0, WCOLS * n, b) for n in range(2)]
        tiles += [("query", 1, 0, WCOLS * j, b) for j in range(4)]
    return tiles


def build(nc, x_in, mix_norm_w, ffn_norm_w, in_w, conv_w, conv_b, dt_bias, a_log, d_skip, ssd_norm_w,
          ssd_out_w, qkv_w, q_norm_w, k_norm_w, lam_q1, lam_k1, lam_q2, lam_k2, subln_w, da_out_w,
          query_w, keys_t, peer_u, peer_v, out):
    PLAN = psum_plan()
    WTILES = weight_plan()
    EXTRA = {("out0", 0, KD, WCOLS): WSLOTS, ("query", 0, 0, 0): WSLOTS + 1}
    WAT, held = {}, [[] for _ in range(WSLOTS + len(EXTRA))]
    second = WTILES.index(("qkv", 0, 0, 0, 0))
    for n, key in enumerate(WTILES):
        if key in EXTRA:
            slot = EXTRA[key]
        elif key[0] == "query" and n < second:
            slot = (key[3] // WCOLS + 1) % WSLOTS
        else:
            slot = n % WSLOTS if n < second else (n - second) % (WSLOTS - 1)
        WAT[key] = (slot, len(held[slot]) + 1, held[slot][-1] if held[slot] else None)
        held[slot].append(key)
    in_cols = in_w.shape[2]

    with ExitStack() as ctx:
        def sb(name, shape, dt=F32):
            return ctx.enter_context(nc.sbuf_tensor(name, shape, dt))

        def sb_under(*parts):
            with ExitStack() as place:
                return [place.enter_context(nc.sbuf_tensor(name, [P, *shape], F32R)) for name, shape in parts]

        def sem(name):
            return ctx.enter_context(nc.semaphore(name))

        ident = sb("ident", [P, P])
        tri = sb("tri", [P, P])
        ones = sb("ones", [P, P])
        mask = sb("mask", [P, NB, T])
        iota = sb("iota", [P, NC])
        eps = sb("eps", [P, 1])
        norm_w = sb("norm_w", [P, 2, D])
        w_dt = sb("w_dt", [P, KD, NH])
        cw = sb("cw", [P, CONV_TILES, CONV])
        cb = sb("cb", [P, CONV_TILES])
        dtb = sb("dtb", [P, NH])
        alog = sb("alog", [P, NH])
        dsk = sb("dsk", [P, NH])
        snw = sb("snw", [P, XS_TILES])
        qkn = sb("qkn", [P, 2])
        lams = sb("lams", [P, 4, AD])
        sub_w = sb("sub_w", [P, 1])
        x = sb("x", [P, NB, D])
        hn = sb("hn", [P, NB, D])
        hnT = sb("hnT", [P, KD, T])
        w_low, = sb_under(("w_low", (WSLOTS, KD, WCOLS)))
        wring = sb("wring", [P, WSLOTS, KD, WCOLS])
        keysT = sb("keysT", [P, HC, NK])
        stat = sb("stat", [P, 8, 4])
        _, w_high = sb_under(("w_high_offset", (8192,)), ("w_high", (2, KD, WCOLS)))
        ring = sb("ring", [P, 2 * GRP, D])
        ring_flat = ring[:, :, :].rearrange("p a b -> p (a b)")
        hn_high, hn_low = sb_under(("hn_high", (KD, T)), ("hn_low", (KD, T)))
        tmp = sb("tmp", [P, 8192])

        def view(base, off, *dims):
            n = math.prod(dims)
            v = base[:, off:off + n]
            if len(dims) == 2:
                return v.rearrange("p (a b) -> p a b", a=dims[0])
            if len(dims) == 3:
                return v.rearrange("p (a b c) -> p a b c", a=dims[0], b=dims[1])
            return v

        xh = view(ring_flat, 0, NB, DI)
        bcT = view(ring_flat, 4096, 2 * NG, T)
        zs = view(ring_flat, 8192, NB, DI)
        ynT = view(ring_flat, 12288, XS_TILES, T)
        tmp_ap = tmp[:, :]
        xd = view(tmp_ap, 0, NH, HP)
        state = view(tmp_ap, 4096, DI)
        cv = view(tmp_ap, 6144, 4, T)
        xsT = view(tmp_ap, 7168, 4, T)
        seg = view(tmp_ap, 6144, 4, HG * P)
        xde = view(ring_flat, 12288, NH, HP)
        b_tok = view(ring_flat, 14336, NG, NS)
        kT = view(tmp_ap, 0, AH, T)
        vv = view(tmp_ap, 2048, NB, D)
        aqT = view(tmp_ap, 4096, AH, P)
        att_ap = wring[:, WSLOTS - 1].rearrange("p a b -> p (a b)")
        qk = view(att_ap, 0, 2 * D)
        o_sb = view(att_ap, 0, D)
        oT = view(att_ap, 1024, AH, P)
        prob = view(att_ap, 2048, 2, 2, T)
        sq = view(att_ap, 2048, 2, WCOLS)
        attn = view(att_ap, 3072, 2, T)
        attnT = view(att_ap, 3584, 2, T)
        qT = view(tmp_ap, 0, 16, P)
        sc = view(tmp_ap, 2048, NB * HC, NK)
        qbT = view(tmp_ap, 5120, 8, P)
        sc2 = view(tmp_ap, 4096, 8, NK)
        eq = view(tmp_ap, 6144, 2, TOPK, NC)
        small = sb("small", [P, 1824])
        small_ap = small[:, :]
        junk = sb("junk", [P, GW])
        topv = view(small_ap, 0, 4, TOPK)
        topf = view(small_ap, 512, 4, TOPK)
        topi = topf.bitcast(U32)
        cs = view(small_ap, 1024, 2, NC)
        ci = view(small_ap, 1424, 2, NC)
        best = sb("best", [P, 2, TOPK])
        posf = sb("posf", [P, 2, TOPK])
        posi = posf[:, :, :].bitcast(U32)
        gsum = sb("gsum", [P, 2, 2])
        gate = sb("gate", [P, NB, PAIRS])
        idx = sb("idx", [P, NB, PAIRS], U32)
        idxf = posf[:, :, :].rearrange("p h k -> p (h k)")
        idx_now = sb("idx_now", [P, 2, GRP], U32)
        acts = sb("acts", [P, 2, GRP])
        gel = sb("gel", [P, 2, GRP])
        wts = sb("wts", [P, 2, GRP])
        diag = sb("diag", [P, DIAGS, P])
        dts = sb("dts", [P, NB, NH])
        adt = sb("adt", [P, NB, NH])
        acs = sb("acs", [P, 2 * NB, NH])
        eacs = sb("eacs", [P, NH])
        toend = sb("toend", [P, NH])
        spt = view(tmp_ap, 4096, 6, NB * NH)
        expa = sb("expa", [P, NH])
        cbm = view(small_ap, 0, NG, P)
        yoff = view(small_ap, 1024, WCOLS)
        gst = sb("gst", [P, NB, 3, NG])
        qst = sb("qst", [P, 3, NB, 2 * 2 * AH])
        lam = sb("lam", [P, 8])
        smx = sb("smx", [P, 4, 2, 2])
        ost = sb("ost", [P, 3, NB, AH])

        banks = [ctx.enter_context(nc.psum_tensor(f"mm{i}", [P, 512], F32)) for i in range(MM_BANKS)]
        ysum = [ctx.enter_context(nc.psum_tensor(f"ysum{i}", [P, 512], F32)) for i in range(2)]

        x_loaded = [sem(f"x{b}_loaded") for b in range(NB)]
        wdt_loaded = sem("wdt_loaded")
        conv_loaded = sem("conv_loaded")
        dt_loaded = sem("dt_loaded")
        ssd_loaded = sem("ssd_loaded")
        attn_loaded = sem("attn_loaded")
        normw_loaded = [sem(f"normw{i}_loaded") for i in range(2 * DEPTH)]
        keys_loaded = sem("keys_loaded")
        w_loaded = [sem(f"w{i}_loaded") for i in range(WSLOTS + len(EXTRA))]
        consts = sem("consts_ready")
        mm_done = sem("mm_done")
        bank_read = [sem(f"bank{i}_read") for i in range(MM_BANKS)]
        dve_seq = sem("dve_seq")
        act_seq = sem("act_seq")
        std_ready = sem("std_ready")
        hn_ready = sem("hn_ready")
        x_fed = sem("x_fed")
        dt_abs_ready = sem("dt_abs_ready")
        dt_exp_ready = sem("dt_exp_ready")
        adt_ready = sem("adt_ready")
        high_ready = sem("high_ready")
        low_ready = sem("low_ready")
        first_tap_ready = sem("first_tap_ready")
        silu_ready = sem("silu_ready")
        toend_ready = sem("toend_ready")
        eacs_ready = sem("eacs_ready")
        xd_ready = sem("xd_ready")
        xde_ready = sem("xde_ready")
        skip_ready = sem("skip_ready")
        decay_ready = sem("decay_ready")
        m_ready = sem("m_ready")
        zexp_ready = sem("zexp_ready")
        gated_ready = [sem(f"gated{b}_ready") for b in range(NB)]
        gstd_ready = sem("gstd_ready")
        yn_ready = sem("yn_ready")
        sq_ready = sem("sq_ready")
        qss_ready = sem("qss_ready")
        qstd_ready = sem("qstd_ready")
        qn_ready = sem("qn_ready")
        lamdot_ready = sem("lamdot_ready")
        lamexp_ready = sem("lamexp_ready")
        max_ready = sem("max_ready")
        exp_ready = sem("exp_ready")
        attn_ready = sem("attn_ready")
        ostd_ready = sem("ostd_ready")
        on_ready = sem("on_ready")
        gsub_ready = sem("gsub_ready")
        gexp_ready = sem("gexp_ready")
        idx_ready = sem("idx_ready")
        idx_now_ready = sem("idx_now_ready")
        u_loaded = [sem(f"u{i}_loaded") for i in range(GRP)]
        v_loaded = [sem(f"v{i}_loaded") for i in range(GRP)]
        u_free = sem("u_free")
        v_free = sem("v_free")
        gelu_ready = sem("gelu_ready")
        wts_ready = sem("wts_ready")
        diag_ready = sem("diag_ready")
        stored = sem("stored")

        def bank(key):
            return banks[PLAN[key][0]]

        def produced(eng, key):
            eng.wait_ge(mm_done, PLAN[key][2] + 1)

        def read_of(key):
            return bank_read[PLAN[key][0]]

        def moved(eng, key):
            eng.wait_ge(read_of(key), PLAN[key][1] + 1)

        def w_slot(slot):
            if slot < WSLOTS:
                return wring[:, slot]
            return view(ring_flat, 8192, KD, WCOLS) if slot == WSLOTS else view(tmp_ap, 4096, KD, WCOLS)

        def w_tile(*key):
            return w_slot(WAT[key][0])

        def w_landed(eng, *key):
            slot, nth, _ = WAT[key]
            eng.wait_ge(w_loaded[slot], 16 * nth)

        def last_use(key):
            name, layer, _, c0 = key[:4]
            if name == "in":
                return ("xbc", 2 * ((c0 - DI) // WCOLS) + 1) if c0 >= DI else ("z", NB - 1, c0 // WCOLS)
            if name == "query":
                return ("q", layer, NB - 1 if layer == 0 else key[4], c0 // WCOLS)
            if name == "qkv":
                return ("qkv", c0 // WCOLS, key[4])
            return ("out", 0, c0 // WCOLS, NB - 1) if name == "out0" else ("out", 1, c0 // WCOLS, key[4])

        def normed(i, b):
            return NORM_ORDER.index((i, b)) + 1

        def q_place(layer, b, c):
            at = 4 * ((2 * c + b) % 4)
            return qT[:, at:at + 4] if layer == 0 else qbT[:, 4 * (c % 2):4 * (c % 2) + 4]

        def s_place(layer, b, c):
            return (sc[:, HC * b + 4 * c:HC * b + 4 * c + 4] if layer == 0
                    else sc2[:, 4 * (c % 2):4 * (c % 2) + 4])

        def chosen(layer, b, c):
            return (layer * NB + b) * CHUNKS + c + 1

        def bcast(ap, n):
            return ap.unsqueeze(2).broadcast_to([ap.shape[0], ap.shape[1], n])

        block = ctx.enter_context(nc.Block())

        @block.sync
        def _(sp):
            for b in range(NB):
                sp.dma_start(x[:, b], x_in[0, b * P:(b + 1) * P, :]).then_inc(x_loaded[b], 16)
            sp.dma_start(norm_w[:, 0], mix_norm_w[0:1, :].broadcast_to([P, D])).then_inc(normw_loaded[0], 16)
            dram = {
                "in": in_w, "out0": ssd_out_w, "qkv": qkv_w, "out1": da_out_w, "query": query_w,
            }

            def weight(n):
                name, layer, k0, c0 = WTILES[n][:4]
                slot, _, before = WAT[WTILES[n]]
                if before:
                    produced(sp, last_use(before))
                elif slot == WSLOTS:
                    sp.wait_ge(gated_ready[1], 4)
                elif slot > WSLOTS:
                    produced(sp, ("yo", NG // 2 - 1))
                src = dram[name][layer].rearrange("(k p) n -> p k n", p=P)[:, k0:k0 + KD, c0:c0 + WCOLS]
                sp.dma_start(w_slot(slot), src).then_inc(w_loaded[slot], 16)

            weight(0)
            sp.dma_start(w_dt[:], in_w[0].rearrange("(k p) n -> p k n", p=P)[:, :, in_cols - NH:in_cols]) \
                .then_inc(wdt_loaded, 16)
            sp.dma_start(cw[:], conv_w).then_inc(conv_loaded, 16)
            sp.dma_start(cb[:], conv_b).then_inc(conv_loaded, 16)
            sp.dma_start(dtb[:], dt_bias.broadcast_to([P, NH])).then_inc(dt_loaded, 16)
            sp.dma_start(alog[:], a_log.broadcast_to([P, NH])).then_inc(dt_loaded, 16)
            for n in range(1, WSLOTS):
                weight(n)
            sp.dma_start(dsk[:], d_skip.broadcast_to([P, NH])).then_inc(ssd_loaded, 16)
            sp.dma_start(snw[:], ssd_norm_w).then_inc(ssd_loaded, 16)
            for half in range(2):
                rows = slice(half * AD, (half + 1) * AD)
                sp.dma_start(qkn[rows, 0:1], q_norm_w.rearrange("a d -> d a")).then_inc(attn_loaded, 16)
                sp.dma_start(qkn[rows, 1:2], k_norm_w.rearrange("a d -> d a")).then_inc(attn_loaded, 16)
            for j, v in enumerate((lam_q1, lam_k1, lam_q2, lam_k2)):
                sp.dma_start(lams[:, j], v.broadcast_to([P, AD])).then_inc(attn_loaded, 16)
            sp.dma_start(sub_w[:], subln_w.rearrange("a d -> d a")).then_inc(attn_loaded, 16)
            sp.dma_start(norm_w[:, 1], ffn_norm_w[0:1, :].broadcast_to([P, D])).then_inc(normw_loaded[1], 16)
            sp.dma_start(keysT[:], keys_t[0].rearrange("h d n -> d h n")).then_inc(keys_loaded, 16)
            for n in range(WSLOTS, second):
                weight(n)
            sp.wait_ge(hn_ready, 2 * NB)
            sp.dma_start(norm_w[:, 0], mix_norm_w[1:2, :].broadcast_to([P, D])).then_inc(normw_loaded[2], 16)
            sp.dma_start(norm_w[:, 1], ffn_norm_w[1:2, :].broadcast_to([P, D])).then_inc(normw_loaded[3], 16)
            produced(sp, ("s", 0, NB - 1, CHUNKS - 1))
            sp.dma_start(keysT[:], keys_t[1].rearrange("h d n -> d h n")).then_inc(keys_loaded, 16)
            for n in range(second, len(WTILES)):
                weight(n)
            for b in range(NB):
                sp.wait_ge(x_fed, 2 * (NB + b) + 2)
                sp.dma_start(out[0, b * P:(b + 1) * P, :], x[:, b]).then_inc(stored, 16)
            sp.wait_ge(stored, 16 * NB)

        @block.gpsimd
        def _(pool):
            pool.memset(ones[:], 1.0).then_inc(consts, 1)
            pool.memset(eps[:], EPS).then_inc(consts, 1)
            pool.memset(mask[:], 0.0).then_inc(consts, 1)
            pool.memset(ident[:], 0.0).then_inc(consts, 1)
            pool.iota(iota[:], pattern=[[1, NC]], base=0, channel_multiplier=0,
                      allow_small_or_imprecise_dtypes=True).then_inc(consts, 1)
            pool.wait_ge(consts, 5)
            pool.affine_select(out=ident[:], in_=ident[:], compare_op=ALU.not_equal, fill=1.0, base=0,
                               pattern=[[-1, P]], channel_multiplier=1).then_inc(consts, 1)
            pool.affine_select(out=tri[:], in_=ones[:], compare_op=ALU.is_ge, fill=0.0, base=0,
                               pattern=[[1, P]], channel_multiplier=-1).then_inc(consts, 1)
            for b in range(NB):
                pool.memset(mask[0:P // 2, b, b * P + P // 2:(b + 1) * P], MASKED).then_inc(consts, 1)
            pool.sem_inc(u_free, GRP)
            pool.sem_inc(v_free, GRP)

            for b in range(NB):
                pool.wait_ge(xd_ready, b + 1)
                if b == 0:
                    pool.wait_ge(eacs_ready, 2)
                    nc.gpsimd.tensor_tensor(xde[:, :, :], xd[:, :, :], bcast(toend[:], HP), ALU.mult) \
                        .then_inc(xde_ready, 1)
                    pool.wait_ge(ssd_loaded, 32)
                xb = xh[:, b].rearrange("p (h e) -> p h e", e=HP)
                nc.gpsimd.tensor_tensor(xb, xb, bcast(dsk[:], HP), ALU.mult).then_inc(skip_ready, 1)

            u_rows, v_rows = (t.rearrange("l e d -> (l e) d") for t in (peer_u, peer_v))

            def gather(layer, b):
                g0 = (layer * NB + b) * (PAIRS // GRP)
                with pool.Fori(0, GROUPS // 2) as i:
                    pool.wait_ge(idx_ready, i + ((layer * NB + b) * GROUPS // 2 + 1))
                    for h in range(2):
                        pool.tensor_copy(idx_now[:, h], idx[:, b, bass.ds(i * (2 * GRP) + h * GRP, GRP)]) \
                            .then_inc(idx_now_ready, 1)
                        pool.wait_ge(idx_now_ready, i * 2 + (g0 + h + 1))
                        for k in range(GRP):
                            pool.wait_ge(u_free, i * (2 * GRP) + ((g0 + h) * GRP + k + 1))
                            pool.nop(nofuse=True)
                            pool.indirect_dma_start(
                                ring[:, k, :], None, u_rows,
                                bass.IndirectOffsetOnAxis(idx_now[:, h, k:k + 1], 0)).then_inc(u_loaded[k], 16)
                        if g0 == 0:
                            produced(pool, ("out", 0, 0, 1))
                        for k in range(GRP):
                            pool.wait_ge(v_free, i * (2 * GRP) + ((g0 + h) * GRP + k + 1))
                            pool.nop(nofuse=True)
                            pool.indirect_dma_start(
                                ring[:, GRP + k, :], None, v_rows,
                                bass.IndirectOffsetOnAxis(idx_now[:, h, k:k + 1], 0)).then_inc(v_loaded[k], 16)

            for layer in range(DEPTH):
                for b in range(NB):
                    gather(layer, b)

        @block.scalar
        def _(act):
            seq = [0]

            def step(ins):
                seq[0] += 1
                ins.then_inc(act_seq, 1)

            def settle():
                act.wait_ge(act_seq, seq[0])

            def norm_stats(i, blocks=range(NB)):
                if i == 0:
                    act.wait_ge(consts, 5)
                for b in blocks:
                    if i == 0:
                        act.wait_ge(x_loaded[b], 16)
                    if i % 2 == 1:
                        moved(act, ("out", i // 2, 0 if (i, b) == (1, 1) else 1, b))
                    elif i:
                        act.wait_ge(x_fed, 2 * b + 2)
                    if i:
                        produced(act, ("nT", i - 1, b, 1))
                    step(act.activation(hn[:, b], x[:, b], ACT.Square, accum_out=stat[:, 2 * i + b, 0:1]))
                    settle()
                    act.activation(stat[:, 2 * i + b, 1:2], stat[:, 2 * i + b, 0:1], ACT.Sqrt,
                                   scale=1.0 / D, bias=eps[:, 0:1]).then_inc(std_ready, 1)

            def norm_copies(i, blocks=range(NB)):
                for b in blocks:
                    for c in range(2):
                        key = ("nT", i, b, c)
                        produced(act, key)
                        act.activation(hnT[:, 4 * c:4 * c + 4, b * P:(b + 1) * P],
                                       bank(key)[:, :].rearrange("p (c t) -> p c t", c=4),
                                       ACT.Copy).then_inc(read_of(key), 1)

            def norm(i, blocks=range(NB)):
                norm_stats(i, blocks)
                norm_copies(i, blocks)

            def high_part(t):
                if t == 0:
                    for b in range(NB):
                        for c in range(2):
                            moved(act, ("nT", 0, b, c))
                    act.activation(hn_high[:, :, :], hnT[:, :, :], ACT.Copy).then_inc(high_ready, 1)
                    return
                key = ("in", 0, 0, DI + WCOLS * t)
                w_landed(act, *key)
                if t >= 3:
                    produced(act, ("xbc", 2 * (t - 2) + 1))
                act.activation(w_high[:, t % 2], w_tile(*key), ACT.Copy).then_inc(high_ready, 1)

            def ssd():
                high_part(0)
                high_part(1)
                act.wait_ge(dt_loaded, 32)
                step(act.activation(expa[:], alog[:], ACT.Exp))
                act.wait_ge(dt_abs_ready, 1)
                act.activation(spt[:, 2], spt[:, 1], ACT.Exp, scale=-1.0).then_inc(dt_exp_ready, 1)
                act.wait_ge(conv_loaded, 32)

                def first_tap(j):
                    key = ("xbc", j)
                    produced(act, key)
                    for s in range(2):
                        c = 2 * j + s
                        if j >= 2:
                            act.wait_ge(silu_ready, c - 3)
                        act.activation(cv[:, c % 4], bank(key)[:, s * T:(s + 1) * T], ACT.Identity,
                                       scale=cw[:, c, CONV - 1:CONV], bias=cb[:, c:c + 1]) \
                            .then_inc(first_tap_ready, 1)

                def silu(j):
                    moved(act, ("xbc", j))
                    for s in range(2):
                        c = 2 * j + s
                        if c < XS_TILES:
                            if j >= 2:
                                produced(act, ("xT", j - 2))
                            dst = xsT[:, c % 4]
                        else:
                            dst = bcT[:, c - XS_TILES]
                        act.activation(dst, cv[:, c % 4], ACT.Silu).then_inc(silu_ready, 1)

                def x_tokens(j):
                    key = ("xT", j)
                    produced(act, key)
                    act.activation(xh[:, :, 2 * j * P:(2 * j + 2) * P],
                                   bank(key)[:, :].rearrange("p (b c) -> p b c", b=NB),
                                   ACT.Copy).then_inc(read_of(key), 1)

                pairs = CONV_TILES // 2
                for j in range(pairs + 2):
                    if j < pairs:
                        first_tap(j)
                        if j % 2 == 1 and j < pairs - 3:
                            high_part(j // 2 + 2)
                    if 1 <= j <= pairs:
                        silu(j - 1)
                    if 2 <= j < XS_TILES // 2 + 2:
                        x_tokens(j - 2)

                def z_exp(b, g):
                    n = Z_AT[b, g] if g is not None else 0
                    key = Z_ORDER[n]
                    _, zb, c = key
                    produced(act, key)
                    act.activation(zs[:, zb, c * WCOLS:(c + 1) * WCOLS], bank(key)[:, :], ACT.Exp,
                                   scale=-1.0).then_inc(zexp_ready, 1)

                def squares(b, q):
                    act.wait_ge(gated_ready[b], q + 1)
                    for g in (2 * q, 2 * q + 1):
                        settle()
                        step(act.activation(junk[:, 0:GW], xh[:, b, g * GW:(g + 1) * GW], ACT.Square,
                                            accum_out=gst[:, b, 0, g:g + 1]))

                def deviations(b):
                    settle()
                    act.activation(gst[:, b, 1], gst[:, b, 0], ACT.Sqrt, scale=1.0 / GW,
                                   bias=eps[:, 0:1]).then_inc(gstd_ready, 1)

                z_exp(0, None)
                for c in range(2):
                    key = ("bT", c)
                    produced(act, key)
                    act.activation(b_tok[:, 4 * c:4 * c + 4],
                                   bank(key)[:, :].rearrange("p (g n) -> p g n", g=4),
                                   ACT.Copy).then_inc(read_of(key), 1)
                act.wait_ge(toend_ready, 1)
                act.activation(toend[:], toend[:], ACT.Exp).then_inc(eacs_ready, 1)
                act.activation(eacs[:], acs[:, 1], ACT.Exp).then_inc(eacs_ready, 1)
                for b in range(NB):
                    for g in range(NG):
                        moved(act, ("bc", b, g))
                        act.activation(seg[:, g % 4], seg[:, g % 4], ACT.Exp).then_inc(decay_ready, 1)
                        if g % 2 == 0 and b == 0 and g:
                            state_out(g // 2 - 1)
                        if (b, g - 2) in Z_AT:
                            z_exp(b, g - 2)
                        if (b, g) == (1, 0):
                            z_exp(0, NG - 1)
                        if (b, g) == (1, 4):
                            for q in range(4):
                                squares(0, q)
                            deviations(0)
                        if (b, g) == (1, 5):
                            squares(1, 0)
                        if (b, g) == (1, 7):
                            squares(1, 1)
                            squares(1, 2)
                    if b == 0:
                        state_out(NG // 2 - 1)
                squares(1, 3)
                deviations(1)

            def state_out(q):
                key = ("st", q)
                produced(act, key)
                act.activation(state[:, q * WCOLS:(q + 1) * WCOLS], bank(key)[:, :],
                               ACT.Copy).then_inc(read_of(key), 1)

            def lambdas():
                act.wait_ge(lamdot_ready, 2)
                act.activation(lam[:, 2:4], lam[:, 0:2], ACT.Exp).then_inc(lamexp_ready, 1)

            def qkv(b, n):
                key = ("qkv", n, b)
                produced(act, key)
                if n < 4:
                    m = 4 * b + n
                    if m >= 2:
                        act.wait_ge(qss_ready, m - 1)
                    act.activation(sq[:, m % 2], bank(key)[:, :], ACT.Square).then_inc(sq_ready, 1)
                    act.activation(qk[:, n * WCOLS:(n + 1) * WCOLS], bank(key)[:, :],
                                   ACT.Copy).then_inc(read_of(key), 1)
                else:
                    act.activation(vv[:, b, (n - 4) * WCOLS:(n - 3) * WCOLS], bank(key)[:, :],
                                   ACT.Copy).then_inc(read_of(key), 1)

            def qk_deviations(b):
                act.wait_ge(qss_ready, 4 * (b + 1))
                act.activation(qst[:, 1, b], qst[:, 0, b], ACT.Sqrt, scale=1.0 / AD,
                               bias=eps[:, 0:1]).then_inc(qstd_ready, 1)

            def exponentials(b, h):
                n = b * AH + h
                nk = (b + 1) * P
                act.wait_ge(max_ready, n + 1)
                for m in range(2):
                    act.activation(prob[:, n % 2, m, 0:nk], prob[:, n % 2, m, 0:nk], ACT.Exp,
                                   bias=smx[:, 0, n % 2, m:m + 1],
                                   accum_out=smx[:, 1, n % 2, m:m + 1]).then_inc(exp_ready, 1)

            def weighted(b, h):
                n = b * AH + h
                nk = (b + 1) * P
                key = ("aT", b, h)
                produced(act, key)
                if n >= 2:
                    produced(act, ("O", *HEADS[n - 2]))
                act.activation(attnT[:, n % 2, 0:nk], bank(key)[:, 0:nk], ACT.Copy) \
                    .then_inc(read_of(key), 1)
                key = ("O", b, h)
                produced(act, key)
                settle()
                step(act.activation(junk[:, 0:P], bank(key)[:, 0:P], ACT.Square,
                                    accum_out=ost[:, 0, b, h:h + 1]))
                act.activation(o_sb[:, h * P:(h + 1) * P], bank(key)[:, 0:P], ACT.Copy) \
                    .then_inc(read_of(key), 1)

            def o_deviations(b):
                settle()
                act.activation(ost[:, 1, b], ost[:, 0, b], ACT.Sqrt, scale=1.0 / P,
                               bias=eps[:, 0:1]).then_inc(ostd_ready, 1)

            def queries(layer, b, c):
                key = ("q", layer, b, c)
                produced(act, key)
                act.activation(q_place(layer, b, c), bank(key)[:, :].rearrange("p (a t) -> p a t", a=4),
                               ACT.Copy).then_inc(read_of(key), 1)

            def scores(layer, b, c):
                key = ("s", layer, b, c)
                produced(act, key)
                if layer and c >= 2:
                    act.wait_ge(gsub_ready, chosen(1, b, c - 2))
                act.activation(s_place(layer, b, c), bank(key)[:, :].rearrange("p (a t) -> p a t", a=4),
                               ACT.Copy).then_inc(read_of(key), 1)

            def first_choice(n):
                for name, b, c in FIRST_CHOICE[n]:
                    (queries if name == "q" else scores)(0, b, c)

            def gates(layer, b, c):
                act.wait_ge(gsub_ready, chosen(layer, b, c))
                part = gate[:, b, 2 * TOPK * c:2 * TOPK * (c + 1)]
                act.activation(part, part, ACT.Exp).then_inc(gexp_ready, 1)

            def gelu(layer, b, i, h):
                g0 = (layer * NB + b) * GROUPS
                act.wait_ge(u_free, i * (2 * GRP) + (g0 + h + 2) * GRP)
                act.activation(gel[:, h], acts[:, h], ACT.Gelu).then_inc(gelu_ready, 1)

            def diagonals(layer, b, i, h):
                g0 = (layer * NB + b) * GROUPS
                act.wait_ge(wts_ready, i * 2 + (g0 + h + 1))
                for k in range(GRP):
                    act.wait_ge(v_free, i * (2 * GRP) + ((g0 + h + 1) * GRP - DIAGS + k + 1))
                    act.activation(diag[:, k % DIAGS], ident[:], ACT.Copy, scale=wts[:, h, k:k + 1]) \
                        .then_inc(diag_ready, 1)

            def group(layer, b, i, h):
                gelu(layer, b, i, h)
                diagonals(layer, b, i, h)

            def groups(layer, b, first):
                with act.Fori(first, GROUPS // 2) as i:
                    for h in range(2):
                        group(layer, b, i, h)

            def front(b, part):
                if part == 0:
                    norm(2, [b])
                if part < 4:
                    qkv(b, part)
                elif part == 4:
                    qkv(b, 4)
                    qk_deviations(b)
                    qkv(b, 5)
                elif 6 <= part <= 10:
                    for h in (2 * (part - 7), 2 * (part - 7) + 1):
                        if part > 6:
                            weighted(b, h)
                    for h in (2 * (part - 6), 2 * (part - 6) + 1):
                        if part < 10:
                            exponentials(b, h)
                    if part == 10:
                        o_deviations(b)
                elif part == 12:
                    norm(3, [b])
                if 12 <= part < 16:
                    queries(1, b, part - 12)
                if 13 <= part:
                    scores(1, b, part - 13)

            norm(0)
            ssd()
            norm(1, [0])
            queries(0, 0, 0)
            scores(0, 0, 0)
            norm_stats(1, [1])
            queries(0, 0, 1)
            scores(0, 0, 1)
            norm_copies(1, [1])
            queries(0, 1, 0)
            gates(0, 0, 0)
            gelu(0, 0, 0, 0)
            for g in range(len(FIRST_CHOICE)):
                diagonals(0, 0, g // 2, g % 2)
                gelu(0, 0, (g + 1) // 2, (g + 1) % 2)
                first_choice(g)
                if g in (2, 3):
                    gates(0, 0, g - 1)
            diagonals(0, 0, 2, 1)
            gates(0, 0, CHUNKS - 1)
            for c in range(CHUNKS):
                group(0, 0, 3 + c // 2, c % 2)
                gates(0, 1, c)
            groups(0, 0, 5)
            lambdas()
            for layer, b, other in ((0, 1, 0), (1, 0, 1)):
                for g in range(GROUPS):
                    gelu(layer, b, g // 2, g % 2)
                    front(other, g)
                    diagonals(layer, b, g // 2, g % 2)
                    if layer and g in (2, 3):
                        gates(layer, b, g)
                front(other, GROUPS)
                gates(1, other, 0)
                gates(1, other, 1)
            for g in range(4):
                group(1, 1, g // 2, g % 2)
                if g >= 2:
                    gates(1, 1, g)
            groups(1, 1, 2)

        @block.tensor
        def _(pe):
            def take(key):
                bk, nth, _ = PLAN[key]
                if nth:
                    pe.wait_ge(bank_read[bk], nth)
                return banks[bk]

            def mm(out_, lhsT, rhs, start=True, stop=True):
                return nc.tensor.matmul(out_, lhsT, rhs, start=start, stop=stop)

            def norm(i, blocks=range(NB)):
                for b in blocks:
                    for c in range(2):
                        bk = take(("nT", i, b, c))
                        pe.wait_ge(hn_ready, normed(i, b))
                        if i == 0:
                            pe.wait_ge(consts, 6)
                        for k in range(4):
                            last = nc.tensor.transpose(bk[:, k * P:(k + 1) * P],
                                                       hn[:, b, (4 * c + k) * P:(4 * c + k + 1) * P], ident[:])
                        last.then_inc(mm_done, 1)
                for b in blocks:
                    for c in range(2):
                        moved(pe, ("nT", i, b, c))

            def project(out_, wcols, tok):
                for k in range(KD):
                    last = mm(out_, wcols(k), tok(k), k == 0, k == KD - 1)
                return last

            def project_parts(out_, high, low):
                for k in range(KD):
                    mm(out_, high[:, k], hn_high[:, k], k == 0, False)
                    mm(out_, high[:, k], hn_low[:, k], False, False)
                    last = mm(out_, low[:, k], hn_high[:, k], False, k == KD - 1)
                return last

            def ssd():
                def x_tokens(j):
                    bk = take(("xT", j))
                    pe.wait_ge(silu_ready, 2 * j + 2)
                    for s in range(2):
                        for b in range(NB):
                            last = nc.tensor.transpose(bk[:, (2 * b + s) * P:(2 * b + s + 1) * P],
                                                       xsT[:, (2 * j + s) % 4, b * P:(b + 1) * P], ident[:])
                    last.then_inc(mm_done, 1)

                def z_products(n):
                    _, zb, zn = Z_ORDER[n]
                    key = ("in", 0, 0, WCOLS * zn)
                    w_landed(pe, *key)
                    w = w_tile(*key)
                    bk = take(Z_ORDER[n])
                    project(bk[:, :], lambda k: hnT[:, k, zb * P:(zb + 1) * P], lambda k: w[:, k]) \
                        .then_inc(mm_done, 1)

                def y_transposes(b):
                    pe.wait_ge(yn_ready, b + 1)
                    for c in range(4):
                        bk = take(("ynT", b, c))
                        for k in range(4):
                            last = nc.tensor.transpose(bk[:, k * P:(k + 1) * P],
                                                       xh[:, b, (4 * c + k) * P:(4 * c + k + 1) * P], ident[:])
                        last.then_inc(mm_done, 1)

                for j in range(CONV_TILES // 2):
                    key = ("in", 0, 0, DI + WCOLS * (j // 2))
                    w_landed(pe, *key)
                    w = w_tile(*key)
                    bk = take(("xbc", j))
                    t = j // 2
                    if t:
                        pe.wait_ge(low_ready, t + 1)
                    for s in range(2):
                        c0 = (2 * (j % 2) + s) * P
                        if t:
                            last = project_parts(bk[:, s * T:(s + 1) * T], w_high[:, t % 2, :, c0:c0 + P],
                                                 w_low[:, WAT[key][0], :, c0:c0 + P])
                        else:
                            last = project(bk[:, s * T:(s + 1) * T], lambda k: w[:, k, c0:c0 + P],
                                           lambda k: hnT[:, k])
                    last.then_inc(mm_done, 1)
                    if j == 0:
                        pe.wait_ge(wdt_loaded, 16)
                        bk = take(("dt",))
                        for b in range(NB):
                            last = project(bk[:, b * NH:(b + 1) * NH],
                                           lambda k: hnT[:, k, b * P:(b + 1) * P], lambda k: w_dt[:, k])
                        last.then_inc(mm_done, 1)
                    if 2 <= j < XS_TILES // 2 + 2:
                        x_tokens(j - 2)
                z_products(0)
                bk = take(("acs",))
                pe.wait_ge(adt_ready, 1)
                pe.wait_ge(consts, 7)
                for b in range(NB):
                    mm(bk[:, b * NH:(b + 1) * NH], tri[:], adt[:, b])
                mm(bk[:, NB * NH:2 * NB * NH], ones[:], adt[:, :, :].rearrange("p b h -> p (b h)")) \
                    .then_inc(mm_done, 1)
                pe.wait_ge(silu_ready, CONV_TILES)
                for c in range(2):
                    bk = take(("bT", c))
                    for g in range(4):
                        last = nc.tensor.transpose(bk[:, g * P:(g + 1) * P], bcT[:, 4 * c + g, 0:P], ident[:])
                    last.then_inc(mm_done, 1)
                for b in range(NB):
                    scan(b, z_products, y_transposes)
                ssd_out(0, 0)
                ssd_out(1, 0)
                y_transposes(1)

            def ssd_out(n, b):
                bk = take(("out", 0, n, b))
                moved(pe, ("ynT", b, 3))
                for kh in range(2):
                    key = ("out0", 0, KD * kh, WCOLS * n)
                    w_landed(pe, *key)
                    w = w_tile(*key)
                    for k in range(KD):
                        last = mm(bk[:, :], ynT[:, KD * kh + k, b * P:(b + 1) * P], w[:, k],
                                  kh == 0 and k == 0, kh == 1 and k == KD - 1)
                last.then_inc(mm_done, 1)

            def scan(b, z_products, y_transposes):
                tok = slice(b * P, (b + 1) * P)
                for c in range(2):
                    bk = take(("cb", b, c))
                    for g in range(4):
                        last = mm(bk[:, g * P:(g + 1) * P], bcT[:, 4 * c + g, tok], bcT[:, NG + 4 * c + g, tok])
                    last.then_inc(mm_done, 1)

                def sums_on_all(g):
                    bk = take(("bc", b, g))
                    for e in range(HG):
                        h = g * HG + e
                        last = mm(bk[:, e * P:(e + 1) * P], adt[:, b, h:h + 1].broadcast_to([P, P]), tri[:])
                    last.then_inc(mm_done, 1)

                sums_on_all(0)
                sums_on_all(1)
                z_products(Z_AT[b, -1])
                for g in range(NG):
                    if g + 2 < NG:
                        sums_on_all(g + 2)
                    if g % 2 == 0:
                        bk = take(("y", b, g // 2))
                    pe.wait_ge(m_ready, b * NG + g + 1)
                    pe.wait_ge(xd_ready, b + 1)
                    for e in range(HG):
                        c0 = (g % 2) * GW + e * HP
                        last = mm(bk[:, c0:c0 + HP], seg[:, g % 4, e * P:(e + 1) * P], xd[:, g * HG + e])
                    if g % 2 == 0:
                        continue
                    last.then_inc(mm_done, 1)
                    bk = take(("st" if b == 0 else "yo", g // 2))
                    for gg in (g - 1, g):
                        cols = slice((gg % 2) * GW, (gg % 2 + 1) * GW)
                        if b == 0:
                            moved(pe, ("bT", 1))
                            pe.wait_ge(xde_ready, 1)
                            last = mm(bk[:, cols], b_tok[:, gg],
                                      xde[:, gg * HG:(gg + 1) * HG].rearrange("p a b -> p (a b)"))
                        else:
                            moved(pe, ("st", NG // 2 - 1))
                            last = mm(bk[:, cols], bcT[:, NG + gg, tok], state[:, gg * GW:(gg + 1) * GW])
                    last.then_inc(mm_done, 1)
                    if (b, g) in Z_AT:
                        z_products(Z_AT[b, g])
                    if (b, g) == (1, 5):
                        y_transposes(0)

            def rows_of(key, out_key, b, left):
                w_landed(pe, *key)
                w = w_tile(*key)
                bk = take(out_key)
                project(bk[:, :], left, lambda k: w[:, k]).then_inc(mm_done, 1)

            def qkv(b, n):
                rows_of(("qkv", 0, 0, WCOLS * n, b), ("qkv", n, b), b,
                        lambda k: hnT[:, k, b * P:(b + 1) * P])

            def qk_transposes(b):
                pe.wait_ge(qn_ready, b + 1)
                for c in range(4):
                    bk = take(("qkT", b, c))
                    for k in range(4):
                        last = nc.tensor.transpose(bk[:, k * P:(k + 1) * P],
                                                   qk[:, (4 * c + k) * P:(4 * c + k + 1) * P], ident[:])
                    last.then_inc(mm_done, 1)

            def head_scores(b, h):
                nk = (b + 1) * P
                if h == 0:
                    moved(pe, ("qkT", b, 3))
                for m in range(2):
                    bk = take(("S", b, h, m))
                    rows = slice(m * AD, (m + 1) * AD)
                    mm(bk[:, 0:nk], aqT[rows, h], kT[rows, h, 0:nk]).then_inc(mm_done, 1)

            def weighted(b, h):
                n = b * AH + h
                bk = take(("aT", b, h))
                pe.wait_ge(attn_ready, n + 1)
                for kb in range(b + 1):
                    last = nc.tensor.transpose(bk[:, kb * P:(kb + 1) * P],
                                               attn[:, n % 2, kb * P:(kb + 1) * P], ident[:])
                last.then_inc(mm_done, 1)
                bk = take(("O", b, h))
                moved(pe, ("aT", b, h))
                for kb in range(b + 1):
                    last = mm(bk[:, 0:P], attnT[:, n % 2, kb * P:(kb + 1) * P],
                              vv[:, kb, h * P:(h + 1) * P], kb == 0, kb == b)
                last.then_inc(mm_done, 1)

            def o_transposes(b):
                pe.wait_ge(on_ready, b + 1)
                for c in range(2):
                    bk = take(("oT", b, c))
                    for k in range(4):
                        last = nc.tensor.transpose(bk[:, k * P:(k + 1) * P],
                                                   o_sb[:, (4 * c + k) * P:(4 * c + k + 1) * P], ident[:])
                    last.then_inc(mm_done, 1)
                moved(pe, ("oT", b, 1))

            def attention_out(b, n):
                rows_of(("out1", 0, 0, WCOLS * n, b), ("out", 1, n, b), b, lambda k: oT[:, k])

            def queries(layer, b, c):
                key = ("query", 0, 0, WCOLS * c) if layer == 0 else ("query", 1, 0, WCOLS * c, b)
                w_landed(pe, *key)
                w = w_tile(*key)
                bk = take(("q", layer, b, c))
                for s in range(4):
                    last = project(bk[:, s * P:(s + 1) * P], lambda k: w[:, k, s * P:(s + 1) * P],
                                   lambda k: hnT[:, k, b * P:(b + 1) * P])
                last.then_inc(mm_done, 1)

            def scores(layer, b, c):
                if b == 0 and c == 0:
                    pe.wait_ge(keys_loaded, 16 * (layer + 1))
                moved(pe, ("q", layer, b, c))
                bk = take(("s", layer, b, c))
                for k in range(4):
                    last = mm(bk[:, k * P:(k + 1) * P], q_place(layer, b, c)[:, k], keysT[:, 4 * c + k])
                last.then_inc(mm_done, 1)

            def front(b, part):
                if part == 0:
                    norm(2, [b])
                if part < 4:
                    qkv(b, part)
                elif part == 4:
                    qkv(b, 4)
                    qkv(b, 5)
                elif part == 5:
                    qk_transposes(b)
                elif 6 <= part <= 10:
                    if part > 6:
                        weighted(b, 2 * (part - 7))
                        weighted(b, 2 * (part - 7) + 1)
                    if part < 10:
                        head_scores(b, 2 * (part - 6))
                        head_scores(b, 2 * (part - 6) + 1)
                    else:
                        o_transposes(b)
                        attention_out(b, 0)
                elif part == 11:
                    attention_out(b, 1)
                elif part == 12:
                    norm(3, [b])
                if 12 <= part < 16:
                    queries(1, b, part - 12)
                if 13 <= part:
                    scores(1, b, part - 13)

            def residual(layer, b):
                n = layer * NB + b
                if n:
                    pe.wait_ge(x_fed, 2 * n)
                for half in range(2):
                    nc.tensor.matmul(ysum[half][:, :], ident[:], x[:, b, half * 512:(half + 1) * 512],
                                     start=True, stop=False, skip_group_check=True)

            def group(layer, b, i):
                n0 = (layer * NB + b) * PAIRS
                for k in range(GRP):
                    pe.wait_ge(diag_ready, i * GRP + (n0 + k + 1))
                    pe.wait_ge(v_loaded[k], i * 16 + 16 * (n0 // GRP + 1))
                    for half in range(2):
                        last = nc.tensor.matmul(ysum[half][:, :], diag[:, k % DIAGS],
                                                ring[:, GRP + k, half * 512:(half + 1) * 512],
                                                start=False, stop=False, skip_group_check=True)
                    last.then_inc(v_free, 1)

            def groups(layer, b, first):
                with pe.Fori(first, GROUPS) as i:
                    group(layer, b, i)

            norm(0)
            ssd()
            norm(1, [0])
            queries(0, 0, 0)
            scores(0, 0, 0)
            ssd_out(1, 1)
            ssd_out(0, 1)
            queries(0, 0, 1)
            scores(0, 0, 1)
            norm(1, [1])
            queries(0, 1, 0)
            residual(0, 0)
            for g in range(len(FIRST_CHOICE)):
                group(0, 0, g)
                for name, b, c in FIRST_CHOICE[g]:
                    (queries if name == "q" else scores)(0, b, c)
            groups(0, 0, len(FIRST_CHOICE))
            for layer, b, other in ((0, 1, 0), (1, 0, 1)):
                for g in range(GROUPS):
                    front(other, g)
                    if g == 0:
                        residual(layer, b)
                    group(layer, b, g)
                front(other, GROUPS)
            residual(1, 1)
            groups(1, 1, 0)

        @block.vector
        def _(dve):
            seq = [0]

            def step(ins):
                seq[0] += 1
                ins.then_inc(dve_seq, 1)

            def settle():
                dve.wait_ge(dve_seq, seq[0])

            V = nc.vector

            def norm(i, blocks=range(NB)):
                dve.wait_ge(normw_loaded[i], 16)
                for b in blocks:
                    st = stat[:, 2 * i + b]
                    dve.wait_ge(std_ready, normed(i, b))
                    step(V.reciprocal(st[:, 2:3], st[:, 1:2]))
                    settle()
                    if i:
                        produced(dve, ("nT", i - 1, b, 1))
                    V.scalar_tensor_tensor(out=hn[:, b], in0=x[:, b], scalar=st[:, 2:3], in1=norm_w[:, i % 2],
                                           op0=ALU.mult, op1=ALU.mult).then_inc(hn_ready, 1)

            def soft_plus():
                produced(dve, ("dt",))
                dve.wait_ge(dt_loaded, 32)
                v, a, e, r, r2, p = (spt[:, j] for j in range(6))
                key = ("dt",)
                V.tensor_tensor(v.rearrange("p (b h) -> p b h", b=NB),
                                bank(key)[:, 0:NB * NH].rearrange("p (b h) -> p b h", b=NB),
                                dtb[:, :].unsqueeze(1).broadcast_to([P, NB, NH]), ALU.add) \
                    .then_inc(read_of(key), 1)
                moved(dve, key)
                V.scalar_tensor_tensor(out=a, in0=v, scalar=-1.0, in1=v, op0=ALU.mult,
                                       op1=ALU.max).then_inc(dt_abs_ready, 1)
                dve.wait_ge(dt_exp_ready, 1)
                step(V.tensor_scalar(r2, e, 2.0, None, ALU.add))
                settle()
                step(V.reciprocal(p, r2))
                settle()
                step(V.tensor_tensor(r, e, p, ALU.mult))
                settle()
                step(V.tensor_tensor(r2, r, r, ALU.mult))
                settle()
                step(V.tensor_scalar(p, r2, ATANH[-1], None, ALU.mult))
                settle()
                for coef in ATANH[-2::-1]:
                    step(V.scalar_tensor_tensor(out=p, in0=p, scalar=coef, in1=r2, op0=ALU.add, op1=ALU.mult))
                    settle()
                step(V.scalar_tensor_tensor(out=p, in0=p, scalar=1.0, in1=r, op0=ALU.add, op1=ALU.mult))
                step(V.tensor_scalar(a, v, 0.0, None, ALU.max))
                settle()
                step(V.scalar_tensor_tensor(out=dts[:, :, :].rearrange("p b h -> p (b h)"), in0=p, scalar=2.0,
                                            in1=a, op0=ALU.mult, op1=ALU.add))
                settle()
                for b in range(NB):
                    last = V.scalar_tensor_tensor(out=adt[:, b], in0=dts[:, b], scalar=-1.0, in1=expa[:],
                                                  op0=ALU.mult, op1=ALU.mult)
                last.then_inc(adt_ready, 1)

            def convolve(j):
                key = ("xbc", j)
                dve.wait_ge(first_tap_ready, 2 * j + 2)
                for tap in range(CONV - 2, -1, -1):
                    back = CONV - 1 - tap
                    for s in range(2):
                        c = 2 * j + s
                        o = cv[:, c % 4, back:T]
                        last = V.scalar_tensor_tensor(out=o, in0=bank(key)[:, s * T:(s + 1) * T - back],
                                                      scalar=cw[:, c, tap:tap + 1], in1=o, op0=ALU.mult,
                                                      op1=ALU.add)
                        if tap:
                            step(last)
                    if tap:
                        settle()
                last.then_inc(read_of(key), 1)

            def low_part(t):
                dve.wait_ge(high_ready, t + 1)
                if t == 0:
                    V.tensor_tensor(hn_low[:, :, :], hnT[:, :, :], hn_high[:, :, :].bitcast(F32), ALU.subtract).then_inc(low_ready, 1)
                else:
                    key = ("in", 0, 0, DI + WCOLS * t)
                    V.tensor_tensor(w_low[:, WAT[key][0]], w_tile(*key), w_high[:, t % 2].bitcast(F32),
                                    ALU.subtract) \
                        .then_inc(low_ready, 1)

            def ssd():
                low_part(0)
                low_part(1)
                soft_plus()
                for j in range(CONV_TILES // 2):
                    convolve(j)
                    if j % 2 == 1 and j < CONV_TILES // 2 - 3:
                        low_part(j // 2 + 2)
                key = ("acs",)
                produced(dve, key)
                V.tensor_copy(acs[:, :, :].rearrange("p b h -> p (b h)"),
                              bank(key)[:, 0:2 * NB * NH]).then_inc(read_of(key), 1)
                moved(dve, key)
                V.tensor_tensor(toend[:], acs[:, NB], acs[:, 0], ALU.subtract).then_inc(toend_ready, 1)
                z_silu(0)
                for b in range(NB):
                    scan(b)
                normed_y(1)
                add_back(0, 0, 0)
                add_back(0, 1, 0)

            def z_silu(n):
                key = Z_ORDER[n]
                _, zb, c = key
                zc = zs[:, zb, c * WCOLS:(c + 1) * WCOLS]
                dve.wait_ge(zexp_ready, n + 1)
                step(V.tensor_scalar(zc, zc, 1.0, None, ALU.add))
                settle()
                step(V.reciprocal(zc, zc))
                settle()
                V.tensor_tensor(zc, zc, bank(key)[:, :], ALU.mult).then_inc(read_of(key), 1)

            def gated(b, q):
                cols = slice(q * WCOLS, (q + 1) * WCOLS)
                settle()
                moved(dve, ("z", b, q))
                V.tensor_tensor(xh[:, b, cols], xh[:, b, cols], zs[:, b, cols], ALU.mult) \
                    .then_inc(gated_ready[b], 1)

            def normed_y(b):
                dve.wait_ge(gstd_ready, b + 1)
                step(V.reciprocal(gst[:, b, 2], gst[:, b, 1]))
                settle()
                yg = xh[:, b].rearrange("p (g c) -> p g c", g=NG)
                V.tensor_tensor(yg, yg, bcast(gst[:, b, 2], GW), ALU.mult).then_inc(yn_ready, 1)

            def y_transposed(b):
                for c in range(4):
                    key = ("ynT", b, c)
                    produced(dve, key)
                    V.tensor_tensor(ynT[:, 4 * c:4 * c + 4, b * P:(b + 1) * P],
                                    bank(key)[:, :].rearrange("p (k t) -> p k t", k=4),
                                    bcast(snw[:, 4 * c:4 * c + 4], P), ALU.mult).then_inc(read_of(key), 1)

            def scan(b):
                yb = xh[:, b]
                xb = yb.rearrange("p (h e) -> p h e", e=HP)
                if b == 0:
                    moved(dve, ("xT", XS_TILES // 2 - 1))
                else:
                    produced(dve, ("y", b - 1, NG // 2 - 1))
                V.tensor_tensor(xd[:, :, :], xb, bcast(dts[:, b], HP), ALU.mult).then_inc(xd_ready, 1)
                for c in range(2):
                    key = ("cb", b, c)
                    produced(dve, key)
                    V.tensor_tensor(cbm[:, 4 * c:4 * c + 4], bank(key)[:, :].rearrange("p (g l) -> p g l", g=4),
                                    tri[:, :].unsqueeze(1).broadcast_to([P, 4, P]), ALU.mult) \
                        .then_inc(read_of(key), 1)

                def differences(g):
                    key = ("bc", b, g)
                    produced(dve, key)
                    if b * NG + g >= 4:
                        pb, pg = (b, g - 4) if g >= 4 else (b - 1, g + 4)
                        produced(dve, ("y", pb, pg // 2))
                    for e in range(HG):
                        h = g * HG + e
                        last = V.tensor_scalar(seg[:, g % 4, e * P:(e + 1) * P], bank(key)[:, e * P:(e + 1) * P],
                                               acs[:, b, h:h + 1], 0.0, ALU.subtract, ALU.min)
                    last.then_inc(read_of(key), 1)

                def collect(q):
                    cols = slice(q * WCOLS, (q + 1) * WCOLS)
                    key = ("y", b, q)
                    produced(dve, key)
                    if q == 0:
                        dve.wait_ge(skip_ready, b + 1)
                        dve.wait_ge(eacs_ready, 2)
                    V.tensor_tensor(yb[:, cols], yb[:, cols], bank(key)[:, :], ALU.add).then_inc(read_of(key), 1)
                    if b:
                        key = ("yo", q)
                        produced(dve, key)
                        V.tensor_tensor(yoff.rearrange("p (h e) -> p h e", e=HP),
                                        bank(key)[:, :].rearrange("p (h e) -> p h e", e=HP),
                                        bcast(eacs[:, 2 * HG * q:2 * HG * (q + 1)], HP), ALU.mult) \
                            .then_inc(read_of(key), 1)
                        moved(dve, key)
                        moved(dve, ("y", b, q))
                        step(V.tensor_tensor(yb[:, cols], yb[:, cols], yoff, ALU.add))

                differences(0)
                moved(dve, ("cb", b, 1))
                for g in range(NG):
                    if g + 1 < NG:
                        differences(g + 1)
                    dve.wait_ge(decay_ready, b * NG + g + 1)
                    sg = seg[:, g % 4].rearrange("p (e l) -> p e l", e=HG)
                    V.tensor_tensor(sg, sg, cbm[:, g:g + 1].broadcast_to([P, HG, P]), ALU.mult) \
                        .then_inc(m_ready, 1)
                    if g % 2 == 0 and g >= 2:
                        collect(g // 2 - 1)
                    if (b, g) == (1, 0):
                        z_silu(Z_AT[0, NG - 1])
                    if (b, g - 2) in Z_AT:
                        z_silu(Z_AT[b, g - 2])
                    if b == 1:
                        if g in (3, 4, 6):
                            gated(1, (g - 2) // 2)
                        if g < 4:
                            gated(0, g)
                        if g == 5:
                            normed_y(0)
                        if g == 6:
                            y_transposed(0)
                collect(NG // 2 - 1)
                moved(dve, ("y", b, NG // 2 - 1))
                if b == 1:
                    gated(1, NG // 2 - 1)

            def add_back(layer, n, b):
                key = ("out", layer, n, b)
                produced(dve, key)
                xc = x[:, b, n * WCOLS:(n + 1) * WCOLS]
                V.tensor_tensor(xc, xc, bank(key)[:, :], ALU.add).then_inc(read_of(key), 1)

            def lambdas():
                dve.wait_ge(attn_loaded, 16 * 9)
                for j in range(2):
                    V.tensor_tensor_reduce(lams[:, 2 * j], lams[:, 2 * j], lams[:, 2 * j + 1], 1.0, 0.0, ALU.mult,
                                           ALU.add, lam[:, j:j + 1]).then_inc(lamdot_ready, 1)
                dve.wait_ge(lamexp_ready, 1)
                step(V.tensor_tensor(lam[:, 4:5], lam[:, 2:3], lam[:, 3:4], ALU.subtract))
                settle()
                step(V.tensor_scalar(lam[:, 5:6], lam[:, 4:5], -1.0, -LAMBDA_INIT, ALU.mult, ALU.add))

            def square_sums(b, n):
                m = 4 * b + n
                dve.wait_ge(sq_ready, m + 1)
                V.tensor_reduce(qst[:, 0, b, 8 * n:8 * n + 8], sq[:, m % 2].rearrange("p (h d) -> p h d", d=AD),
                                AX.X, ALU.add).then_inc(qss_ready, 1)

            def qk_normed(b):
                dve.wait_ge(qstd_ready, b + 1)
                step(V.reciprocal(qst[:, 2, b], qst[:, 1, b]))
                settle()
                q3 = qk.rearrange("p (h d) -> p h d", d=AD)
                V.tensor_tensor(q3, q3, bcast(qst[:, 2, b], AD), ALU.mult).then_inc(qn_ready, 1)

            def qk_transposed(b):
                for c in range(4):
                    key = ("qkT", b, c)
                    produced(dve, key)
                    which = c // 2
                    heads = slice(4 * (c % 2), 4 * (c % 2) + 4)
                    V.tensor_scalar(aqT[:, heads] if which == 0 else kT[:, heads, b * P:(b + 1) * P],
                                    bank(key)[:, :].rearrange("p (k t) -> p k t", k=4),
                                    qkn[:, which:which + 1], AD ** -0.5 if which == 0 else 1.0,
                                    ALU.mult, ALU.mult).then_inc(read_of(key), 1)

            def masked(b, h):
                n = b * AH + h
                nk = (b + 1) * P
                if n >= 2:
                    dve.wait_ge(attn_ready, n - 1)
                for m in range(2):
                    key = ("S", b, h, m)
                    produced(dve, key)
                    V.tensor_tensor(prob[:, n % 2, m, 0:nk], bank(key)[:, 0:nk], mask[:, b, 0:nk],
                                    ALU.add).then_inc(read_of(key), 1)
                for m in range(2):
                    moved(dve, ("S", b, h, m))
                V.tensor_reduce(smx[:, 0, n % 2], prob[:, n % 2, :, 0:nk], AX.X, ALU.max,
                                negate=True).then_inc(max_ready, 1)

            def combined(b, h):
                n = b * AH + h
                nk = (b + 1) * P
                dve.wait_ge(exp_ready, 2 * n + 2)
                step(V.reciprocal(smx[:, 2, n % 2], smx[:, 1, n % 2]))
                settle()
                step(V.tensor_tensor(smx[:, 3, n % 2, 0:1], smx[:, 2, n % 2, 1:2], lam[:, 5:6], ALU.mult))
                if n >= 2:
                    produced(dve, ("aT", *HEADS[n - 2]))
                step(V.tensor_scalar(attn[:, n % 2, 0:nk], prob[:, n % 2, 0, 0:nk],
                                     smx[:, 2, n % 2, 0:1], None, ALU.mult))
                settle()
                V.scalar_tensor_tensor(out=attn[:, n % 2, 0:nk], in0=prob[:, n % 2, 1, 0:nk],
                                       scalar=smx[:, 3, n % 2, 0:1], in1=attn[:, n % 2, 0:nk],
                                       op0=ALU.mult, op1=ALU.add).then_inc(attn_ready, 1)

            def o_normed(b):
                dve.wait_ge(ostd_ready, b + 1)
                step(V.reciprocal(ost[:, 2, b], ost[:, 1, b]))
                settle()
                o3 = o_sb.rearrange("p (h e) -> p h e", h=AH)
                V.tensor_tensor(o3, o3, bcast(ost[:, 2, b], P), ALU.mult).then_inc(on_ready, 1)
                for c in range(2):
                    key = ("oT", b, c)
                    produced(dve, key)
                    V.tensor_scalar(oT[:, 4 * c:4 * c + 4],
                                    bank(key)[:, :].rearrange("p (k t) -> p k t", k=4), sub_w[:, 0:1],
                                    1.0 - LAMBDA_INIT, ALU.mult, ALU.mult).then_inc(read_of(key), 1)

            def best_16(values, top, where):
                sets = range(values.shape[1])
                for half in range(2):
                    ks = slice(8 * half, 8 * half + 8)
                    for j in sets:
                        step(V.max(top[:, j, ks], values[:, j]))
                    settle()
                    for j in sets:
                        step(V.max_index(where[:, j, ks], top[:, j, ks], values[:, j]))
                    settle()
                    if half == 0:
                        for j in sets:
                            step(V.match_replace(values[:, j], top[:, j, ks], values[:, j], MASKED))
                        settle()

            def pairs_of(out_, first, second):
                nh = first.shape[1]
                for i in range(5):
                    n, o = CAND_LEN[i], CAND_OFF[i]
                    V.tensor_tensor(out_[:, :, o:o + n], first[:, :, i:i + 1].broadcast_to([P, nh, n]),
                                    second[:, :, 0:n], ALU.add)
                o = CAND_OFF[5]
                V.tensor_tensor(out_[:, :, o:o + 6].rearrange("p h (i j) -> p h i j", j=2),
                                first[:, :, 5:8].unsqueeze(3).broadcast_to([P, nh, 3, 2]),
                                second[:, :, 0:2].unsqueeze(2).broadcast_to([P, nh, 3, 2]), ALU.add)
                o = CAND_OFF[8]
                step(V.tensor_tensor(out_[:, :, o:o + 8], first[:, :, 8:16],
                                     second[:, :, 0:1].broadcast_to([P, nh, 8]), ALU.add))

            def choose(layer, b, c):
                moved(dve, ("s", layer, b, c))
                done = 2 * (chosen(layer, b, c) - 1)
                for h in ([0], [1]) if done == 0 else ([0, 1],):
                    done += len(h)
                    choose_heads(layer, b, c, slice(h[0], h[-1] + 1), done)

            def choose_heads(layer, b, c, hs, done):
                nh = hs.stop - hs.start
                top, where, where_f = (t[:, 0:2 * nh] for t in (topv, topi, topf))
                keys = s_place(layer, b, c)[:, 2 * hs.start:2 * hs.stop]
                first = (2 * c + hs.start) * TOPK
                cols = slice(first, first + nh * TOPK)
                best_16(keys, top, where)
                step(V.tensor_copy(where_f, where))
                settle()
                values, places = (t.rearrange("p (h c) k -> p h c k", c=2) for t in (top, where_f))
                step(V.tensor_scalar(places[:, :, 0], places[:, :, 0], float(NK), None, ALU.mult))
                pairs_of(cs[:, 0:nh], values[:, :, 0], values[:, :, 1])
                settle()
                pairs_of(ci[:, 0:nh], places[:, :, 0], places[:, :, 1])
                best_16(cs[:, 0:nh], best[:, 0:nh], posi[:, 0:nh])
                step(V.tensor_copy(posf[:, 0:nh], posi[:, 0:nh]))
                less = V.tensor_tensor(gate[:, b, cols].rearrange("p (h k) -> p h k", h=nh), best[:, 0:nh],
                                       best[:, 0:nh, 0:1].broadcast_to([P, nh, TOPK]), ALU.subtract)
                if hs.stop == 2:
                    less.then_inc(gsub_ready, 1)
                settle()
                shape = [P, nh, TOPK, NC]
                same = eq if nh == 2 else view(tmp_ap, 3072, 1, TOPK, NC)
                step(V.tensor_tensor(same, posf[:, 0:nh].unsqueeze(3).broadcast_to(shape),
                                     iota[:, :].unsqueeze(1).unsqueeze(1).broadcast_to(shape), ALU.is_equal))
                settle()
                step(V.tensor_tensor(same, same, ci[:, 0:nh].unsqueeze(2).broadcast_to(shape), ALU.mult))
                settle()
                numbers = idxf[:, 0:nh * TOPK]
                step(V.tensor_reduce(numbers.rearrange("p (a k) -> p a k", a=nh), same, AX.X, ALU.add))
                settle()
                V.tensor_scalar(idx[:, b, cols], numbers, float(layer * NE), None, ALU.add) \
                    .then_inc(idx_ready, nh)
                dve.wait_ge(idx_ready, done)

            def gates(layer, b, c):
                part = gate[:, b, 2 * TOPK * c:2 * TOPK * (c + 1)].rearrange("p (h k) -> p h k", h=2)
                dve.wait_ge(gexp_ready, chosen(layer, b, c))
                step(V.tensor_reduce(gsum[:, 0], part, AX.X, ALU.add))
                settle()
                step(V.reciprocal(gsum[:, 1], gsum[:, 0]))
                settle()
                step(V.tensor_tensor(part, part, bcast(gsum[:, 1], TOPK), ALU.mult))
                settle()

            def group(layer, b, i, h, first_of=None):
                g0 = (layer * NB + b) * GROUPS
                for k in range(GRP):
                    dve.wait_ge(u_loaded[k], i * 32 + 16 * (g0 + h + 1))
                    V.tensor_tensor_reduce(ring[:, k], ring[:, k], hn[:, b], 1.0, 0.0, ALU.mult, ALU.add,
                                           acts[:, h, k:k + 1]).then_inc(u_free, 1)
                if first_of is not None:
                    gates(layer, b, first_of)
                dve.wait_ge(gelu_ready, i * 2 + (g0 + h + 1))
                V.tensor_tensor(wts[:, h], gel[:, h], gate[:, b, bass.ds(i * (2 * GRP) + h * GRP, GRP)],
                                ALU.mult).then_inc(wts_ready, 1)

            def nth_group(layer, b, g):
                group(layer, b, g // 2, g % 2, g // CHUNK_GROUPS if g % CHUNK_GROUPS == 0 else None)

            def groups(layer, b, first):
                for c in range((first - 1) // 2 + 1, CHUNKS):
                    gates(layer, b, c)
                with dve.Fori(first, GROUPS // 2) as i:
                    for h in range(2):
                        group(layer, b, i, h)

            def finish(layer, b):
                dve.wait_ge(v_free, GRP + (layer * NB + b + 1) * PAIRS)
                for half in range(2):
                    V.tensor_copy(x[:, b, half * 512:(half + 1) * 512], ysum[half][:, :]).then_inc(x_fed, 1)

            def front(b, part):
                if part == 0:
                    norm(2, [b])
                if part < 4:
                    square_sums(b, part)
                elif part == 4:
                    qk_normed(b)
                elif part == 5:
                    qk_transposed(b)
                elif 6 <= part <= 9:
                    for h in (2 * (part - 6), 2 * (part - 6) + 1):
                        masked(b, h)
                    for h in (2 * (part - 6), 2 * (part - 6) + 1):
                        combined(b, h)
                elif part == 10:
                    o_normed(b)
                    add_back(1, 0, b)
                elif part == 11:
                    add_back(1, 1, b)
                elif part == 12:
                    norm(3, [b])
                elif part in (14, 16):
                    choose(1, b, (part - 14) // 2)

            norm(0)
            ssd()
            norm(1, [0])
            y_transposed(1)
            choose(0, 0, 0)
            add_back(0, 1, 1)
            add_back(0, 0, 1)
            norm(1, [1])
            for g in range(6):
                nth_group(0, 0, g)
                if g in (1, 2, 4):
                    choose(0, 0, g if g < 4 else 3)
            for c in range(CHUNKS):
                choose(0, 1, c)
                nth_group(0, 0, 6 + c)
            groups(0, 0, 5)
            lambdas()
            finish(0, 0)
            for layer, b, other in ((0, 1, 0), (1, 0, 1)):
                for g in range(GROUPS):
                    nth_group(layer, b, g)
                    front(other, g)
                    if layer and g in (1, 2):
                        choose(1, b, g + 1)
                front(other, GROUPS)
                finish(layer, b)
            for g in range(4):
                nth_group(1, 1, g)
                if g in (1, 2):
                    choose(1, 1, g + 1)
            groups(1, 1, 2)
            finish(1, 1)


def kernel(**inputs):
    import numpy as np
    import concourse.bacc as bacc
    from concourse.bass_utils import run_bass_kernel_spmd

    a = {name: np.asarray(v) for name, v in inputs.items()}
    tiles = CONV_TILES
    arrays = {
        "x_in": a["x"],
        "mix_norm_w": a["mix_norm_w"],
        "ffn_norm_w": a["ffn_norm_w"],
        "in_w": a["ssd_in_w"],
        "conv_w": a["ssd_conv_w"][0].T.reshape(tiles, P, CONV).transpose(1, 0, 2),
        "conv_b": a["ssd_conv_b"][0].reshape(tiles, P).T,
        "dt_bias": a["ssd_dt_bias"],
        "a_log": a["ssd_a_log"],
        "d_skip": a["ssd_d"],
        "ssd_norm_w": a["ssd_norm_w"][0].reshape(XS_TILES, P).T,
        "ssd_out_w": a["ssd_out_w"],
        "qkv_w": a["da_qkv_w"],
        "q_norm_w": a["da_q_norm_w"],
        "k_norm_w": a["da_k_norm_w"],
        "lam_q1": a["da_lam_q1"],
        "lam_k1": a["da_lam_k1"],
        "lam_q2": a["da_lam_q2"],
        "lam_k2": a["da_lam_k2"],
        "subln_w": a["da_subln_w"],
        "da_out_w": a["da_out_w"],
        "query_w": a["peer_query_w"],
        "keys_t": a["peer_sub_keys"].reshape(DEPTH, HC, NK, -1).transpose(0, 1, 3, 2),
        "peer_u": a["peer_u"],
        "peer_v": a["peer_v"],
    }
    arrays = {name: np.ascontiguousarray(v) for name, v in arrays.items()}
    nc = bacc.Bacc("TRN2", target_bir_lowering=False, num_devices=1)
    args = [nc.dram_tensor(f"in_{name}", v.shape, mybir.dt.from_np(v.dtype), kind="ExternalInput").ap()
            for name, v in arrays.items()]
    args.append(nc.dram_tensor("out_y", a["x"].shape, mybir.dt.from_np(a["x"].dtype),
                               kind="ExternalOutput").ap())
    build(nc, *args)
    r = run_bass_kernel_spmd(nc, [{f"in_{name}": v for name, v in arrays.items()}], core_ids=[0])
    return r.results[0]["out_y"]
```
